# Optimizing a Trainium2 kernel written in Bass

```python
import math
import jax, jax.numpy as jnp
from jax import lax
import numpy as np

D_MODEL = 1024
BATCH = 1
SEQ = 256
DEPTH = 2

GRID_W = 64
CTX_LEN = 256
NORM_EPS = 1e-6
A_HEADS = 4
A_DK = 128
A_DV = 128
A_CONV = 5
A_CHUNK = 64
B_HEADS = 8
B_Q_RANK = 384
B_KV_RANK = 256
B_NOPE = 64
B_ROPE = 32
B_DV = 64
B_QBLOCK = 128
ROPE_THETA = 10000.0
C_HEADS = 16
C_DH = D_MODEL // C_HEADS
WIN_R = 8
WIN_C = 16
D_FF = 2816
N_EXPERTS = 8
TOP_K = 2
D_FF_EXPERT = 3584

N_EVEN = (DEPTH + 1) // 2
N_ODD = DEPTH // 2
IN_SPLITS = (A_HEADS * A_DK, A_HEADS * A_DK, A_HEADS * A_DV, A_HEADS * A_DV, 2 * A_HEADS, 2 * A_HEADS, B_Q_RANK, B_KV_RANK, B_ROPE)
IN_DIM = sum(IN_SPLITS)
MIX_OUT = A_HEADS * A_DV + B_HEADS * B_DV

kernel_name = 'hybrid_gdn_mla_nat_moe_dit'

F32 = jnp.float32

def rmsnorm(x, g):
    xf = x.astype(F32)
    y = xf * lax.rsqrt(jnp.mean(xf * xf, axis=-1, keepdims=True) + NORM_EPS)
    return (y * g.astype(F32)).astype(x.dtype)

def l2norm(x):
    xf = x.astype(F32)
    return (xf * lax.rsqrt(jnp.sum(xf * xf, axis=-1, keepdims=True) + 1e-6)).astype(x.dtype)

def split_cols(t, sizes):
    offs = [int(o) for o in np.cumsum(sizes)[:-1]]
    return jnp.split(t, offs, axis=-1)

def dwconv_centred(x, w):
    k = w.shape[0]
    return lax.conv_general_dilated(x, w[:, None, :].astype(x.dtype), window_strides=(1,), padding=[((k - 1) // 2, (k - 1) // 2)], dimension_numbers=('NWC', 'WIO', 'NWC'), feature_group_count=x.shape[-1])

def axial_rope_tables(L):
    t = jnp.arange(L)
    row = (t // GRID_W).astype(F32)
    col = (t % GRID_W).astype(F32)
    half = B_ROPE // 2
    inv = ROPE_THETA ** (-jnp.arange(0, half, 2, dtype=F32) / half)
    ar = row[:, None] * inv[None, :]
    ac = col[:, None] * inv[None, :]
    ang = jnp.concatenate([ar, ar, ac, ac], axis=-1)
    return jnp.cos(ang), jnp.sin(ang)

def apply_rope(x, cos, sin):
    x1, x2, x3, x4 = jnp.split(x.astype(F32), 4, axis=-1)
    rot = jnp.concatenate([-x2, x1, -x4, x3], axis=-1)
    shp = (cos.shape[0],) + (1,) * (x.ndim - 3) + (cos.shape[1],)
    return (x.astype(F32) * cos.reshape(shp) + rot * sin.reshape(shp)).astype(x.dtype)

def gated_delta_chunked(q, k, v, g, beta, s0):
    b, h, L, dk = q.shape
    dv = v.shape[-1]
    n = L // A_CHUNK

    def blocks(t):
        return t.astype(F32).reshape(b, h, n, A_CHUNK, *t.shape[3:])

    q = blocks(q) * (dk ** -0.5)
    k, v, g, beta = blocks(k), blocks(v), blocks(g), blocks(beta)
    gc = jnp.cumsum(g, axis=-1)
    lower = jnp.tril(jnp.ones((A_CHUNK, A_CHUNK), bool))
    strict = jnp.tril(jnp.ones((A_CHUNK, A_CHUNK), bool), -1)
    diff = gc[..., :, None] - gc[..., None, :]
    decay = jnp.where(lower, jnp.exp(jnp.where(lower, diff, 0.0)), 0.0)
    kb = k * beta[..., None]
    a_mat = jnp.where(strict, jnp.einsum('bhnid,bhnjd->bhnij', kb, k) * decay, 0.0)
    tmat = a_mat + jnp.eye(A_CHUNK, dtype=F32)
    u = lax.linalg.triangular_solve(tmat, v * beta[..., None], left_side=True, lower=True, unit_diagonal=True)
    w = lax.linalg.triangular_solve(tmat, kb * jnp.exp(gc)[..., None], left_side=True, lower=True, unit_diagonal=True)
    qk = jnp.einsum('bhnid,bhnjd->bhnij', q, k) * decay
    qg = q * jnp.exp(gc)[..., None]
    kg = k * jnp.exp(gc[..., -1:] - gc)[..., None]
    g_last = jnp.exp(gc[..., -1])

    def step(s, xs):
        qg_i, kg_i, u_i, w_i, qk_i, gl_i = xs
        v_new = u_i - jnp.einsum('bhid,bhde->bhie', w_i, s)
        o = jnp.einsum('bhid,bhde->bhie', qg_i, s) + jnp.einsum('bhij,bhje->bhie', qk_i, v_new)
        s = s * gl_i[..., None, None] + jnp.einsum('bhid,bhie->bhde', kg_i, v_new)
        return s, o

    xs = (jnp.moveaxis(qg, 2, 0), jnp.moveaxis(kg, 2, 0), jnp.moveaxis(u, 2, 0), jnp.moveaxis(w, 2, 0), jnp.moveaxis(qk, 2, 0), jnp.moveaxis(g_last, 2, 0))
    s_final, o = lax.scan(step, s0, xs)
    return jnp.moveaxis(o, 0, 2).reshape(b, h, L, dv), s_final

def gdn_prepare(q, k, v, a, bg, conv_w, a_log, dt_bias):
    bsz, L, _ = q.shape
    qkv = jax.nn.silu(dwconv_centred(jnp.concatenate([q, k, v], axis=-1), conv_w))
    q, k, v = split_cols(qkv, (A_HEADS * A_DK, A_HEADS * A_DK, A_HEADS * A_DV))
    q = l2norm(q.reshape(bsz, L, A_HEADS, A_DK))
    k = l2norm(k.reshape(bsz, L, A_HEADS, A_DK))
    v = v.reshape(bsz, L, A_HEADS, A_DV)
    a = a.reshape(bsz, L, 2, A_HEADS).astype(F32)
    bg = bg.reshape(bsz, L, 2, A_HEADS).astype(F32)
    g = -jnp.exp(a_log.astype(F32)) * jax.nn.softplus(a + dt_bias.astype(F32))
    beta = jax.nn.sigmoid(bg)
    return (jnp.moveaxis(q, 1, 2), jnp.moveaxis(k, 1, 2), jnp.moveaxis(v, 1, 2), jnp.moveaxis(g, 1, -1), jnp.moveaxis(beta, 1, -1))

def gdn_bidirectional(ctx_in, lat_in):
    qc, kc, vc, gcx, bcx = ctx_in
    ql, kl, vl, glt, blt = lat_in
    s0 = jnp.zeros((qc.shape[0], A_HEADS, A_DK, A_DV), F32)
    fl = lambda t: jnp.flip(t, axis=2)
    oc_f, sc_f = gated_delta_chunked(qc, kc, vc, gcx[:, 0], bcx[:, 0], s0)
    ol_f, _ = gated_delta_chunked(ql, kl, vl, glt[:, 0], blt[:, 0], sc_f)
    oc_b, sc_b = gated_delta_chunked(fl(qc), fl(kc), fl(vc), fl(gcx[:, 1]), fl(bcx[:, 1]), s0)
    ol_b, _ = gated_delta_chunked(fl(ql), fl(kl), fl(vl), fl(glt[:, 1]), fl(blt[:, 1]), sc_b)
    return oc_f + fl(oc_b), ol_f + fl(ol_b)

def gdn_output(o, z, g):
    bsz, H, L, dv = o.shape
    o = rmsnorm(jnp.moveaxis(o, 1, 2), g) * jax.nn.silu(z.reshape(bsz, L, H, dv).astype(F32))
    return o.reshape(bsz, L, H * dv).astype(z.dtype)

def mla_project(cq, ckv, kr, q_g, w_uq, kv_g, w_ukv):
    bsz, L, _ = cq.shape
    q = (rmsnorm(cq, q_g) @ w_uq).reshape(bsz, L, B_HEADS, B_NOPE + B_ROPE)
    kv = (rmsnorm(ckv, kv_g) @ w_ukv).reshape(bsz, L, B_HEADS, B_NOPE + B_DV)
    return q[..., :B_NOPE], q[..., B_NOPE:], kv[..., :B_NOPE], kr, kv[..., B_NOPE:]

def mla_attend(qn, qr, kn, kr, v):
    s = jnp.einsum('bqhd,bkhd->bhqk', qn, kn).astype(F32) + jnp.einsum('bqhr,bkr->bhqk', qr, kr).astype(F32)
    p = jax.nn.softmax(s * ((B_NOPE + B_ROPE) ** -0.5), axis=-1).astype(v.dtype)
    return jnp.einsum('bhqk,bkhd->bqhd', p, v)

def mla_latent_attention(qn, qr, kn, kr, v):
    bsz, L, H, _ = qn.shape
    nb = L // B_QBLOCK
    blk = lambda t: jnp.moveaxis(t.reshape(bsz, nb, B_QBLOCK, *t.shape[2:]), 1, 0)
    o = lax.map(lambda qs: mla_attend(qs[0], qs[1], kn, kr, v), (blk(qn), blk(qr)))
    return jnp.moveaxis(o, 0, 1).reshape(bsz, L, H * B_DV)

def dense_attention(q, k, v):
    s = jnp.einsum('bqhd,bkhd->bhqk', q, k).astype(F32) * (q.shape[-1] ** -0.5)
    p = jax.nn.softmax(s, axis=-1).astype(v.dtype)
    return jnp.einsum('bhqk,bkhd->bqhd', p, v)

def neighbourhood_attention(q, k, v, k_ctx, v_ctx, rpb):
    bsz, L, H, dh = q.shape
    rows = L // GRID_W
    wr = min(WIN_R, rows)
    n_nb = wr * WIN_C
    scale = dh ** -0.5
    qg = q.reshape(bsz, rows, GRID_W, H, dh)
    kg = k.reshape(bsz, rows, GRID_W, H, dh)
    vg = v.reshape(bsz, rows, GRID_W, H, dh)
    col = jnp.arange(GRID_W)
    col_idx = jnp.clip(col - WIN_C // 2, 0, GRID_W - WIN_C)[:, None] + jnp.arange(WIN_C)[None, :]
    dc_idx = col_idx - col[:, None] + (WIN_C - 1)

    def row_block(r):
        r0 = jnp.clip(r - wr // 2, 0, rows - wr)
        k_win = lax.dynamic_slice_in_dim(kg, r0, wr, axis=1)[:, :, col_idx]
        v_win = lax.dynamic_slice_in_dim(vg, r0, wr, axis=1)[:, :, col_idx]
        q_r = lax.dynamic_index_in_dim(qg, r, axis=1, keepdims=False)
        dr_idx = r0 + jnp.arange(wr) - r + (WIN_R - 1)
        bias = rpb[:, dr_idx[None, :, None], dc_idx[:, None, :]].astype(F32)
        s_nb = jnp.einsum('bqhd,brqwhd->bhqrw', q_r, k_win).astype(F32) * scale + bias
        s_ctx = jnp.einsum('bqhd,bkhd->bhqk', q_r, k_ctx).astype(F32) * scale
        s = jnp.concatenate([s_nb.reshape(bsz, H, GRID_W, n_nb), s_ctx], axis=-1)
        p = jax.nn.softmax(s, axis=-1).astype(v.dtype)
        p_nb = p[..., :n_nb].reshape(bsz, H, GRID_W, wr, WIN_C)
        return jnp.einsum('bhqrw,brqwhd->bqhd', p_nb, v_win) + jnp.einsum('bhqk,bkhd->bqhd', p[..., n_nb:], v_ctx)

    o = lax.map(row_block, jnp.arange(rows))
    return jnp.moveaxis(o, 0, 1).reshape(bsz, L, H, dh)

def even_mixer(h_c, h_l, cos, sin, need_ctx, w_in, conv_w, a_log, dt_bias, gdn_g, q_g, w_uq, kv_g, w_ukv, w_out):
    pc = split_cols(h_c @ w_in, IN_SPLITS)
    pl = split_cols(h_l @ w_in, IN_SPLITS)
    a_ctx = gdn_prepare(pc[0], pc[1], pc[2], pc[4], pc[5], conv_w, a_log, dt_bias)
    a_lat = gdn_prepare(pl[0], pl[1], pl[2], pl[4], pl[5], conv_w, a_log, dt_bias)
    oa_c, oa_l = gdn_bidirectional(a_ctx, a_lat)
    ya_l = gdn_output(oa_l, pl[3], gdn_g)
    qn_c, qr_c, kn_c, kr_c, v_c = mla_project(pc[6], pc[7], pc[8], q_g, w_uq, kv_g, w_ukv)
    qn_l, qr_l, kn_l, kr_l, v_l = mla_project(pl[6], pl[7], pl[8], q_g, w_uq, kv_g, w_ukv)
    qr_l = apply_rope(qr_l, cos, sin)
    kr_l = apply_rope(kr_l, cos, sin)
    yb_l = mla_latent_attention(qn_l, qr_l, jnp.concatenate([kn_c, kn_l], axis=1), jnp.concatenate([kr_c, kr_l], axis=1), jnp.concatenate([v_c, v_l], axis=1))
    out_l = jnp.concatenate([ya_l, yb_l], axis=-1) @ w_out
    out_c = None
    if need_ctx:
        bsz, Lc, _ = h_c.shape
        ya_c = gdn_output(oa_c, pc[3], gdn_g)
        yb_c = mla_attend(qn_c, qr_c, kn_c, kr_c, v_c).reshape(bsz, Lc, B_HEADS * B_DV)
        out_c = jnp.concatenate([ya_c, yb_c], axis=-1) @ w_out
    return out_c, out_l

def odd_mixer(h_c, h_l, need_ctx, w_qkv, rpb, w_out):
    bsz, L, D = h_l.shape
    Lc = h_c.shape[1]
    q_l, k_l, v_l = [t.reshape(bsz, L, C_HEADS, C_DH) for t in jnp.split(h_l @ w_qkv, 3, axis=-1)]
    q_c, k_c, v_c = [t.reshape(bsz, Lc, C_HEADS, C_DH) for t in jnp.split(h_c @ w_qkv, 3, axis=-1)]
    out_l = neighbourhood_attention(q_l, k_l, v_l, k_c, v_c, rpb).reshape(bsz, L, D) @ w_out
    out_c = None
    if need_ctx:
        out_c = dense_attention(q_c, k_c, v_c).reshape(bsz, Lc, D) @ w_out
    return out_c, out_l

def swiglu(h, wg, wu, wd):
    return (jax.nn.silu(h @ wg) * (h @ wu)) @ wd

def moe_swiglu(h, w_router, wg, wu, wd):
    shp = h.shape
    t = h.reshape(-1, shp[-1])
    logits = (t @ w_router).astype(F32)
    top_v, top_i = lax.top_k(logits, TOP_K)
    gates = jax.nn.softmax(top_v, axis=-1)
    out = jnp.zeros_like(t)
    for e in range(N_EXPERTS):
        w_e = jnp.sum(jnp.where(top_i == e, gates, 0.0), axis=-1).astype(t.dtype)
        out = out + w_e[:, None] * swiglu(t, wg[e], wu[e], wd[e])
    return out.reshape(shp)

def setup_inputs(seed: int = 0) -> dict:
    key = jax.random.key(seed)
    ks = iter(list(jax.random.split(key, 40)))
    D = D_MODEL
    nrm = lambda shape, scale: jax.random.normal(next(ks), shape, F32) * scale
    gain = lambda shape: 1.0 + 0.02 * jax.random.normal(next(ks), shape, F32)
    dt = jnp.exp(jax.random.uniform(next(ks), (N_EVEN, 2, A_HEADS), F32, math.log(1e-3), math.log(1e-1)))
    return {
        'x': nrm((BATCH, SEQ, D), 1.0),
        'c': nrm((BATCH, D), 1.0),
        'ctx': nrm((BATCH, CTX_LEN, D), 1.0),
        'c_ctx': nrm((D,), 1.0),
        'ada_w': nrm((DEPTH, D, 6 * D), 0.5 * D ** -0.5),
        'ada_b': nrm((DEPTH, 6 * D), 0.01),
        'norm_g': gain((DEPTH, 2, D)),
        'ev_w_in': nrm((N_EVEN, D, IN_DIM), D ** -0.5),
        'ev_conv_w': nrm((N_EVEN, A_CONV, 2 * A_HEADS * A_DK + A_HEADS * A_DV), A_CONV ** -0.5),
        'ev_a_log': jnp.log(jax.random.uniform(next(ks), (N_EVEN, 2, A_HEADS), F32, 1.0, 16.0)),
        'ev_dt_bias': dt + jnp.log(-jnp.expm1(-dt)),
        'ev_gdn_norm_g': gain((N_EVEN, A_DV)),
        'ev_q_norm_g': gain((N_EVEN, B_Q_RANK)),
        'ev_w_uq': nrm((N_EVEN, B_Q_RANK, B_HEADS * (B_NOPE + B_ROPE)), B_Q_RANK ** -0.5),
        'ev_kv_norm_g': gain((N_EVEN, B_KV_RANK)),
        'ev_w_ukv': nrm((N_EVEN, B_KV_RANK, B_HEADS * (B_NOPE + B_DV)), B_KV_RANK ** -0.5),
        'ev_w_out': nrm((N_EVEN, MIX_OUT, D), MIX_OUT ** -0.5),
        'ev_ffn_wg': nrm((N_EVEN, D, D_FF), D ** -0.5),
        'ev_ffn_wu': nrm((N_EVEN, D, D_FF), D ** -0.5),
        'ev_ffn_wd': nrm((N_EVEN, D_FF, D), D_FF ** -0.5),
        'od_w_qkv': nrm((N_ODD, D, 3 * D), D ** -0.5),
        'od_rpb': nrm((N_ODD, C_HEADS, 2 * WIN_R - 1, 2 * WIN_C - 1), 0.1),
        'od_w_out': nrm((N_ODD, D, D), D ** -0.5),
        'od_router': nrm((N_ODD, D, N_EXPERTS), D ** -0.5),
        'od_exp_wg': nrm((N_ODD, N_EXPERTS, D, D_FF_EXPERT), D ** -0.5),
        'od_exp_wu': nrm((N_ODD, N_EXPERTS, D, D_FF_EXPERT), D ** -0.5),
        'od_exp_wd': nrm((N_ODD, N_EXPERTS, D_FF_EXPERT, D), D_FF_EXPERT ** -0.5),
        'final_norm_g': gain((D,)),
    }

def reference(x, c, ctx, c_ctx, ada_w, ada_b, norm_g, ev_w_in, ev_conv_w, ev_a_log, ev_dt_bias, ev_gdn_norm_g, ev_q_norm_g, ev_w_uq, ev_kv_norm_g, ev_w_ukv, ev_w_out, ev_ffn_wg, ev_ffn_wu, ev_ffn_wd, od_w_qkv, od_rpb, od_w_out, od_router, od_exp_wg, od_exp_wu, od_exp_wd, final_norm_g):
    L = x.shape[1]
    cos, sin = axial_rope_tables(L)
    s_c = jax.nn.silu(c)
    s_cc = jax.nn.silu(c_ctx)
    x_l, x_c = x, ctx
    for i in range(DEPTH):
        need_ctx = i < DEPTH - 1
        j = i // 2
        mod_l = (s_c @ ada_w[i] + ada_b[i])[:, None, :]
        mod_c = (s_cc @ ada_w[i] + ada_b[i])[None, None, :]
        sh1_l, sc1_l, g1_l, sh2_l, sc2_l, g2_l = jnp.split(mod_l, 6, axis=-1)
        sh1_c, sc1_c, g1_c, sh2_c, sc2_c, g2_c = jnp.split(mod_c, 6, axis=-1)
        h_l = rmsnorm(x_l, norm_g[i, 0]) * (1.0 + sc1_l) + sh1_l
        h_c = rmsnorm(x_c, norm_g[i, 0]) * (1.0 + sc1_c) + sh1_c
        if i % 2 == 0:
            out_c, out_l = even_mixer(h_c, h_l, cos, sin, need_ctx, ev_w_in[j], ev_conv_w[j], ev_a_log[j], ev_dt_bias[j], ev_gdn_norm_g[j], ev_q_norm_g[j], ev_w_uq[j], ev_kv_norm_g[j], ev_w_ukv[j], ev_w_out[j])
        else:
            out_c, out_l = odd_mixer(h_c, h_l, need_ctx, od_w_qkv[j], od_rpb[j], od_w_out[j])
        x_l = x_l + g1_l * out_l
        f_l = rmsnorm(x_l, norm_g[i, 1]) * (1.0 + sc2_l) + sh2_l
        if i % 2 == 0:
            x_l = x_l + g2_l * swiglu(f_l, ev_ffn_wg[j], ev_ffn_wu[j], ev_ffn_wd[j])
        else:
            x_l = x_l + g2_l * moe_swiglu(f_l, od_router[j], od_exp_wg[j], od_exp_wu[j], od_exp_wd[j])
        if need_ctx:
            x_c = x_c + g1_c * out_c
            f_c = rmsnorm(x_c, norm_g[i, 1]) * (1.0 + sc2_c) + sh2_c
            if i % 2 == 0:
                x_c = x_c + g2_c * swiglu(f_c, ev_ffn_wg[j], ev_ffn_wu[j], ev_ffn_wd[j])
            else:
                x_c = x_c + g2_c * moe_swiglu(f_c, od_router[j], od_exp_wg[j], od_exp_wu[j], od_exp_wd[j])
    return rmsnorm(x_l, final_norm_g)


_drawn_inputs = setup_inputs


def setup_inputs(seed=0):
    import zlib

    import numpy as np

    out = dict(_drawn_inputs(seed))
    spreads = {}
    factors = {'ev_a_log': 2.788,
     'ev_gdn_norm_g': 38.884,
     'ev_q_norm_g': 8.0,
     'ev_kv_norm_g': 8.0,
     'od_rpb': 45.304,
     'final_norm_g': 10.055}
    for name, (base, spread) in spreads.items():
        noise = np.random.default_rng([zlib.crc32(name.encode()), seed]).standard_normal(out[name].shape)
        drawn = base * np.exp(spread * noise) if base else spread * noise
        out[name] = __import__('jax').numpy.asarray(drawn.astype(out[name].dtype))
    for name, factor in factors.items():
        out[name] = (out[name] * factor).astype(out[name].dtype)
    return out
```

```python
import math
from contextlib import ExitStack

import concourse.bass as bass
import numpy as np
from concourse import mybir

P = 128
D = 1024
KB = D // P
L = 256
NT = 2 * L // P
T = 2 * L
EPS = 1e-6
H_A, DK = 4, 128
TAPS = 5
H_B, NOPE, ROPE, DV = 8, 64, 32, 64
QR, KVR = 384, 256
QD = NOPE + ROPE
H_C, DH = 16, 64
GRID_W, WIN_C, WIN_R = 64, 16, 8
RPB_R, RPB_C = 2 * WIN_R - 1, 2 * WIN_C - 1
ROWS = L // GRID_W
FF = 2816
E, FFE = 8, 3584
QKV_A = 3 * H_A * DK
Z0 = QKV_A
AB0 = Z0 + H_A * DK
IN_DIM = AB0 + 16 + QR + KVR + ROPE
REST = IN_DIM - AB0
CQ0, CKV0, KR0 = 16, 16 + QR, 16 + QR + KVR
SLOT = 4096
RING, RING_E = 3, 7
LEVELS = 7
IDENT, UP, LO, SLO, SUP, LEV, ROT, IOTA, FLIP = 0, 1, 2, 3, 4, 5, 5 + LEVELS, 6 + LEVELS, 7 + LEVELS
N_CONST = 8 + LEVELS
R_C, R_NG, R_CONV, R_QG, R_KVG = 0, 16, 48, 108, 111
WAVES = E + 3

STAGES = ["prep", "ada0", "norm0", "win", "tok", "mproj", "matt", "l2", "gdn", "gout", "out0", "norm1", "up",
          "down", "ada1", "norm2", "qkv", "natt", "out1", "norm3", "route", "moe", "final"]
WORKS = {
    "pe": set(STAGES) - {"moe", "final"},
    "act": set(STAGES) - {"final"},
    "dve": set(STAGES) - {"moe", "final"},
    "pool": {"prep", "gdn", "natt"},
}


def constants():
    i = np.arange(P)
    m = np.zeros((P, N_CONST, P), np.float32)
    r, c = i[:, None], i[None, :]
    m[:, IDENT] = r == c
    m[:, UP] = r <= c
    m[:, LO] = r >= c
    m[:, SLO] = r > c
    m[:, SUP] = r < c
    for n in range(LEVELS):
        m[:, LEV + n] = (r >> (n + 1) == c >> (n + 1)) & (r >> n != c >> n)
    q = ROPE // 4
    for a in range(q):
        for half in (0, 2 * q):
            m[NOPE + half + q + a, ROT, NOPE + half + a] = -1.0
            m[NOPE + half + a, ROT, NOPE + half + q + a] = 1.0
    m[:, IOTA] = c
    m[:, FLIP] = ((r // GRID_W == c // GRID_W) & (r % GRID_W == GRID_W - 1 - c % GRID_W)) * float(DH) ** 0.5
    t = np.arange(L)
    inv = np.float32(10000.0) ** (-np.arange(0, ROPE // 2, 2, dtype=np.float32) / np.float32(ROPE // 2))
    ar = (t // GRID_W).astype(np.float32)[:, None] * inv[None]
    ac = (t % GRID_W).astype(np.float32)[:, None] * inv[None]
    ang = np.concatenate([ar, ar, ac, ac], axis=-1)
    rope = np.stack([np.cos(ang).T, np.sin(ang).T], axis=1).astype(np.float32)
    col = GRID_W - 1 - i % GRID_W
    first = np.clip(col - WIN_C // 2, 0, GRID_W - WIN_C)[:, None]
    key = np.arange(GRID_W)[None]
    window = np.where((key >= first) & (key < first + WIN_C), 0.0, -1e30).astype(np.float32)
    return m.reshape(P, -1), rope, window


def build(nc, A, out):
    f32, i32 = mybir.dt.float32, mybir.dt.int32
    ALU, ACT, AX = mybir.AluOpType, mybir.ActivationFunctionType, mybir.AxisListType

    ctx = ExitStack()
    with ctx:
        def sb(name, shape, dt=f32):
            return ctx.enter_context(nc.sbuf_tensor(name, shape, dt))

        def sem(name):
            return ctx.enter_context(nc.semaphore(name))

        BIG = sb("BIG", [P, RING_E * SLOT])
        HB = sb("HB", [P, KB * T])
        QB = sb("QB", [P, 12 * T])
        X = sb("X", [P, NT, D])
        ZS = sb("ZS", [P, NT, 512])
        YB = sb("YB", [P, 4, T])
        CM = sb("CM", [P, N_CONST, P])
        CS = sb("CS", [P, 2, L])
        WM = sb("WM", [P, GRID_W])
        MOD = sb("MOD", [P, 3, 512])
        MT = sb("MT", [P, 3, 4, 4, 2])
        AB = sb("AB", [P, 2, 2, 2, KB])
        ROWSB = sb("ROWSB", [P, P])
        SM = sb("SM", [P, P])
        ST = sb("ST", [P, KB, 32])
        DTB = sb("DTB", [P, 2, 8])
        GG = sb("GG", [P, P])
        ONE = sb("ONE", [P, P])
        SS = sb("SS", [P, 64])
        RT = sb("RT", [P, 64])
        GB8 = sb("GB8", [P, NT, 3, 8])
        EG = sb("EG", [P, 2, 12])
        RW = sb("RW", [P, KB, E])
        EPSC = sb("EPSC", [P, 2])
        EA = sb("EA", [P, 1, 8])
        SELM = sb("SELM", [P, 2, E])
        WR = sb("WR", [P, 2, WAVES])
        WG = sb("WG", [P, 2, WAVES])
        RF = sb("RF", [P, 4])
        RI = sb("RI", [P, 4], i32)

        hT = HB[:, :].rearrange("p (k t) -> p k t", t=T)
        qkvT = QB[:, :].rearrange("p (b t) -> p b t", t=T)
        mixT = QB[:, 0:KB * T].rearrange("p (b t) -> p b t", t=T)
        XN = QB[:, 0:2 * D].rearrange("p (a n) -> p a n", a=2)
        GB = QB[:, KB * T:KB * T + 2 * D].rearrange("p (r n) -> p r n", r=2)
        AR = BIG[:, RING * SLOT:]

        class Cut:
            def __init__(self, region, at=0):
                self.region, self.at = region, at

            def __call__(self, *shape):
                n = int(np.prod(shape))
                v = self.region[:, self.at:self.at + n]
                self.at += n
                if len(shape) == 2:
                    v = v.rearrange("p (a b) -> p a b", a=shape[0])
                if len(shape) == 3:
                    v = v.rearrange("p (a b c) -> p a b c", a=shape[0], b=shape[1])
                return v

        cut = Cut(AR)
        BADD = cut(3, 512)
        cut = Cut(AR)
        CIN = cut(2, 2, L + TAPS - 1)
        CACC = cut(2, T)
        cut = Cut(AR)
        P2 = cut(NT, REST)
        CQT = cut(3, T)
        CKVT = cut(2, T)
        QT = cut(H_B, T)
        KT = cut(H_B, T)
        VB = cut(NT, H_B * DV)
        cut = Cut(HB)
        PM = cut(2, T)
        PT = cut(2, 4, P)
        RTMP = cut(2, L)
        cut = Cut(AR)
        KTOK = cut(NT, 4 * DK)
        VTOK = cut(NT, 4 * DK)
        DIR = [{n: cut(4, P) for n in ("gU", "dec", "decT", "A", "AT", "Dm", "Em", "kbe", "kg", "vb", "S", "sp")}
               for _ in range(2)]
        OD = HB[:, :].rearrange("p (d t n) -> p d t n", d=2, t=NT)
        SQ = HB[:, 0:2 * T].rearrange("p (a t) -> p a t", a=2)
        cut = Cut(AR)
        H2T = cut(FF // P, T)
        SG = cut(2, T)
        cut = Cut(AR)
        QC = cut(KB, L)
        KC = cut(KB, T)
        VC = cut(NT, D)
        PC = cut(2, T)
        PCT = cut(2, 4, P)
        BM = cut(4, L)
        OC = HB[:, 0:KB * L].rearrange("p (k t) -> p k t", t=L)
        cut = Cut(QB)
        XG = cut(KB, P)
        HE = cut(2, 512)
        HET = cut(FFE // P, P)
        cut = Cut(HB, KB * L)
        SE = cut(2, 512)
        YE = cut(1, D)
        fT = HB[:, 0:KB * L].rearrange("p (k t) -> p k t", t=L)
        SEL = ZS[:, 0, :].rearrange("p (a b) -> p a b", a=4)
        SELT = ZS[:, 1, 0:2 * P].rearrange("p (a b) -> p a b", a=2)
        RTB = ZS[:, 2, :]
        FG = YB[:, 0:2, :].rearrange("p a b -> p (a b)")
        GE = YB[:, 2:4, :].rearrange("p a b -> p (a b)")
        ACC = HB[:, 0:2 * D].rearrange("p (t n) -> p t n", t=2)

        TILE_OF = [[2, 3, 0, 1], [3, 2, 1, 0]]
        M_ITEMS = [(h, t, 4 if t < 2 else 2) for h in range(H_B) for t in range(NT)]
        N_ITEMS = [(h, t, 4) for h in range(H_C) for t in range(2)]

        PS = ctx.enter_context(nc.psum_tensor("PS", [P, 8, 512], f32))

        done = {e: sem(f"{e}_stage_done") for e in WORKS}

        def qkv_place(i):
            if i < 8:
                return QC[:, i, :], PS[:, i % 4, 0:L]
            if i < 16:
                return KC[:, i - 8, :], PS[:, i % 4, :]
            return VC[:, i % 4, 512 * (i // 20):512 * (i // 20) + 512], PS[:, i % 4, :]

        def begin(eng, me, stage):
            for e in WORKS:
                n = sum(s in WORKS[e] for s in STAGES[:STAGES.index(stage)])
                if e != me and n:
                    eng.wait_ge(done[e], n)

        arrived = [sem(f"weights_arrived{i}") for i in range(RING)]
        arrived_e = [sem(f"expert_weights_arrived{i}") for i in range(RING_E)]
        ada_mm, win_mm, tok_mm, mproj_mm = sem("ada_mm"), sem("win_mm"), sem("tok_mm"), sem("mproj_mm")
        out_mm, up_mm, down_mm, qkv_mm = sem("out_mm"), sem("up_mm"), sem("down_mm"), sem("qkv_mm")
        stream = []

        def by_rows(w, r0, nb, c0, nc_):
            return w[r0:r0 + nb * P, c0:c0 + nc_].rearrange("(k p) n -> p k n", p=P)

        first = {}

        def chunk(key, shape, source, free):
            first.setdefault(key, len(stream))
            stream.append((shape, source, free))

        def ada_chunks(l):
            for g in range(3):
                for q in range(4):
                    chunk(f"ada{l}", (2, 2048), by_rows(A["ada_w"][l], 256 * q, 2, 2048 * g, 2048),
                          (ada_mm, 12 * l + 4 * g + q + 1))

        ada_chunks(0)
        w_in = A["ev_w_in"][0]
        for c in range(3):
            chunk("win", (KB, 512), by_rows(w_in, 0, KB, 512 * c, 512), (win_mm, 4 * c + 4))
        TOKC = [(Z0, 512), (AB0, REST // 2), (AB0 + REST // 2, REST // 2)]
        for c, (c0, n) in enumerate(TOKC):
            chunk("tok", (KB, n), by_rows(w_in, 0, KB, c0, n), (tok_mm, 4 * c + 4))
        chunk("mproj", (3, H_B * QD), by_rows(A["ev_w_uq"][0], 0, 3, 0, H_B * QD), (mproj_mm, H_B))
        chunk("mproj", (2, H_B * 128), by_rows(A["ev_w_ukv"][0], 0, 2, 0, H_B * 128), (mproj_mm, 2 * H_B + NT))
        for n in range(2):
            chunk("out0", (KB, 512), by_rows(A["ev_w_out"][0], 0, KB, 512 * n, 512), (out_mm, 4 * n + 4))
        for s in range(FF // 256):
            chunk("up", None, (by_rows(A["ev_ffn_wg"][0], 0, KB, 256 * s, 256),
                               by_rows(A["ev_ffn_wu"][0], 0, KB, 256 * s, 256)), (up_mm, 2 * s + 2))
        DOWNC = [(0, 8), (8, 8), (16, 6)]
        for n in range(2):
            for c, (k0, nk) in enumerate(DOWNC):
                chunk("down", (nk, 512), by_rows(A["ev_ffn_wd"][0], k0 * P, nk, 512 * n, 512), (down_mm, 3 * n + c + 1))
        ada_chunks(1)
        for c in range(6):
            chunk("qkv", (KB, 512), by_rows(A["od_w_qkv"][0], 0, KB, 512 * c, 512), (qkv_mm, 4 * c + 4))
        for n in range(2):
            chunk("out1", (KB, 512), by_rows(A["od_w_out"][0], 0, KB, 512 * n, 512), (out_mm, 8 + 2 * n + 2))

        def slot(i, shape):
            v = BIG[:, (i % RING) * SLOT:(i % RING) * SLOT + shape[0] * shape[1]]
            return v.rearrange("p (k n) -> p k n", k=shape[0])

        loads_before = [0] * RING
        counts = []
        for i, (shape, source, _) in enumerate(stream):
            loads_before[i % RING] += 1 if shape else 2
            counts.append(16 * loads_before[i % RING])

        def wait_chunk(eng, i):
            eng.wait_ge(arrived[i % RING], counts[i])
            return slot(i, stream[i][0] or (KB, 512))

        NUP, NDN = FFE // 512, FFE // 512
        NEC = 2 * NUP + NDN
        assert NEC % RING_E == 0
        gu_mm, dn_mm = sem("gate_up_mm"), sem("expert_down_mm")

        s_const, s_rows, s_x, s_bias, s_misc = (sem(n) for n in ("const_in", "rows_in", "x_in", "ada_b_in", "misc_in"))
        rows_zero, st_zero = sem("rows_zeroed"), sem("padding_zeroed")
        sm_tr, sm_cols, st_ready = sem("small_transposed"), sem("small_columns"), sem("silu_c_ready")
        mod_rows, ada_tr, mod_cols, gb_mm = sem("mod_rows"), sem("ada_transposed"), sem("mod_columns"), sem("gate_rows_mm")
        norm_sd, norm_rstd, xn_ready, norm_tr, norm_ev = (sem(n) for n in (
            "norm_sd", "norm_rstd", "xn_ready", "norm_transposed", "norm_evacuated"))
        cin_ready, conv_done, win_ev = sem("conv_input"), sem("conv_done"), sem("win_used")
        tok_ev = sem("tok_evacuated")
        dve_seq, act_seq, pool_seq = sem("dve_seq"), sem("act_seq"), sem("pool_seq")
        m_sd, m_rstd, m_nrm, m_tr, m_trev = (sem(n) for n in ("mla_sd", "mla_rstd", "mla_normed", "mla_transposed",
                                                              "mla_latents"))
        mproj_ev, rot_mm, rot_ev = sem("mproj_evacuated"), sem("rot_mm"), sem("rope_done")
        att_s, att_max, att_p, att_pn, att_tr, att_pt, att_o, att_oe = (sem(n) for n in (
            "scores_mm", "scores_max", "probs_ready", "probs_normed", "probs_transposed", "probs_t_ready", "pv_mm",
            "pv_evacuated"))
        bias_in, bias_ok = [sem(f"rpb_in{i}") for i in range(4)], sem("bias_masked")
        l2_sq, l2_ss, l2_sd, l2_r, l2_bc, l2_ok, l2_tr, l2_ev = (sem(n) for n in (
            "l2_squares", "l2_sums", "l2_sd", "l2_rstd", "l2_broadcast", "l2_scaled", "kv_transposed", "kv_tokens"))
        dirs = range(2)

        def both(d, n):
            return 2 * (n - 1) + d + 1

        g_gU, g_seg, g_exp, g_msk, g_kk, g_A, g_At, g_AT, g_D1 = (sem(n) for n in (
            "gU", "seg_mm", "decay", "decay_masked", "kk_mm", "A_ready", "A_transposed", "AT_ready", "inverse1"))
        g_LT, g_M1, g_M1e, g_PQ, g_DE, g_eg, g_sm, g_vec, g_wT, g_wTe, g_vn, g_vne, g_o, g_oe, g_S = (sem(n) for n in (
            "level_masked", "M1_mm", "M1_ready", "update_mm", "inverse", "sums_exp", "sums_mm", "kbe_kg_vb", "wT_mm",
            "wT_ready", "vnew_mm", "vnew_ready", "o_mm", "o_ready", "S_ready"))
        gb_ready, go_tr, go_ev, go_sd, go_r, go_n = (sem(n) for n in ("g_beta", "o_transposed", "o_columns", "o_sd",
                                                                "o_rstd", "o_gated"))
        out_ev = sem("out_added")
        up_silu, up_ev = sem("up_silu"), sem("up_ready")
        down_ev = sem("down_added")
        qkv_ev = [sem(f"qkv_evacuated{i}") for i in range(2)]
        rt_mm, rt_ev, rk_mm, rt_ok, rt_tab = (sem(n) for n in ("router_mm", "router_read", "rank_mm", "chosen",
                                                              "wave_tables"))
        e_sel, e_gmm, e_gev, e_tr, e_trev = (sem(n) for n in ("sel_ready", "gather_mm", "gathered", "sel_transposed",
                                                             "sel_t_ready"))
        e_silu, e_h, e_htr, e_htev, e_y, e_sc, e_add = (sem(n) for n in (
            "expert_silu", "expert_h", "h_transposed", "h_columns", "y_ready", "scatter_mm", "scatter_added"))
        s_out = sem("out_stored")
        bias_zero, cin_zero, conv_ev, tok_z = sem("ada_b_zeroed"), sem("conv_padding_zeroed"), sem("conv_evacuated"), sem("z_ready")
        sp_in, sp_ln, go_ss, s_fg = sem("softplus_in"), sem("softplus_ln"), sem("o_sums"), sem("final_gain_in")
        ge_ready, rt_d, rt_e, fin_x = sem("expert_gate_rows"), sem("logit_difference"), sem("logit_exp"), sem("final_x")
        fin_sd, fin_r, fin_n, fin_ok = sem("final_sd"), sem("final_rstd"), sem("final_normed"), sem("final_ready")

        block = ctx.enter_context(nc.Block())

        @block.sync
        def _(sp):
            for i, (shape, source, _) in enumerate(stream):
                if i >= RING:
                    sp.wait_ge(*stream[i - RING][2])
                if shape:
                    sp.dma_start(slot(i, shape), source).then_inc(arrived[i % RING], 16)
                else:
                    for half in range(2):
                        sp.dma_start(slot(i, (KB, 512))[:, :, 256 * half:256 * half + 256],
                                     source[half]).then_inc(arrived[i % RING], 16)

            begin(sp, None, "natt")
            rpb = A["od_rpb"]
            for j in range(2 * H_C):
                h, qt = j // 2, j % 2
                if j >= 4:
                    sp.wait_ge(att_s, len(M_ITEMS) + j - 3)
                for r in range(2):
                    at = h * RPB_R * RPB_C + (WIN_R - 1 - (2 * qt + r)) * RPB_C + WIN_C - GRID_W
                    src = bass.AP(tensor=rpb.tensor, offset=at, ap=[[1, GRID_W], [RPB_C, ROWS], [1, GRID_W]])
                    sp.dma_start(BM[64 * r:64 * r + 64, j % 4, :].rearrange("p (a b) -> p a b", a=ROWS),
                                 src).then_inc(bias_in[j % 4], 16)

            wg, wu = (A[n].rearrange("o e (k p) n -> (o e) p k n", p=P) for n in ("od_exp_wg", "od_exp_wu"))
            wd = A["od_exp_wd"].rearrange("o e (k p) n -> (o e) p k n", p=P)

            def wave_loads(w, e, first):
                for i in range(NEC):
                    if i >= RING_E:
                        j = i - RING_E
                        if j < 2 * NUP:
                            sp.wait_ge(gu_mm, NUP * w + j // 2 + 1)
                        else:
                            sp.wait_ge(dn_mm, NDN * w + j - 2 * NUP + 1)
                    elif first and i == RING:
                        begin(sp, None, "norm3")
                    elif first and i < RING:
                        sp.wait_ge(*stream[-RING:][(i - len(stream)) % RING][2])
                    elif not first:
                        sp.wait_ge(dn_mm, NDN * w + i - RING_E + 1)
                    dst = BIG[:, (i % RING_E) * SLOT:(i % RING_E) * SLOT + SLOT]
                    if i < 2 * NUP:
                        src = (wg, wu)[i % 2][e, :, :, 512 * (i // 2):512 * (i // 2) + 512]
                        sp.dma_start(dst.rearrange("p (k n) -> p k n", k=KB), src).then_inc(arrived_e[i % RING_E], 16)
                    else:
                        j = 4 * (i - 2 * NUP)
                        sp.dma_start(dst.rearrange("p (k n) -> p k n", k=4),
                                     wd[e, :, j:j + 4, :]).then_inc(arrived_e[i % RING_E], 16)

            wave_loads(0, 0, True)
            with sp.Fori(1, E) as w:
                wave_loads(w, w, False)
            sp.wait_ge(rt_tab, 1)
            waves = sp.value_load(RI[0:1, 0:1], min_val=E, max_val=WAVES)
            with sp.If(waves > E):
                with sp.Fori(E, waves) as w:
                    e = sp.value_load(RI[0:1, bass.ds(w - E + 1, 1)], min_val=0, max_val=E - 1)
                    wave_loads(w, e, False)

            sp.wait_ge(fin_ok, 2)
            sp.dma_start(out[0].rearrange("(t p) n -> p t n", p=P), X[:, 0:2, :]).then_inc(s_out, 16)
            sp.wait_ge(s_out, 16)

        @block.gpsimd
        def _(pool):
            def seq(ins, count=[0]):
                count[0] += 1
                ins.then_inc(pool_seq, 1)
                pool.wait_ge(pool_seq, count[0])

            pool.memset(ROWSB[:, :], 0.0).then_inc(rows_zero, 1)
            pool.memset(ST[:, :, :], 0.0).then_inc(st_zero, 1)
            pool.memset(ONE[:, :], 1.0).then_inc(done["pool"], 1)

            begin(pool, "pool", "gdn")

            def heads(m):
                return CM[:, m, :].rearrange("p (a b) -> p a b", a=1).to_broadcast([P, 4, P])

            for s in range(NT):
                for d in dirs:
                    b, t = DIR[d], TILE_OF[d][s]
                    if s:
                        pool.wait_ge(g_DE, both(d, (LEVELS - 1) * s))
                    for h in range(4):
                        last = pool.tensor_scalar(b["gU"][:, h, :], CM[:, UP if d == 0 else LO, :],
                                                  GB8[:, t, 0, 4 * d + h:4 * d + h + 1], None, ALU.mult)
                    last.then_inc(g_gU, 1)
                for d in dirs:
                    b = DIR[d]
                    pool.wait_ge(g_exp, both(d, s + 1))
                    pool.tensor_tensor(b["dec"], b["dec"], heads(SLO if d == 0 else SUP), ALU.mult)
                    pool.tensor_tensor(b["decT"], b["decT"], heads(UP if d == 0 else LO), ALU.mult).then_inc(g_msk, 1)
                for d in dirs:
                    b = DIR[d]
                    pool.wait_ge(g_AT, both(d, s + 1))
                    if s:
                        pool.wait_ge(g_vn, both(d, s))
                    seq(pool.tensor_tensor(b["sp"], b["A"], heads(LEV), ALU.mult))
                    seq(pool.tensor_tensor(b["Dm"], heads(IDENT), b["sp"], ALU.subtract))
                    seq(pool.tensor_tensor(b["sp"], b["AT"], heads(LEV), ALU.mult))
                    pool.tensor_tensor(b["Em"], heads(IDENT), b["sp"], ALU.subtract).then_inc(g_D1, 1)
                for n in range(1, LEVELS):
                    for d in dirs:
                        b = DIR[d]
                        if n > 1:
                            pool.wait_ge(g_M1, both(d, (LEVELS - 1) * s + n - 1))
                        last = pool.tensor_tensor(b["gU"], b["AT"], heads(LEV + n), ALU.mult)
                        last.then_inc(g_LT, 1)
            pool.wait_ge(g_LT, both(1, (LEVELS - 1) * NT))
            pool.nop().then_inc(done["pool"], 1)

            begin(pool, "pool", "natt")
            for j in range(2 * H_C):
                pool.wait_ge(bias_in[j % 4], 32 * (j // 4 + 1))
                v = BM[:, j % 4, :].rearrange("p (a b) -> p a b", a=ROWS)
                m = WM[:, :].rearrange("p (a b) -> p a b", a=1).to_broadcast([P, ROWS, GRID_W])
                pool.tensor_tensor(v, v, m, ALU.add).then_inc(bias_ok, 1)
            pool.wait_ge(bias_ok, 2 * H_C)
            pool.nop().then_inc(done["pool"], 1)

        @block.scalar
        def _(act):
            def seq(ins, count=[0]):
                count[0] += 1
                ins.then_inc(act_seq, 1)
                act.wait_ge(act_seq, count[0])

            def everywhere(ap, n):
                return bass.AP(tensor=ap.tensor, offset=0, ap=[[0, P], [1, n]])

            def load_ada_b(l):
                rows = A["ada_b"][l:l + 1, :].rearrange("o (g c n) -> o g c n", g=3, c=4)
                for c in range(4):
                    for r in range(2):
                        act.dma_start(BADD[32 * c + r:32 * c + r + 1, :, :], rows[:, :, c, :]).then_inc(s_bias, 16)

            act.wait_ge(rows_zero, 1)
            act.dma_start(ROWSB[0:KB, :], A["c"].rearrange("o (k n) -> (o k) n", n=P)).then_inc(s_rows, 16)
            act.dma_start(ROWSB[KB:2 * KB, :], A["c_ctx"].rearrange("(k n) -> k n", n=P)).then_inc(s_rows, 16)
            act.dma_start(ROWSB[R_NG:R_NG + 4 * KB, :],
                          A["norm_g"].rearrange("l w (k n) -> (l w k) n", n=P)).then_inc(s_rows, 16)
            act.dma_start(ROWSB[R_CONV:R_CONV + 12 * TAPS, :],
                          A["ev_conv_w"].rearrange("o j (b n) -> (o j b) n", n=P)).then_inc(s_rows, 16)
            act.dma_start(ROWSB[R_QG:R_QG + 3, :],
                          A["ev_q_norm_g"].rearrange("o (k n) -> (o k) n", n=P)).then_inc(s_rows, 16)
            act.dma_start(ROWSB[R_KVG:R_KVG + 2, :],
                          A["ev_kv_norm_g"].rearrange("o (k n) -> (o k) n", n=P)).then_inc(s_rows, 16)
            act.dma_start(CM[:, :, :].rearrange("p a b -> p (a b)"), A["masks"]).then_inc(s_const, 16)
            act.dma_start(X[:, 0:2, :], A["x"][0].rearrange("(t p) n -> p t n", p=P)).then_inc(s_x, 16)
            act.dma_start(X[:, 2:4, :], A["ctx"][0].rearrange("(t p) n -> p t n", p=P)).then_inc(s_x, 16)
            act.dma_start(CS[NOPE:NOPE + ROPE, :, :], A["rope"]).then_inc(s_misc, 16)
            act.dma_start(WM[:, :], A["window"]).then_inc(s_misc, 16)
            act.dma_start(DTB[:, 0, :], everywhere(A["ev_dt_bias"], 8)).then_inc(s_misc, 16)
            act.dma_start(DTB[:, 1, :], everywhere(A["ev_a_log"], 8)).then_inc(s_misc, 16)
            act.dma_start(GG[:, :], everywhere(A["ev_gdn_norm_g"], P)).then_inc(s_misc, 16)
            act.dma_start(RW[:, :, :], A["od_router"][0].rearrange("(k p) n -> p k n", p=P)).then_inc(s_misc, 16)
            act.wait_ge(st_zero, 1)
            act.wait_ge(bias_zero, 1)
            load_ada_b(0)
            act.wait_ge(sm_cols, 1)
            act.activation(ST[:, :, 0:2], SM[:, 0:2 * KB].rearrange("p (r k) -> p k r", r=2),
                           ACT.Silu).then_inc(done["act"], 1)

            def norm(stage, n, nt0, xn):
                begin(act, "act", stage)
                for i in range(n):
                    seq(act.activation(xn(0), X[:, i, :], ACT.Square, accum_out=SS[:, i:i + 1]))
                act.activation(SS[:, 8:8 + n], SS[:, 0:n], ACT.Sqrt, bias=EPSC[:, 0:1], scale=1.0 / D).then_inc(norm_sd, 1)
                act.wait_ge(norm_rstd, ("norm0", "norm1", "norm2", "norm3").index(stage) + 1)
                for i in range(n):
                    if i >= 2:
                        act.wait_ge(norm_tr, nt0 + i - 1)
                    last = act.activation(xn(i), X[:, i, :], ACT.Copy, scale=SS[:, 16 + i:17 + i])
                    last.then_inc(xn_ready, 1)
                act.wait_ge(xn_ready, nt0 + n)
                act.nop().then_inc(done["act"], 1)

            act.wait_ge(s_misc, 96)
            act.activation(EA[:, :], DTB[:, 1, :], ACT.Exp).then_inc(done["act"], 1)

            norm("norm0", NT, 0, lambda i: XN[:, i % 2, :])

            begin(act, "act", "win")
            act.wait_ge(cin_zero, 1)

            def conv_in(b):
                act.wait_ge(win_mm, b + 1)
                if b >= 2:
                    act.wait_ge(conv_done, b - 1)
                act.activation(CIN[:, b % 2, :, 2:2 + L], PS[:, b % 4, :].rearrange("p (a t) -> p a t", a=2),
                               ACT.Copy).then_inc(cin_ready, 1)

            def conv_out(b):
                act.wait_ge(conv_done, b + 1)
                return act.activation(qkvT[:, b, :], CACC[:, b % 2, :], ACT.Silu)

            conv_in(0)
            for b in range(12):
                if b < 11:
                    conv_in(b + 1)
                conv_out(b).then_inc(conv_ev if b < 11 else done["act"], 1)

            begin(act, "act", "tok")
            for t in range(NT):
                act.wait_ge(tok_mm, t + 1)
                act.activation(ZS[:, t, :], PS[:, t % 4, :], ACT.Silu).then_inc(tok_z, 1)
            act.wait_ge(tok_z, NT)
            act.nop().then_inc(done["act"], 1)

            begin(act, "act", "mproj")
            for t in range(NT):
                seq(act.activation(PM[:, 0, 0:QR], P2[:, t, CQ0:CQ0 + QR], ACT.Square, accum_out=SS[:, t:t + 1]))
                seq(act.activation(PM[:, 0, 0:KVR], P2[:, t, CKV0:CKV0 + KVR], ACT.Square,
                                   accum_out=SS[:, 4 + t:5 + t]))
            act.activation(SS[:, 8:12], SS[:, 0:4], ACT.Sqrt, bias=EPSC[:, 0:1], scale=1.0 / QR).then_inc(m_sd, 1)
            act.activation(SS[:, 12:16], SS[:, 4:8], ACT.Sqrt, bias=EPSC[:, 0:1], scale=1.0 / KVR).then_inc(m_sd, 1)
            act.wait_ge(sp_in, 1)
            seq(act.activation(GB8[:, :, 0, :], GB8[:, :, 2, :], ACT.Abs))
            seq(act.activation(GB8[:, :, 0, :], GB8[:, :, 0, :], ACT.Exp, scale=-1.0))
            act.activation(GB8[:, :, 0, :], GB8[:, :, 0, :], ACT.Ln, bias=ONE[:, 0:1]).then_inc(sp_ln, 1)
            act.activation(GB8[:, :, 1, :], P2[:, :, 8:16], ACT.Sigmoid).then_inc(sp_ln, 1)
            for j in range(2 * H_B + NT):
                act.wait_ge(mproj_mm, j + 1)
                if j < H_B:
                    to, of = QT[0:QD, j, :], PS[0:QD, j % 4, :]
                elif j < 2 * H_B:
                    to, of = KT[0:NOPE, j - H_B, :], PS[0:NOPE, j % 4, :]
                else:
                    to, of = VB[:, j - 2 * H_B, :], PS[:, j % 4, :]
                act.activation(to, of, ACT.Copy).then_inc(mproj_ev, 1)
            act.wait_ge(mproj_ev, 2 * H_B + NT)
            act.nop().then_inc(done["act"], 1)

            def attention(items, base, pm, pt, scale):
                def exp(j):
                    n = items[j][2]
                    act.wait_ge(att_max, base + j + 1)
                    if j >= 2:
                        act.wait_ge(att_tr, base + j - 1)
                    act.activation(pm[:, j % 2, 0:n * P], PS[:, j % 2, 0:n * P], ACT.Exp, bias=RT[:, j % 2:j % 2 + 1],
                                   scale=scale, accum_out=RT[:, 4 + j % 2:5 + j % 2]).then_inc(att_p, 1)

                exp(0)
                for j in range(len(items)):
                    if j + 1 < len(items):
                        exp(j + 1)
                    act.wait_ge(att_tr, base + j + 1)
                    if j >= 2:
                        act.wait_ge(att_o, base + j - 1)
                    n = items[j][2]
                    act.activation(pt[:, j % 2, 0:n, :],
                                   PS[:, 2 + j % 2, 0:n * P].rearrange("p (a b) -> p a b", a=n),
                                   ACT.Copy).then_inc(att_pt, 1)
                act.wait_ge(att_pt, base + len(items))
                act.nop().then_inc(done["act"], 1)

            begin(act, "act", "matt")
            attention(M_ITEMS, 0, PM, PT, QD ** -0.5)

            begin(act, "act", "l2")
            for b in range(8):
                if b >= 2:
                    act.wait_ge(l2_ss, b - 1)
                act.activation(SQ[:, b % 2, :], qkvT[:, b, :], ACT.Square).then_inc(l2_sq, 1)
            act.wait_ge(l2_ss, 8)
            act.activation(SS[:, 0:16], PS[:, 0, 0:16], ACT.Sqrt, bias=EPSC[:, 1:2], scale=float(DK)).then_inc(l2_sd, 1)
            act.activation(SS[:, 16:32], PS[:, 0, 16:32], ACT.Sqrt, bias=EPSC[:, 0:1]).then_inc(l2_sd, 1)
            for i in range(8):
                act.wait_ge(l2_tr, i + 1)
                act.activation((KTOK, VTOK)[i % 2][:, i // 2, :], PS[:, 6 + i % 2, :], ACT.Copy).then_inc(l2_ev, 1)
            act.wait_ge(l2_ev, 8)
            act.nop().then_inc(done["act"], 1)

            begin(act, "act", "gdn")
            for s in range(NT):
                for d in dirs:
                    b, B = DIR[d], 4 * d
                    act.wait_ge(g_seg, both(d, s + 1))
                    act.activation(b["decT"], PS[:, B, :], ACT.Exp)
                    act.activation(b["dec"], PS[:, B + 1, :], ACT.Exp).then_inc(g_exp, 1)
                    act.wait_ge(g_sm, both(d, s + 1))
                    act.activation(EG[:, d, :], PS[:, B + 2, 0:12], ACT.Exp).then_inc(g_eg, 1)
                for d in dirs:
                    b, B = DIR[d], 4 * d
                    act.wait_ge(g_At, both(d, s + 1))
                    act.activation(b["AT"], PS[:, B, :], ACT.Copy).then_inc(g_AT, 1)
                for n in range(1, LEVELS):
                    for d in dirs:
                        b, B = DIR[d], 4 * d
                        act.wait_ge(g_M1, both(d, (LEVELS - 1) * s + n))
                        act.activation(b["dec"], PS[:, B + 1, :], ACT.Copy).then_inc(g_M1e, 1)
                for d in dirs:
                    b, B = DIR[d], 4 * d
                    act.wait_ge(g_wT, both(d, s + 1))
                    act.activation(b["Dm"], PS[:, B + 1, :], ACT.Copy, scale=-1.0).then_inc(g_wTe, 1)
                for d in dirs:
                    b, B = DIR[d], 4 * d
                    act.wait_ge(g_vn, both(d, s + 1))
                    act.activation(b["A"], PS[:, B, :], ACT.Copy).then_inc(g_vne, 1)
            for d in dirs:
                act.wait_ge(g_vne, both(d, NT))
            act.nop().then_inc(done["act"], 1)

            begin(act, "act", "gout")
            act.wait_ge(go_ss, 1)
            act.activation(SS[:, 16:32], SS[:, 0:16], ACT.Sqrt, bias=EPSC[:, 0:1], scale=1.0 / DK).then_inc(go_sd, 1)
            for t in range(NT):
                act.wait_ge(go_tr, t + 1)
                last = act.activation(mixT[:, 0:4, t * P:t * P + P], PS[:, t, :].rearrange("p (h n) -> p h n", h=4),
                                      ACT.Copy)
                last.then_inc(go_ev if t < NT - 1 else done["act"], 1)

            def gate_rows(stage, k, to, n):
                begin(act, "act", stage)
                act.wait_ge(gb_mm, k + 1)
                for r in range(n):
                    for c in range(2):
                        last = act.activation(to[:, r, 512 * c:512 * c + 512], PS[:, 4 + 2 * r + c, :], ACT.Copy)
                last.then_inc(done["act"], 1)

            gate_rows("out0", 0, GB, 2)
            norm("norm1", NT, 4, lambda i: XN[:, i % 2, :])

            begin(act, "act", "up")
            for f in range(FF // P):
                act.wait_ge(up_mm, f + 1)
                if f >= 2:
                    act.wait_ge(up_ev, f - 1)
                act.activation(SG[:, f % 2, :], PS[:, 2 * (f % 2), :], ACT.Silu).then_inc(up_silu, 1)
            act.wait_ge(up_silu, FF // P)
            act.nop().then_inc(done["act"], 1)

            gate_rows("down", 1, GB, 2)

            begin(act, "act", "ada1")
            act.wait_ge(bias_zero, 2)
            load_ada_b(1)
            act.dma_start(FG, everywhere(A["final_norm_g"], D)).then_inc(s_fg, 16)
            act.nop().then_inc(done["act"], 1)

            norm("norm2", NT, 8, lambda i: XN[:, i % 2, :])

            begin(act, "act", "qkv")
            for i in range(0, 24, 2):
                act.wait_ge(qkv_mm, i + 1)
                to, of = qkv_place(i)
                act.activation(to, of, ACT.Copy).then_inc(qkv_ev[0], 1)
            act.wait_ge(qkv_ev[0], 12)
            act.nop().then_inc(done["act"], 1)

            begin(act, "act", "natt")
            attention(N_ITEMS, len(M_ITEMS), PC, PCT, DH ** -0.5)

            gate_rows("out1", 2, GB, 1)
            norm("norm3", 2, 12, lambda i: X[:, 2 + i, :])

            begin(act, "act", "route")
            act.wait_ge(gb_mm, 4)
            for c in range(2):
                last = act.activation(GE[:, 512 * c:512 * c + 512], PS[:, 4 + c, :], ACT.Copy)
            last.then_inc(ge_ready, 1)
            act.wait_ge(rt_d, 1)
            act.activation(RTB[:, 80:82], RTB[:, 82:84], ACT.Exp).then_inc(rt_e, 1)
            act.wait_ge(rt_e, 1)
            act.wait_ge(ge_ready, 1)
            act.nop().then_inc(done["act"], 1)

            begin(act, "act", "moe")
            waves = act.value_load(RI[0:1, 0:1], min_val=E, max_val=WAVES)
            with act.Fori(0, waves) as w:
                act.wait_ge(e_tr, w + 1)
                act.activation(SELT, PS[:, 6, 0:2 * P].rearrange("p (a b) -> p a b", a=2), ACT.Copy).then_inc(e_trev, 1)

                def silu(s):
                    act.wait_ge(gu_mm, NUP * w + s + 1)
                    if s >= 2:
                        act.wait_ge(e_h, NUP * w + s - 1)
                    act.activation(SE[:, s % 2, :], PS[:, 2 * (s % 2), :], ACT.Silu).then_inc(e_silu, 1)

                silu(0)
                for s in range(NUP):
                    if s < NUP - 1:
                        silu(s + 1)
                    act.wait_ge(e_htr, NUP * w + s + 1)
                    act.activation(HET[:, 4 * s:4 * s + 4, :], PS[:, 4 + s % 2, :].rearrange("p (a b) -> p a b", a=4),
                                   ACT.Copy).then_inc(e_htev, 1)
                act.wait_ge(dn_mm, NDN * w + NDN)
                for n in range(2):
                    last = act.activation(YE[:, 0, 512 * n:512 * n + 512], PS[:, 6 + n, :], ACT.Copy)
                last.then_inc(e_y, 1)
            act.nop().then_inc(done["act"], 1)

            act.wait_ge(fin_x, 2)
            for i in range(2):
                seq(act.activation(QB[:, 0:D], X[:, i, :], ACT.Square, accum_out=SS[:, i:i + 1]))
            act.activation(SS[:, 8:10], SS[:, 0:2], ACT.Sqrt, bias=EPSC[:, 0:1], scale=1.0 / D).then_inc(fin_sd, 1)

        @block.vector
        def _(dve):
            def seq(ins, count=[0]):
                count[0] += 1
                ins.then_inc(dve_seq, 1)
                dve.wait_ge(dve_seq, count[0])

            def end(ins):
                ins.then_inc(done["dve"], 1)

            dve.memset(EPSC[:, 0:1], EPS)
            dve.memset(EPSC[:, 1:2], EPS * DK)
            dve.memset(BADD, 0.0).then_inc(bias_zero, 1)
            dve.wait_ge(sm_tr, 1)
            dve.tensor_copy(SM[:, :], PS[:, 7, 0:P]).then_inc(sm_cols, 1)
            dve.wait_ge(sm_cols, 1)
            dve.nop().then_inc(done["dve"], 1)

            def ada(l):
                begin(dve, "dve", f"ada{l}")
                if l:
                    dve.memset(BADD, 0.0).then_inc(bias_zero, 1)
                dve.wait_ge(s_bias, 128 * (l + 1))
                for g in range(3):
                    dve.wait_ge(ada_mm, 12 * l + 4 * g + 4)
                    dve.tensor_tensor(MOD[:, g, :], PS[:, g, :], BADD[:, g, :], ALU.add).then_inc(mod_rows, 1)
                for g in range(3):
                    dve.wait_ge(ada_tr, 3 * l + g + 1)
                    v = PS[:, 3 + g, :].rearrange("p (j c q) -> p j c q", j=4, c=4)
                    seq(dve.tensor_copy(MT[:, g, :, :, :], v[:, :, :, 0:2]))
                for which in range(2):
                    sh, sc = ((0, 0), (0, 2)) if which == 0 else ((1, 2), (2, 0))
                    ng = SM[:, R_NG + (2 * l + which) * KB:R_NG + (2 * l + which + 1) * KB]
                    for r in range(2):
                        for c in range(2):
                            to = slice(4 * c, 4 * c + 4)
                            dve.scalar_tensor_tensor(AB[:, which, r, 0, to], MT[:, sc[0], :, sc[1] + c, r], 1.0,
                                                     ng[:, to], ALU.add, ALU.mult)
                            last = dve.tensor_copy(AB[:, which, r, 1, to], MT[:, sh[0], :, sh[1] + c, r])
                end(last)

            def norm(stage, n, nt0, l, which, dst):
                idx = ("norm0", "norm1", "norm2", "norm3").index(stage)
                begin(dve, "dve", stage)
                dve.wait_ge(norm_sd, idx + 1)
                dve.reciprocal(SS[:, 16:16 + n], SS[:, 8:8 + n]).then_inc(norm_rstd, 1)
                for i in range(n):
                    dve.wait_ge(norm_tr, nt0 + i + 1)
                    for k in range(KB):
                        r = i // 2
                        last = dve.tensor_scalar(dst[:, k, i * P:i * P + P],
                                                 PS[:, 2 * (i % 2) + k // 4, (k % 4) * P:(k % 4) * P + P],
                                                 AB[:, which, r, 0, k:k + 1], AB[:, which, r, 1, k:k + 1],
                                                 ALU.mult, ALU.add)
                    last.then_inc(norm_ev if i < n - 1 else done["dve"], 1)

            ada(0)
            norm("norm0", NT, 0, 0, 0, hT)

            begin(dve, "dve", "win")
            dve.memset(CIN, 0.0).then_inc(cin_zero, 1)
            for b in range(12):
                dve.wait_ge(cin_ready, b + 1)
                if b >= 2:
                    dve.wait_ge(conv_ev, b - 1)
                acc = CACC[:, b % 2, :].rearrange("p (a t) -> p a t", a=2)
                for j in range(TAPS):
                    w = SM[:, R_CONV + 12 * j + b:R_CONV + 12 * j + b + 1]
                    of = CIN[:, b % 2, :, j:j + L]
                    if j == 0:
                        seq(dve.tensor_scalar(acc, of, w, None, ALU.mult))
                    else:
                        ins = dve.scalar_tensor_tensor(acc, of, w, acc, ALU.mult, ALU.add)
                        if j < TAPS - 1:
                            seq(ins)
                ins.then_inc(conv_done, 1)
            dve.wait_ge(conv_done, 12)
            dve.nop().then_inc(done["dve"], 1)

            begin(dve, "dve", "tok")
            for j in range(NT, 3 * NT):
                dve.wait_ge(tok_mm, j + 1)
                c, t = j // NT - 1, j % NT
                dve.tensor_copy(P2[:, t, c * (REST // 2):(c + 1) * (REST // 2)],
                                PS[:, j % 4, 0:REST // 2]).then_inc(tok_ev, 1)
            dve.wait_ge(tok_ev, 2 * NT)
            dve.nop().then_inc(done["dve"], 1)

            begin(dve, "dve", "mproj")
            dve.wait_ge(s_misc, 96)
            dt = DTB[:, 0:1, :].to_broadcast([P, NT, 8])
            dve.tensor_tensor(GB8[:, :, 2, :], P2[:, :, 0:8], dt, ALU.add).then_inc(sp_in, 1)
            dve.wait_ge(m_sd, 2)
            seq(dve.reciprocal(SS[:, 16:24], SS[:, 8:16]))
            for t in range(NT):
                v = P2[:, t, CQ0:CQ0 + QR]
                dve.tensor_scalar(v, v, SS[:, 16 + t:17 + t], None, ALU.mult)
                v = P2[:, t, CKV0:CKV0 + KVR]
                last = dve.tensor_scalar(v, v, SS[:, 20 + t:21 + t], None, ALU.mult)
            last.then_inc(m_nrm, 1)
            for k in range(3):
                dve.wait_ge(m_tr, k + 1)
                dve.tensor_scalar(CQT[:, k, :], PS[:, k, :], SM[:, R_QG + k:R_QG + k + 1], None,
                                  ALU.mult).then_inc(m_trev, 1)
            for k in range(2):
                dve.wait_ge(m_tr, k + 4)
                dve.tensor_scalar(CKVT[:, k, :], PS[:, 3 + k, :], SM[:, R_KVG + k:R_KVG + k + 1], None,
                                  ALU.mult).then_inc(m_trev, 1)
            dve.wait_ge(m_tr, 6)
            dve.tensor_copy(KT[NOPE:QD, 0, :], PS[NOPE:QD, 5, :]).then_inc(m_trev, 1)
            dve.wait_ge(sp_ln, 2)
            seq(dve.scalar_tensor_tensor(GB8[:, :, 2, :], GB8[:, :, 2, :], 0.0, GB8[:, :, 0, :], ALU.max, ALU.add))
            ea = EA[:, 0:1, :].to_broadcast([P, NT, 8])
            seq(dve.scalar_tensor_tensor(GB8[:, :, 0, :], GB8[:, :, 2, :], -1.0, ea, ALU.mult, ALU.mult))
            rs = slice(NOPE, QD)
            for j in range(H_B + 1):
                dve.wait_ge(rot_mm, j + 1)
                v = (QT[rs, j, 0:L] if j < H_B else KT[rs, 0, 0:L])
                seq(dve.tensor_tensor(RTMP[rs, j % 2, :], PS[rs, 4 + j % 2, 0:L], CS[rs, 1, :], ALU.mult))
                seq(dve.tensor_tensor(v, v, CS[rs, 0, :], ALU.mult))
                ins = dve.tensor_tensor(v, v, RTMP[rs, j % 2, :], ALU.add)
                ins.then_inc(rot_ev, 1)
            dve.wait_ge(rot_ev, H_B + 1)
            for h in range(1, H_B):
                last = dve.tensor_copy(KT[rs, h, :], KT[rs, 0, :])
            end(last)

            def attention(items, base, pm, out_of, scale):
                def largest(j):
                    n = items[j][2]
                    dve.wait_ge(att_s, base + j + 1)
                    seq(dve.tensor_reduce(RT[:, 2 + j % 2:3 + j % 2], PS[:, j % 2, 0:n * P], AX.X, ALU.max))
                    dve.tensor_scalar(RT[:, j % 2:j % 2 + 1], RT[:, 2 + j % 2:3 + j % 2], -scale, None,
                                      ALU.mult).then_inc(att_max, 1)

                def take_out(j):
                    dve.wait_ge(att_o, base + j + 1)
                    r0 = 64 * (items[j][0] % 2)
                    dve.tensor_copy(out_of(j), PS[r0:r0 + 64, 4 + j % 2, 0:P]).then_inc(att_oe, 1)

                largest(0)
                for j in range(len(items)):
                    if j + 1 < len(items):
                        largest(j + 1)
                    dve.wait_ge(att_p, base + j + 1)
                    seq(dve.reciprocal(RT[:, 6 + j % 2:7 + j % 2], RT[:, 4 + j % 2:5 + j % 2]))
                    v = pm[:, j % 2, 0:items[j][2] * P]
                    dve.tensor_scalar(v, v, RT[:, 6 + j % 2:7 + j % 2], None, ALU.mult).then_inc(att_pn, 1)
                    if j:
                        take_out(j - 1)
                take_out(len(items) - 1)
                dve.wait_ge(att_oe, base + len(items))
                dve.nop().then_inc(done["dve"], 1)

            begin(dve, "dve", "matt")

            def out_of(j):
                h, t, _ = M_ITEMS[j]
                return YB[64 * (h % 2):64 * (h % 2) + 64, h // 2, t * P:t * P + P]

            attention(M_ITEMS, 0, PM, out_of, QD ** -0.5)

            begin(dve, "dve", "l2")
            for d in dirs:
                dve.memset(DIR[d]["S"], 0.0)
            dve.wait_ge(l2_sd, 2)
            dve.reciprocal(SS[:, 32:64], SS[:, 0:32]).then_inc(l2_r, 1)
            for b in range(8):
                dve.wait_ge(l2_bc, b + 1)
                dve.tensor_tensor(qkvT[:, b, :], qkvT[:, b, :], PS[:, 2 + b % 4, :], ALU.mult).then_inc(l2_ok, 1)
            dve.wait_ge(l2_ok, 8)
            dve.nop().then_inc(done["dve"], 1)

            begin(dve, "dve", "gdn")
            for s in range(NT):
                for d in dirs:
                    b, B, t = DIR[d], 4 * d, TILE_OF[d][s]
                    dve.wait_ge(g_kk, both(d, s + 1))
                    dve.wait_ge(g_msk, both(d, s + 1))
                    for h in range(4):
                        beta = GB8[:, t, 1, 4 * d + h:4 * d + h + 1]
                        dve.scalar_tensor_tensor(b["A"][:, h, :], PS[:, B + 3, h * P:h * P + P], beta,
                                                 b["dec"][:, h, :], ALU.mult, ALU.mult)
                    dve.tensor_tensor(b["decT"], PS[:, B, :].rearrange("p (h n) -> p h n", h=4), b["decT"],
                                      ALU.mult).then_inc(g_A, 1)
                for d in dirs:
                    b, t = DIR[d], TILE_OF[d][s]
                    dve.wait_ge(g_eg, both(d, s + 1))
                    be = RT[:, 8 + 4 * d:12 + 4 * d]
                    seq(dve.tensor_tensor(be, GB8[:, t, 1, 4 * d:4 * d + 4], EG[:, d, 0:4], ALU.mult))
                    for h in range(4):
                        kk, vv = KTOK[:, t, h * DK:h * DK + DK], VTOK[:, t, h * DK:h * DK + DK]
                        dve.tensor_scalar(b["kbe"][:, h, :], kk, be[:, h:h + 1], None, ALU.mult)
                        dve.tensor_scalar(b["kg"][:, h, :], kk, EG[:, d, 4 + h:5 + h], None, ALU.mult)
                        last = dve.tensor_scalar(b["vb"][:, h, :], vv, GB8[:, t, 1, 4 * d + h:4 * d + h + 1], None,
                                                 ALU.mult)
                    last.then_inc(g_vec, 1)
                for n in range(1, LEVELS):
                    for d in dirs:
                        b, B = DIR[d], 4 * d
                        dve.wait_ge(g_PQ, both(d, (LEVELS - 1) * s + n))
                        if n < LEVELS - 1:
                            dve.tensor_tensor(b["Dm"], b["Dm"], PS[:, B + 2, :].rearrange("p (h n) -> p h n", h=4),
                                              ALU.subtract)
                        dve.tensor_tensor(b["Em"], b["Em"], PS[:, B + 3, :].rearrange("p (h n) -> p h n", h=4),
                                          ALU.subtract).then_inc(g_DE, 1)
                for d in dirs:
                    b, B, t = DIR[d], 4 * d, TILE_OF[d][s]
                    dve.wait_ge(g_o, both(d, s + 1))
                    seq(dve.tensor_copy(OD[:, d, t, :], PS[:, B + 3, :]))
                    for h in range(4):
                        hs = slice(h * DK, h * DK + DK)
                        dve.scalar_tensor_tensor(OD[:, d, t, hs], PS[:, B + 2, hs], EG[:, d, h:h + 1],
                                                 OD[:, d, t, hs], ALU.mult, ALU.add)
                        last = dve.scalar_tensor_tensor(b["S"][:, h, :], b["S"][:, h, :], EG[:, d, 8 + h:9 + h],
                                                        PS[:, B + 1, hs], ALU.mult, ALU.add)
                    last.then_inc(g_S, 1)
            for d in dirs:
                dve.wait_ge(g_S, both(d, NT))
            dve.nop().then_inc(done["dve"], 1)

            begin(dve, "dve", "gout")
            sq = AR[:, 0:NT * 512].rearrange("p (t n) -> p t n", t=NT)
            for t in range(NT):
                seq(dve.tensor_tensor(OD[:, 0, t, :], OD[:, 0, t, :], OD[:, 1, t, :], ALU.add))
                seq(dve.tensor_tensor(sq[:, t, :], OD[:, 0, t, :], OD[:, 0, t, :], ALU.mult))
                seq(dve.tensor_reduce(SS[:, 4 * t:4 * t + 4], sq[:, t, :].rearrange("p (h n) -> p h n", h=4), AX.X,
                                      ALU.add))
                z = ZS[:, t, :].rearrange("p (h n) -> p h n", h=4)
                gain = GG[:, :].rearrange("p (a n) -> p a n", a=1).to_broadcast([P, 4, P])
                seq(dve.tensor_tensor(z, z, gain, ALU.mult))
            dve.nop().then_inc(go_ss, 1)
            dve.wait_ge(go_sd, 1)
            seq(dve.reciprocal(SS[:, 32:48], SS[:, 16:32]))
            for t in range(NT):
                for h in range(4):
                    hs = slice(h * DK, h * DK + DK)
                    last = dve.scalar_tensor_tensor(OD[:, 0, t, hs], OD[:, 0, t, hs],
                                                    SS[:, 32 + 4 * t + h:33 + 4 * t + h], ZS[:, t, hs], ALU.mult, ALU.mult)
                last.then_inc(go_n, 1)
            dve.wait_ge(go_n, NT)
            dve.nop().then_inc(done["dve"], 1)

            def add_out(stage, base, nt):
                begin(dve, "dve", stage)
                dve.wait_ge(done["act"], sum(s in WORKS["act"] for s in STAGES[:STAGES.index(stage) + 1]))
                for i in range(2 * nt):
                    n, t = i // nt, i % nt
                    cols = slice(512 * n, 512 * n + 512)
                    dve.wait_ge(out_mm, base + i + 1)
                    seq(dve.tensor_tensor(ZS[:, i % 2, :], PS[:, i % 4, :], GB[:, t // 2, cols], ALU.mult))
                    dve.tensor_tensor(X[:, t, cols], X[:, t, cols], ZS[:, i % 2, :], ALU.add).then_inc(out_ev, 1)
                dve.wait_ge(out_ev, base + 2 * nt)
                dve.nop().then_inc(done["dve"], 1)

            add_out("out0", 0, NT)
            norm("norm1", NT, 4, 0, 1, hT)

            begin(dve, "dve", "up")
            for f in range(FF // P):
                dve.wait_ge(up_silu, f + 1)
                dve.tensor_tensor(H2T[:, f, :], SG[:, f % 2, :], PS[:, 2 * (f % 2) + 1, :], ALU.mult).then_inc(up_ev, 1)
            dve.wait_ge(up_ev, FF // P)
            dve.nop().then_inc(done["dve"], 1)

            begin(dve, "dve", "down")
            dve.wait_ge(done["act"], sum(s in WORKS["act"] for s in STAGES[:STAGES.index("down") + 1]))
            for n in range(2):
                dve.wait_ge(down_mm, 3 * n + 3)
                for t in range(NT):
                    cols = slice(512 * n, 512 * n + 512)
                    seq(dve.tensor_tensor(ZS[:, t % 2, :], PS[:, 4 * n + t, :], GB[:, t // 2, cols], ALU.mult))
                    dve.tensor_tensor(X[:, t, cols], X[:, t, cols], ZS[:, t % 2, :], ALU.add).then_inc(down_ev, 1)
            dve.wait_ge(down_ev, 2 * NT)
            dve.nop().then_inc(done["dve"], 1)

            ada(1)
            norm("norm2", NT, 8, 1, 0, hT)

            begin(dve, "dve", "qkv")
            for i in range(1, 24, 2):
                dve.wait_ge(qkv_mm, i + 1)
                to, of = qkv_place(i)
                dve.tensor_copy(to, of).then_inc(qkv_ev[1], 1)
            dve.wait_ge(qkv_ev[1], 12)
            dve.nop().then_inc(done["dve"], 1)

            begin(dve, "dve", "natt")

            def out_of(j):
                h, t, _ = N_ITEMS[j]
                return OC[64 * (h % 2):64 * (h % 2) + 64, h // 2, t * P:t * P + P]

            attention(N_ITEMS, len(M_ITEMS), PC, out_of, DH ** -0.5)

            add_out("out1", 2 * NT, 2)
            norm("norm3", 2, 12, 1, 1, fT)

            begin(dve, "dve", "route")

            def r8(at, n=2):
                return RTB[:, at:at + 8 * n].rearrange("p (t e) -> p t e", t=n)

            LG, PK1, PK2, TMP, WT, PRIO = r8(0), r8(16), r8(32), r8(48), r8(64), RTB[:, 96:104]
            M1, M2 = RTB[:, 84:86], RTB[:, 86:88]
            dve.wait_ge(rt_mm, 1)
            seq(dve.tensor_copy(LG, PS[:, 0, 0:16].rearrange("p (t e) -> p t e", t=2)))
            seq(dve.tensor_scalar(PRIO, CM[:, IOTA, 0:8], -1.0, 8.0, ALU.mult, ALU.add))

            def pick(mx, pk):
                seq(dve.tensor_reduce(mx, LG, AX.X, ALU.max))
                for t in range(2):
                    seq(dve.scalar_tensor_tensor(TMP[:, t, :], LG[:, t, :], mx[:, t:t + 1], PRIO, ALU.is_equal, ALU.mult))
                seq(dve.tensor_reduce(RTB[:, 88:90], TMP, AX.X, ALU.max))
                for t in range(2):
                    seq(dve.tensor_scalar(pk[:, t, :], TMP[:, t, :], RTB[:, 88 + t:89 + t], None, ALU.is_equal))

            pick(M1, PK1)
            seq(dve.scalar_tensor_tensor(LG, PK1, -3e38, LG, ALU.mult, ALU.add))
            pick(M2, PK2)
            dve.tensor_tensor(RTB[:, 82:84], M2, M1, ALU.subtract).then_inc(rt_d, 1)
            seq(dve.tensor_tensor(SELM[:, :, :], PK1, PK2, ALU.add))
            dve.nop().then_inc(rt_ev, 1)
            dve.wait_ge(rt_e, 1)
            G1, G2 = RTB[:, 90:92], RTB[:, 92:94]
            seq(dve.tensor_scalar(G1, RTB[:, 80:82], 1.0, None, ALU.add))
            seq(dve.reciprocal(G1, G1))
            seq(dve.tensor_tensor(G2, G1, RTB[:, 80:82], ALU.mult))
            for t in range(2):
                seq(dve.tensor_scalar(TMP[:, t, :], PK1[:, t, :], G1[:, t:t + 1], None, ALU.mult))
                seq(dve.scalar_tensor_tensor(WT[:, t, :], PK2[:, t, :], G2[:, t:t + 1], TMP[:, t, :], ALU.mult, ALU.add))
            dve.wait_ge(rk_mm, 1)
            RK = r8(0)
            for t in range(2):
                seq(dve.scalar_tensor_tensor(RK[:, t, :], PS[:, 1, 8 * t:8 * t + 8], 1.0, SELM[:, t, :], ALU.add,
                                             ALU.mult))
            seq(dve.tensor_scalar(RK, RK, -1.0, None, ALU.add))
            OV, ORD, OH = RTB[:, 104:112], RTB[:, 112:120], RTB[:, 120:128]
            seq(dve.tensor_scalar(OV, PS[:, 1, 16:24], float(P), None, ALU.is_gt))
            seq(dve.memset(ORD, 0.0))
            for e in range(1, E):
                seq(dve.tensor_tensor(ORD[:, e:e + 1], ORD[:, e - 1:e], OV[:, e - 1:e], ALU.add))
            for t in range(2):
                seq(dve.tensor_copy(WR[:, t, 0:E], RK[:, t, :]))
                seq(dve.tensor_copy(WG[:, t, 0:E], WT[:, t, :]))
            seq(dve.tensor_reduce(RF[:, 0:1], OV, AX.X, ALU.add))
            seq(dve.tensor_scalar(RF[:, 0:1], RF[:, 0:1], float(E), None, ALU.add))
            for j in range(WAVES - E):
                seq(dve.scalar_tensor_tensor(OH, ORD, float(j), OV, ALU.is_equal, ALU.mult))
                seq(dve.tensor_tensor(PRIO, OH, CM[:, IOTA, 0:8], ALU.mult))
                seq(dve.tensor_reduce(RF[:, 1 + j:2 + j], PRIO, AX.X, ALU.add))
                for t in range(2):
                    seq(dve.scalar_tensor_tensor(PRIO, RK[:, t, :], float(1 - P), OH, ALU.add, ALU.mult))
                    seq(dve.tensor_reduce(WR[:, t, E + j:E + j + 1], PRIO, AX.X, ALU.add))
                    seq(dve.tensor_scalar(WR[:, t, E + j:E + j + 1], WR[:, t, E + j:E + j + 1], -1.0, None, ALU.add))
                    seq(dve.tensor_tensor(PRIO, WT[:, t, :], OH, ALU.mult))
                    seq(dve.tensor_reduce(WG[:, t, E + j:E + j + 1], PRIO, AX.X, ALU.add))
            dve.tensor_copy(RI[:, 0:4], RF[:, 0:4]).then_inc(rt_tab, 1)
            dve.wait_ge(rt_tab, 1)
            dve.nop().then_inc(done["dve"], 1)

            begin(dve, "dve", "moe")
            waves = dve.value_load(RI[0:1, 0:1], min_val=E, max_val=WAVES)
            dve.memset(ACC, 0.0).then_inc(e_add, 4)
            with dve.Fori(0, waves) as w:
                for t in range(2):
                    dve.tensor_scalar(SEL[:, t, :], CM[:, IOTA, :], WR[:, t, bass.ds(w, 1)], None, ALU.is_equal)
                    last = dve.tensor_scalar(SEL[:, 2 + t, :], CM[:, IOTA, :], WR[:, t, bass.ds(w, 1)],
                                             WG[:, t, bass.ds(w, 1)], ALU.is_equal, ALU.mult)
                last.then_inc(e_sel, 1)
                for half in range(2):
                    dve.wait_ge(e_gmm, 2 * w + half + 1)
                    for k in range(4 * half, 4 * half + 4):
                        last = dve.tensor_scalar(XG[:, k, :], PS[:, 4 + half, (k % 4) * P:(k % 4) * P + P],
                                                 AB[:, 1, 0, 0, k:k + 1], AB[:, 1, 0, 1, k:k + 1], ALU.mult, ALU.add)
                    last.then_inc(e_gev, 1)
                for s in range(NUP):
                    dve.wait_ge(e_silu, NUP * w + s + 1)
                    if s >= 2:
                        dve.wait_ge(e_htr, NUP * w + s - 1)
                    dve.tensor_tensor(HE[:, s % 2, :], SE[:, s % 2, :], PS[:, 2 * (s % 2) + 1, :],
                                      ALU.mult).then_inc(e_h, 1)
                for i in range(4):
                    dve.wait_ge(e_sc, 4 * w + i + 1)
                    v = ACC[:, i // 2, 512 * (i % 2):512 * (i % 2) + 512]
                    dve.tensor_tensor(v, v, PS[:, i, :], ALU.add).then_inc(e_add, 1)
            dve.wait_ge(e_add, 4 * waves + 4)
            for t in range(2):
                seq(dve.tensor_tensor(ACC[:, t, :], ACC[:, t, :], GE, ALU.mult))
                seq(dve.tensor_tensor(X[:, t, :], X[:, t, :], ACC[:, t, :], ALU.add))
                dve.nop().then_inc(fin_x, 1)

            dve.wait_ge(fin_sd, 1)
            seq(dve.reciprocal(SS[:, 16:18], SS[:, 8:10]))
            dve.wait_ge(s_fg, 16)
            for t in range(2):
                dve.scalar_tensor_tensor(X[:, t, :], X[:, t, :], SS[:, 16 + t:17 + t], FG, ALU.mult,
                                         ALU.mult).then_inc(fin_ok, 1)

        @block.tensor
        def _(pe):
            mm = pe.matmul

            def end():
                pe.nop().then_inc(done["pe"], 1)

            def ident(n=P):
                return CM[0:n, IDENT, 0:n]

            pe.wait_ge(s_rows, 96)
            pe.wait_ge(s_const, 16)
            pe.transpose(PS[:, 7, 0:P], ROWSB[:, :], ident()).then_inc(sm_tr, 1)
            pe.wait_ge(sm_tr, 1)
            end()

            def ada(l):
                begin(pe, "pe", f"ada{l}")
                for g in range(3):
                    for q in range(4):
                        w = wait_chunk(pe, first[f"ada{l}"] + 4 * g + q)
                        for k in range(2):
                            for c in range(4):
                                last = mm(PS[32 * c:32 * c + 32, g, :], ST[:, 2 * q + k, :],
                                          w[:, k, 512 * c:512 * c + 512], start=(q + k == 0), stop=(q == 3 and k == 1),
                                          tile_position=(0, 32 * c))
                        last.then_inc(ada_mm, 1)
                for g in range(3):
                    pe.wait_ge(mod_rows, 3 * l + g + 1)
                    for j in range(4):
                        last = pe.transpose(PS[:, 3 + g, j * P:j * P + P], MOD[:, g, j * P:j * P + P], ident())
                    last.then_inc(ada_tr, 1)
                pe.wait_ge(ada_tr, 3 * l + 3)
                end()

            evbase = [0]

            def norm(stage, n, nt0, xn):
                begin(pe, "pe", stage)
                for i in range(n):
                    pe.wait_ge(xn_ready, nt0 + i + 1)
                    if i >= 2:
                        pe.wait_ge(norm_ev, evbase[0] + i - 1)
                    for k in range(KB):
                        last = pe.transpose(PS[:, 2 * (i % 2) + k // 4, (k % 4) * P:(k % 4) * P + P],
                                            xn(i)[:, k * P:k * P + P], ident())
                    last.then_inc(norm_tr, 1)
                evbase[0] += n - 1
                pe.wait_ge(norm_tr, nt0 + n)
                end()

            ada(0)
            norm("norm0", NT, 0, lambda i: XN[:, i % 2, :])

            begin(pe, "pe", "win")
            for b in range(12):
                w = wait_chunk(pe, first["win"] + b // 4)
                if b >= 4:
                    pe.wait_ge(cin_ready, b - 3)
                for k in range(KB):
                    last = mm(PS[:, b % 4, :], w[:, k, (b % 4) * P:(b % 4) * P + P], hT[:, k, :],
                              start=(k == 0), stop=(k == KB - 1))
                last.then_inc(win_mm, 1)
            pe.wait_ge(win_mm, 12)
            end()

            begin(pe, "pe", "tok")
            for j in range(3 * NT):
                c, t = j // NT, j % NT
                n = TOKC[c][1]
                w = wait_chunk(pe, first["tok"] + c)
                if 4 <= j < 8:
                    pe.wait_ge(tok_z, j - 3)
                elif j >= 8:
                    pe.wait_ge(tok_ev, j - 7)
                for k in range(KB):
                    last = mm(PS[:, j % 4, 0:n], hT[:, k, t * P:t * P + P], w[:, k, :],
                              start=(k == 0), stop=(k == KB - 1))
                last.then_inc(tok_mm, 1)
            pe.wait_ge(tok_mm, 3 * NT)
            end()

            begin(pe, "pe", "mproj")
            pe.wait_ge(m_nrm, 1)
            for k in range(6):
                c0 = (CQ0 + P * k) if k < 3 else (CKV0 + P * (k - 3)) if k < 5 else KR0 - NOPE
                n = P if k < 5 else QD
                for t in range(NT):
                    last = pe.transpose(PS[0:n, k, t * P:t * P + P], P2[:, t, c0:c0 + n], ident())
                last.then_inc(m_tr, 1)
            pe.wait_ge(m_trev, 6)
            for j in range(2 * H_B + NT):
                if j >= 4:
                    pe.wait_ge(mproj_ev, j - 3)
                if j < H_B:
                    w = wait_chunk(pe, first["mproj"])
                    for k in range(3):
                        last = mm(PS[0:QD, j % 4, :], w[:, k, j * QD:j * QD + QD], CQT[:, k, :],
                                  start=(k == 0), stop=(k == 2))
                elif j < 2 * H_B:
                    w = wait_chunk(pe, first["mproj"] + 1)
                    h = j - H_B
                    for k in range(2):
                        last = mm(PS[0:NOPE, j % 4, :], w[:, k, h * P:h * P + NOPE], CKVT[:, k, :],
                                  start=(k == 0), stop=(k == 1))
                else:
                    t = j - 2 * H_B
                    for k in range(2):
                        wv = w[:, k, :].rearrange("p (h n) -> p h n", h=H_B)[:, :, NOPE:NOPE + DV]
                        last = mm(PS[:, j % 4, :], CKVT[:, k, t * P:t * P + P], wv, start=(k == 0), stop=(k == 1))
                last.then_inc(mproj_mm, 1)
            pe.wait_ge(mproj_ev, H_B + 1)
            for j in range(H_B + 1):
                if j >= 2:
                    pe.wait_ge(rot_ev, j - 1)
                of = QT[0:QD, j, 0:L] if j < H_B else KT[0:QD, 0, 0:L]
                mm(PS[0:QD, 4 + j % 2, 0:L], CM[0:QD, ROT, 0:QD], of, start=True, stop=True).then_inc(rot_mm, 1)
            pe.wait_ge(rot_mm, H_B + 1)
            end()

            def attention(items, base, pm, pt, scores, pv):
                def score(j):
                    if j >= 2:
                        pe.wait_ge(att_p, base + j - 1)
                    scores(j).then_inc(att_s, 1)

                score(0)
                for j in range(len(items)):
                    if j + 1 < len(items):
                        score(j + 1)
                    h, t, n = items[j]
                    pe.wait_ge(att_pn, base + j + 1)
                    if j >= 2:
                        pe.wait_ge(att_pt, base + j - 1)
                    for i in range(n):
                        last = pe.transpose(PS[:, 2 + j % 2, i * P:i * P + P], pm[:, j % 2, i * P:i * P + P], ident())
                    last.then_inc(att_tr, 1)
                    pe.wait_ge(att_pt, base + j + 1)
                    if j >= 2:
                        pe.wait_ge(att_oe, base + j - 1)
                    r0 = 64 * (h % 2)
                    for i in range(n):
                        last = mm(PS[r0:r0 + 64, 4 + j % 2, 0:P], pv(h, i, n), pt[:, j % 2, i, :], start=(i == 0),
                                  stop=(i == n - 1))
                    last.then_inc(att_o, 1)
                pe.wait_ge(att_o, base + len(items))
                end()

            begin(pe, "pe", "matt")

            def scores(j):
                h, t, n = M_ITEMS[j]
                return mm(PS[:, j % 2, 0:n * P], QT[0:QD, h, t * P:t * P + P], KT[0:QD, h, T - n * P:T],
                          start=True, stop=True)

            attention(M_ITEMS, 0, PM, PT, scores, lambda h, i, n: VB[:, NT - n + i, h * DV:h * DV + DV])

            begin(pe, "pe", "l2")
            for b in range(8):
                pe.wait_ge(l2_sq, b + 1)
                for t in range(NT):
                    last = mm(PS[:, 0, 4 * b + t:4 * b + t + 1], SQ[:, b % 2, t * P:t * P + P], ONE[:, 0:1],
                              start=True, stop=True)
                last.then_inc(l2_ss, 1)
            pe.wait_ge(l2_r, 1)
            for b in range(8):
                if b >= 4:
                    pe.wait_ge(l2_ok, b - 3)
                for t in range(NT):
                    last = mm(PS[:, 2 + b % 4, t * P:t * P + P],
                              SS[:, 32 + 4 * b + t:33 + 4 * b + t].to_broadcast([P, P]), ident(), start=True, stop=True)
                last.then_inc(l2_bc, 1)
            pe.wait_ge(l2_ok, 8)
            for i in range(8):
                if i >= 2:
                    pe.wait_ge(l2_ev, i - 1)
                for h in range(4):
                    last = pe.transpose(PS[:, 6 + i % 2, h * P:h * P + P],
                                        qkvT[:, 4 + 4 * (i % 2) + h, (i // 2) * P:(i // 2) * P + P], ident())
                last.then_inc(l2_tr, 1)
            pe.wait_ge(l2_tr, 8)
            end()

            begin(pe, "pe", "gdn")
            hh = range(4)
            for s in range(NT):
                for d in dirs:
                    b, B, t = DIR[d], 4 * d, TILE_OF[d][s]
                    tc = slice(t * P, t * P + P)
                    upto, after = CM[:, UP if d == 0 else LO, :], CM[:, SLO if d == 0 else SUP, :]
                    pe.wait_ge(g_gU, both(d, s + 1))
                    if s:
                        pe.wait_ge(g_S, both(d, s))
                    mm(PS[:, B, :], after, b["gU"].rearrange("p h n -> p (h n)"), start=True, stop=True)
                    for h in hh:
                        last = mm(PS[:, B + 1, h * P:h * P + P], b["gU"][:, h, :], after, start=True, stop=True)
                    last.then_inc(g_seg, 1)
                    g = GB8[:, t, 0, 4 * d:4 * d + 4]
                    mm(PS[:, B + 2, 0:4], upto, g, start=True, stop=True)
                    mm(PS[:, B + 2, 4:8], after, g, start=True, stop=True)
                    mm(PS[:, B + 2, 8:12], ONE[:, :], g, start=True, stop=True).then_inc(g_sm, 1)
                    for h in hh:
                        mm(PS[:, B + 3, h * P:h * P + P], qkvT[:, 4 + h, tc], qkvT[:, 4 + h, tc], start=True, stop=True)
                for d in dirs:
                    B, t = 4 * d, TILE_OF[d][s]
                    tc = slice(t * P, t * P + P)
                    pe.wait_ge(g_exp, both(d, s + 1))
                    for h in hh:
                        last = mm(PS[:, B, h * P:h * P + P], qkvT[:, 4 + h, tc], qkvT[:, h, tc], start=True, stop=True)
                    last.then_inc(g_kk, 1)
                for d in dirs:
                    b, B = DIR[d], 4 * d
                    pe.wait_ge(g_A, both(d, s + 1))
                    for h in hh:
                        last = pe.transpose(PS[:, B, h * P:h * P + P], b["A"][:, h, :], ident())
                    last.then_inc(g_At, 1)
                for n in range(1, LEVELS):
                    at = (LEVELS - 1) * s + n
                    for d in dirs:
                        b, B = DIR[d], 4 * d
                        pe.wait_ge(g_LT, both(d, at))
                        if n == 1:
                            pe.wait_ge(g_D1, both(d, s + 1))
                            pe.wait_ge(g_eg, both(d, s + 1))
                        else:
                            pe.wait_ge(g_DE, both(d, at - 1))
                        for h in hh:
                            last = mm(PS[:, B + 1, h * P:h * P + P], b["gU"][:, h, :], b["Dm"][:, h, :],
                                      start=True, stop=True)
                        last.then_inc(g_M1, 1)
                    for d in dirs:
                        b, B = DIR[d], 4 * d
                        pe.wait_ge(g_M1e, both(d, at))
                        for h in hh:
                            if n < LEVELS - 1:
                                mm(PS[:, B + 2, h * P:h * P + P], b["Em"][:, h, :], b["dec"][:, h, :],
                                   start=True, stop=True)
                            last = mm(PS[:, B + 3, h * P:h * P + P], b["dec"][:, h, :], b["Em"][:, h, :],
                                      start=True, stop=True)
                        last.then_inc(g_PQ, 1)
                for d in dirs:
                    b, B = DIR[d], 4 * d
                    pe.wait_ge(g_DE, both(d, (LEVELS - 1) * (s + 1)))
                    pe.wait_ge(g_vec, both(d, s + 1))
                    for h in hh:
                        last = mm(PS[:, B + 1, h * P:h * P + P], b["kbe"][:, h, :], b["Em"][:, h, :],
                                  start=True, stop=True)
                    last.then_inc(g_wT, 1)
                for d in dirs:
                    b, B, t = DIR[d], 4 * d, TILE_OF[d][s]
                    pe.wait_ge(g_wTe, both(d, s + 1))
                    for h in hh:
                        mm(PS[:, B, h * P:h * P + P], b["Em"][:, h, :], b["vb"][:, h, :], start=True, stop=False)
                        last = mm(PS[:, B, h * P:h * P + P], b["Dm"][:, h, :], b["S"][:, h, :], start=False, stop=True)
                    last.then_inc(g_vn, 1)
                    for h in hh:
                        mm(PS[:, B + 2, h * P:h * P + P], qkvT[:, h, t * P:t * P + P], b["S"][:, h, :],
                           start=True, stop=True)
                for d in dirs:
                    b, B = DIR[d], 4 * d
                    pe.wait_ge(g_vne, both(d, s + 1))
                    for h in hh:
                        mm(PS[:, B + 3, h * P:h * P + P], b["decT"][:, h, :], b["A"][:, h, :], start=True, stop=True)
                    for h in hh:
                        last = mm(PS[:, B + 1, h * P:h * P + P], b["kg"][:, h, :], b["A"][:, h, :],
                                  start=True, stop=True)
                    last.then_inc(g_o, 1)
            for d in dirs:
                pe.wait_ge(g_o, both(d, NT))
            end()

            begin(pe, "pe", "gout")
            for t in range(NT):
                pe.wait_ge(go_n, t + 1)
                for h in range(4):
                    last = pe.transpose(PS[:, t, h * P:h * P + P], OD[:, 0, t, h * P:h * P + P], ident())
                last.then_inc(go_tr, 1)
            pe.wait_ge(go_tr, NT)
            end()

            def gate_rows(g, c0, n):
                for r in range(n):
                    for c in range(2):
                        q = 32 * (c0 + c) + r
                        last = mm(PS[:, 4 + 2 * r + c, :], ident()[:, q:q + 1].to_broadcast([P, P]), MOD[:, g, :],
                                  start=True, stop=True)
                last.then_inc(gb_mm, 1)

            def project(stage, base, nt, lhs):
                begin(pe, "pe", stage)
                gate_rows(1, 0, nt // 2)
                for i in range(2 * nt):
                    n, t = i // nt, i % nt
                    w = wait_chunk(pe, first[stage] + n)
                    if i >= 4:
                        pe.wait_ge(out_ev, base + i - 3)
                    for k in range(KB):
                        last = mm(PS[:, i % 4, :], lhs(k, t), w[:, k, :], start=(k == 0), stop=(k == KB - 1))
                    last.then_inc(out_mm, 1)
                pe.wait_ge(out_mm, base + 2 * nt)
                end()

            project("out0", 0, NT, lambda k, t: (mixT[:, k, t * P:t * P + P] if k < 4 else YB[:, k - 4, t * P:t * P + P]))
            norm("norm1", NT, 4, lambda i: XN[:, i % 2, :])

            begin(pe, "pe", "up")
            for f in range(FF // P):
                w = wait_chunk(pe, first["up"] + f // 2)
                if f >= 2:
                    pe.wait_ge(up_ev, f - 1)
                for u in range(2):
                    for k in range(KB):
                        c0 = 256 * u + P * (f % 2)
                        last = mm(PS[:, 2 * (f % 2) + u, :], w[:, k, c0:c0 + P], hT[:, k, :],
                                  start=(k == 0), stop=(k == KB - 1))
                last.then_inc(up_mm, 1)
            pe.wait_ge(up_mm, FF // P)
            end()

            begin(pe, "pe", "down")
            gate_rows(2, 2, 2)
            for n in range(2):
                for c, (k0, nk) in enumerate(DOWNC):
                    w = wait_chunk(pe, first["down"] + 3 * n + c)
                    if n == 1 and c == 0:
                        pe.wait_ge(done["act"], sum(s in WORKS["act"] for s in STAGES[:STAGES.index("down") + 1]))
                    for k in range(nk):
                        for t in range(NT):
                            last = mm(PS[:, 4 * n + t, :], H2T[:, k0 + k, t * P:t * P + P], w[:, k, :],
                                      start=(k0 + k == 0), stop=(k0 + k == FF // P - 1))
                    last.then_inc(down_mm, 1)
            pe.wait_ge(down_mm, 6)
            end()

            ada(1)
            norm("norm2", NT, 8, lambda i: XN[:, i % 2, :])

            begin(pe, "pe", "qkv")
            for i in range(24):
                w = wait_chunk(pe, first["qkv"] + i // 4)
                if i >= 4:
                    pe.wait_ge(qkv_ev[i % 2], (i - 4) // 2 + 1)
                for k in range(KB):
                    blk = slice((i % 4) * P, (i % 4) * P + P)
                    if i < 8:
                        last = mm(PS[:, i % 4, 0:L], w[:, k, blk], hT[:, k, 0:L], start=(k == 0), stop=(k == KB - 1))
                    elif i < 16:
                        last = mm(PS[:, i % 4, :], w[:, k, blk], hT[:, k, :], start=(k == 0), stop=(k == KB - 1))
                    else:
                        last = mm(PS[:, i % 4, :], hT[:, k, blk], w[:, k, :], start=(k == 0), stop=(k == KB - 1))
                last.then_inc(qkv_mm, 1)
            pe.wait_ge(qkv_mm, 24)
            end()

            begin(pe, "pe", "natt")

            def scores(j):
                h, t, n = N_ITEMS[j]
                rs = slice(64 * (h % 2), 64 * (h % 2) + 64)
                mm(PS[:, j % 2, :], QC[rs, h // 2, t * P:t * P + P], KC[rs, h // 2, :], start=True, stop=False)
                pe.wait_ge(bias_ok, j + 1)
                return mm(PS[:, j % 2, 0:L], CM[:, FLIP, :], BM[:, j % 4, :], start=False, stop=True)

            attention(N_ITEMS, len(M_ITEMS), PC, PCT, scores, lambda h, i, n: VC[:, i, h * DH:h * DH + DH])

            project("out1", 2 * NT, 2, lambda k, t: OC[:, k, t * P:t * P + P])
            norm("norm3", 2, 12, lambda i: X[:, 2 + i, :])

            begin(pe, "pe", "route")
            for t in range(2):
                for k in range(KB):
                    last = mm(PS[:, 0, 8 * t:8 * t + 8], fT[:, k, t * P:t * P + P], RW[:, k, :], start=(k == 0),
                              stop=(k == KB - 1))
            last.then_inc(rt_mm, 1)
            gate_rows(2, 2, 1)
            pe.wait_ge(rt_ev, 1)
            mm(PS[:, 1, 0:8], CM[:, SUP, :], SELM[:, 0, :], start=True, stop=True)
            mm(PS[:, 1, 8:16], CM[:, SUP, :], SELM[:, 1, :], start=True, stop=False)
            mm(PS[:, 1, 8:16], ONE[:, :], SELM[:, 0, :], start=False, stop=True)
            mm(PS[:, 1, 16:24], ONE[:, :], SELM[:, 0, :], start=True, stop=False)
            mm(PS[:, 1, 16:24], ONE[:, :], SELM[:, 1, :], start=False, stop=True).then_inc(rk_mm, 1)
            pe.wait_ge(rk_mm, 1)
            end()

            begin(pe, "pe", "moe")
            waves = pe.value_load(RI[0:1, 0:1], min_val=E, max_val=WAVES)

            def arrive(w, i):
                pe.wait_ge(arrived_e[i % RING_E], (16 * (NEC // RING_E)) * w + 16 * (i // RING_E + 1))
                return BIG[:, (i % RING_E) * SLOT:(i % RING_E) * SLOT + SLOT]

            with pe.Fori(0, waves) as w:
                pe.wait_ge(e_sel, w + 1)
                for k in range(KB):
                    for t in range(2):
                        last = mm(PS[:, 4 + k // 4, (k % 4) * P:(k % 4) * P + P], X[:, 2 + t, k * P:k * P + P],
                                  SEL[:, t, :], start=(t == 0), stop=(t == 1))
                    if k % 4 == 3:
                        last.then_inc(e_gmm, 1)
                for t in range(2):
                    last = pe.transpose(PS[:, 6, t * P:t * P + P], SEL[:, 2 + t, :], ident())
                last.then_inc(e_tr, 1)

                def columns(s):
                    pe.wait_ge(e_h, NUP * w + s + 1)
                    if s >= 2:
                        pe.wait_ge(e_htev, NUP * w + s - 1)
                    for j in range(4):
                        last = pe.transpose(PS[:, 4 + s % 2, j * P:j * P + P], HE[:, s % 2, j * P:j * P + P], ident())
                    last.then_inc(e_htr, 1)

                pe.wait_ge(e_gev, 2 * w + 2)
                pe.wait_ge(e_add, 4 * w + 4)
                for s in range(NUP):
                    for u in range(2):
                        slot_e = arrive(w, 2 * s + u).rearrange("p (k n) -> p k n", k=KB)
                        if s >= 2 and u == 0:
                            pe.wait_ge(e_h, NUP * w + s - 1)
                        for k in range(KB):
                            last = mm(PS[:, 2 * (s % 2) + u, :], XG[:, k, :], slot_e[:, k, :], start=(k == 0),
                                      stop=(k == KB - 1))
                    last.then_inc(gu_mm, 1)
                    if s:
                        columns(s - 1)
                columns(NUP - 1)
                pe.wait_ge(e_trev, w + 1)
                for i in range(NDN):
                    slot_e = arrive(w, 2 * NUP + i).rearrange("p (k n) -> p k n", k=4)
                    pe.wait_ge(e_htev, NUP * w + i + 1)
                    for k in range(4):
                        for n in range(2):
                            last = mm(PS[:, 6 + n, :], HET[:, 4 * i + k, :], slot_e[:, k, 512 * n:512 * n + 512],
                                      start=(i + k == 0), stop=(i == NDN - 1 and k == 3))
                    last.then_inc(dn_mm, 1)
                pe.wait_ge(e_y, w + 1)
                for t in range(2):
                    for n in range(2):
                        mm(PS[:, 2 * t + n, :], SELT[:, t, :], YE[:, 0, 512 * n:512 * n + 512], start=True,
                           stop=True).then_inc(e_sc, 1)



_CONSTS = ("masks", "rope", "window")
_INS = ("x", "c", "ctx", "c_ctx", "ada_w", "ada_b", "norm_g", "ev_w_in", "ev_conv_w", "ev_a_log", "ev_dt_bias",
        "ev_gdn_norm_g", "ev_q_norm_g", "ev_w_uq", "ev_kv_norm_g", "ev_w_ukv", "ev_w_out", "ev_ffn_wg", "ev_ffn_wu",
        "ev_ffn_wd", "od_w_qkv", "od_rpb", "od_w_out", "od_router", "od_exp_wg", "od_exp_wu", "od_exp_wd",
        "final_norm_g")


def kernel(**inputs):
    import concourse.bacc as bacc
    from concourse.bass_utils import run_bass_kernel_spmd

    nc = bacc.Bacc("TRN2", target_bir_lowering=False, num_devices=1)
    arrays, A = {}, {}
    for name, a in list(zip(_CONSTS, constants())) + [(n, inputs[n]) for n in _INS]:
        a = np.ascontiguousarray(a)
        arrays[f"in_{name}"] = a
        A[name] = nc.dram_tensor(f"in_{name}", a.shape, mybir.dt.from_np(a.dtype), kind="ExternalInput").ap()
    out = nc.dram_tensor("out", (1, L, D), mybir.dt.float32, kind="ExternalOutput").ap()
    build(nc, A, out)
    r = run_bass_kernel_spmd(nc, [arrays], core_ids=[0])
    return r.results[0]["out"]
```

```python
import math
from contextlib import ExitStack

import concourse.bass as bass
import numpy as np
from concourse import mybir

P = 128
D = 1024
KB = D // P
L = 256
NT = 2 * L // P
T = 2 * L
EPS = 1e-6
H_A, DK = 4, 128
TAPS = 5
H_B, NOPE, ROPE, DV = 8, 64, 32, 64
QR, KVR = 384, 256
QD = NOPE + ROPE
H_C, DH = 16, 64
GRID_W, WIN_C, WIN_R = 64, 16, 8
RPB_R, RPB_C = 2 * WIN_R - 1, 2 * WIN_C - 1
ROWS = L // GRID_W
FF = 2816
E, FFE = 8, 3584
QKV_A = 3 * H_A * DK
Z0 = QKV_A
AB0 = Z0 + H_A * DK
IN_DIM = AB0 + 16 + QR + KVR + ROPE
REST = IN_DIM - AB0
CQ0, CKV0, KR0 = 16, 16 + QR, 16 + QR + KVR
SLOT = 4096
RING, RING_E = 3, 7
LEVELS = 7
IDENT, UP, LO, SLO, SUP, LEV, ROT, IOTA, FLIP = 0, 1, 2, 3, 4, 5, 5 + LEVELS, 6 + LEVELS, 7 + LEVELS
N_CONST = 8 + LEVELS
R_C, R_NG, R_CONV, R_QG, R_KVG = 0, 16, 48, 108, 111
WAVES = E + 3

STAGES = ["prep", "ada0", "norm0", "win", "tok", "mproj", "matt", "l2", "gdn", "gout", "out0", "norm1", "up",
          "down", "norm2", "qkv", "natt", "out1", "norm3", "route", "moe", "final"]
WORKS = {
    "pe": set(STAGES) - {"moe", "final"},
    "act": set(STAGES) - {"final"},
    "dve": set(STAGES) - {"moe", "final"},
    "pool": {"prep", "gdn", "natt"},
}


def constants():
    i = np.arange(P)
    m = np.zeros((P, N_CONST, P), np.float32)
    r, c = i[:, None], i[None, :]
    m[:, IDENT] = r == c
    m[:, UP] = r <= c
    m[:, LO] = r >= c
    m[:, SLO] = r > c
    m[:, SUP] = r < c
    for n in range(LEVELS):
        m[:, LEV + n] = (r >> (n + 1) == c >> (n + 1)) & (r >> n != c >> n)
    q = ROPE // 4
    for a in range(q):
        for half in (0, 2 * q):
            m[NOPE + half + q + a, ROT, NOPE + half + a] = -1.0
            m[NOPE + half + a, ROT, NOPE + half + q + a] = 1.0
    m[:, IOTA] = c
    m[:, FLIP] = ((r // GRID_W == c // GRID_W) & (r % GRID_W == GRID_W - 1 - c % GRID_W)) * float(DH) ** 0.5
    t = np.arange(L)
    inv = np.float32(10000.0) ** (-np.arange(0, ROPE // 2, 2, dtype=np.float32) / np.float32(ROPE // 2))
    ar = (t // GRID_W).astype(np.float32)[:, None] * inv[None]
    ac = (t % GRID_W).astype(np.float32)[:, None] * inv[None]
    ang = np.concatenate([ar, ar, ac, ac], axis=-1)
    rope = np.stack([np.cos(ang).T, np.sin(ang).T], axis=1).astype(np.float32)
    col = GRID_W - 1 - i % GRID_W
    first = np.clip(col - WIN_C // 2, 0, GRID_W - WIN_C)[:, None]
    key = np.arange(GRID_W)[None]
    window = np.where((key >= first) & (key < first + WIN_C), 0.0, -1e30).astype(np.float32)
    return m.reshape(P, -1), rope, window


def build(nc, A, out):
    f32, i32 = mybir.dt.float32, mybir.dt.int32
    ALU, ACT, AX = mybir.AluOpType, mybir.ActivationFunctionType, mybir.AxisListType

    ctx = ExitStack()
    with ctx:
        def sb(name, shape, dt=f32):
            return ctx.enter_context(nc.sbuf_tensor(name, shape, dt))

        def sem(name):
            return ctx.enter_context(nc.semaphore(name))

        BIG = sb("BIG", [P, RING_E * SLOT])
        HB = sb("HB", [P, KB * T])
        QB = sb("QB", [P, 12 * T])
        X = sb("X", [P, NT, D])
        ZS = sb("ZS", [P, NT, 512])
        YB = sb("YB", [P, 4, T])
        CM = sb("CM", [P, N_CONST, P])
        CS = sb("CS", [P, 2, L])
        WM = sb("WM", [P, GRID_W])
        MOD = sb("MOD", [P, 3, 512])
        MT = sb("MT", [P, 3, 4, 4, 2])
        AB = sb("AB", [P, 2, 2, 2, KB])
        ROWSB = sb("ROWSB", [P, P])
        SM = sb("SM", [P, P])
        ST = sb("ST", [P, KB, 32])
        DTB = sb("DTB", [P, 2, 8])
        GG = sb("GG", [P, P])
        ONE = sb("ONE", [P, P])
        SS = sb("SS", [P, 64])
        RT = sb("RT", [P, 64])
        GB8 = sb("GB8", [P, NT, 3, 8])
        EG = sb("EG", [P, 2, 12])
        RW = sb("RW", [P, KB, E])
        EPSC = sb("EPSC", [P, 2])
        EA = sb("EA", [P, 1, 8])
        SELM = sb("SELM", [P, 2, E])
        WR = sb("WR", [P, 2, WAVES])
        WG = sb("WG", [P, 2, WAVES])
        RF = sb("RF", [P, 4])
        RI = sb("RI", [P, 4], i32)
        RFB = sb("RFB", [P, WAVES])
        RIB = sb("RIB", [P, WAVES], i32)

        hT = HB[:, :].rearrange("p (k t) -> p k t", t=T)
        qkvT = QB[:, :].rearrange("p (b t) -> p b t", t=T)
        mixT = QB[:, 0:KB * T].rearrange("p (b t) -> p b t", t=T)
        XN = QB[:, 0:2 * D].rearrange("p (a n) -> p a n", a=2)
        GB = QB[:, KB * T:KB * T + 2 * D].rearrange("p (r n) -> p r n", r=2)
        AR = BIG[:, RING * SLOT:]

        class Cut:
            def __init__(self, region, at=0):
                self.region, self.at = region, at

            def __call__(self, *shape):
                n = int(np.prod(shape))
                v = self.region[:, self.at:self.at + n]
                self.at += n
                if len(shape) == 2:
                    v = v.rearrange("p (a b) -> p a b", a=shape[0])
                if len(shape) == 3:
                    v = v.rearrange("p (a b c) -> p a b c", a=shape[0], b=shape[1])
                return v

        cut = Cut(AR, (RING_E - RING) * SLOT - 3 * 512)
        BADD = cut(3, 512)
        cut = Cut(AR)
        CIN = cut(2, 2, L + TAPS - 1)
        CACC = cut(2, T)
        cut = Cut(AR)
        P2 = cut(NT, REST)
        CQT = cut(3, T)
        CKVT = cut(2, T)
        QT = cut(H_B, T)
        KT = cut(H_B, T)
        VB = cut(NT, H_B * DV)
        cut = Cut(HB)
        PM = cut(3, T)
        PT = cut(2, 4, P)
        RTMP = cut(2, L)
        cut = Cut(AR)
        KTOK = cut(NT, 4 * DK)
        VTOK = cut(NT, 4 * DK)
        DIR = [{n: cut(4, P) for n in ("gU", "dec", "decT", "A", "AT", "Dm", "Em", "kbe", "kg", "vb", "S", "LT")}
               for _ in range(2)]
        OD = HB[:, :].rearrange("p (d t n) -> p d t n", d=2, t=NT)
        SQ = HB[:, 0:2 * T].rearrange("p (a t) -> p a t", a=2)
        cut = Cut(AR)
        H2T = cut(FF // P, T)
        SG = cut(2, T)
        cut = Cut(AR)
        QC = cut(KB, L)
        KC = cut(KB, T)
        VC = cut(NT, D)
        PC = cut(3, T)
        PCT = cut(2, 4, P)
        BM = cut(4, L)
        OC = HB[:, 0:KB * L].rearrange("p (k t) -> p k t", t=L)
        cut = Cut(QB)
        XG = cut(KB, P)
        HE = cut(2, 512)
        HET = cut(FFE // P, P)
        SEB = [QB[:, cut.at:cut.at + 512], ZS[:, 3, :]]
        cut = Cut(HB, KB * L)
        SE = cut(2, 512)
        YE = cut(1, D)
        fT = HB[:, 0:KB * L].rearrange("p (k t) -> p k t", t=L)
        SEL = ZS[:, 0, :].rearrange("p (a b) -> p a b", a=4)
        SELT = ZS[:, 1, 0:2 * P].rearrange("p (a b) -> p a b", a=2)
        RTB = ZS[:, 2, :]
        FG = YB[:, 0:2, :].rearrange("p a b -> p (a b)")
        GE = YB[:, 2:4, :].rearrange("p a b -> p (a b)")
        ACC = HB[:, 0:2 * D].rearrange("p (t n) -> p t n", t=2)

        TILE_OF = [[2, 3, 0, 1], [3, 2, 1, 0]]
        M_ITEMS = [(h, t, 4 if t < 2 else 2) for h in range(H_B) for t in range(NT)]
        N_ITEMS = [(h, t, 4) for h in range(H_C) for t in range(2)]

        PS = ctx.enter_context(nc.psum_tensor("PS", [P, 8, 512], f32))

        done = {e: sem(f"{e}_stage_done") for e in WORKS}

        def qkv_place(i):
            if i < 8:
                return QC[:, i, :], PS[:, i % 4, 0:L]
            if i < 16:
                return KC[:, i - 8, :], PS[:, i % 4, :]
            return VC[:, i % 4, 512 * (i // 20):512 * (i // 20) + 512], PS[:, i % 4, :]

        def begin(eng, me, stage):
            for e in WORKS:
                n = sum(s in WORKS[e] for s in STAGES[:STAGES.index(stage)])
                if e != me and n:
                    eng.wait_ge(done[e], n)

        arrived = [sem(f"weights_arrived{i}") for i in range(RING)]
        arrived_e = [sem(f"expert_weights_arrived{i}") for i in range(RING_E)]
        ada_mm, win_mm, tok_mm, mproj_mm = sem("ada_mm"), sem("win_mm"), sem("tok_mm"), sem("mproj_mm")
        out_mm, up_mm, down_mm, qkv_mm = sem("out_mm"), sem("up_mm"), sem("down_mm"), sem("qkv_mm")
        stream = []

        def by_rows(w, r0, nb, c0, nc_):
            return w[r0:r0 + nb * P, c0:c0 + nc_].rearrange("(k p) n -> p k n", p=P)

        first = {}

        def chunk(key, shape, source, free):
            first.setdefault(key, len(stream))
            stream.append((shape, source, free))

        def ada_chunk(l, i):
            g, q = i // 4, i % 4
            chunk(f"ada{l}_{i}", (2, 2048), by_rows(A["ada_w"][l], 256 * q, 2, 2048 * g, 2048), (ada_mm, 12 * l + i + 1))

        ADA_IN = {("win", 0): (0, (4, 5)), ("win", 1): (0, (6, 7)), ("win", 2): (0, (8, 9)), ("tok", 0): (0, (10,)),
                  ("tok", 1): (0, (11,))}
        ADA_IN |= {("up", n): (1, (n,) if n < FF // 256 - 1 else (n, n + 1)) for n in range(FF // 256)}

        def ada_between(stage, n):
            l, which = ADA_IN.get((stage, n), (0, ()))
            for i in which:
                ada_chunk(l, i)

        for i in range(4):
            ada_chunk(0, i)
        w_in = A["ev_w_in"][0]
        for c in range(3):
            chunk(f"win{c}", (KB, 512), by_rows(w_in, 0, KB, 512 * c, 512), (win_mm, 4 * c + 4))
            ada_between("win", c)
        TOKC = [(Z0, 512), (AB0, REST // 2), (AB0 + REST // 2, REST // 2)]
        for c, (c0, n) in enumerate(TOKC):
            chunk(f"tok{c}", (KB, n), by_rows(w_in, 0, KB, c0, n), (tok_mm, 4 * c + 4))
            ada_between("tok", c)
        chunk("mproj", (3, H_B * QD), by_rows(A["ev_w_uq"][0], 0, 3, 0, H_B * QD), (mproj_mm, H_B))
        chunk("mproj", (2, H_B * 128), by_rows(A["ev_w_ukv"][0], 0, 2, 0, H_B * 128), (mproj_mm, 2 * H_B + NT))
        for n in range(2):
            chunk("out0", (KB, 512), by_rows(A["ev_w_out"][0], 0, KB, 512 * n, 512), (out_mm, 4 * n + 4))
        for s in range(FF // 256):
            chunk(f"up{s}", None, (by_rows(A["ev_ffn_wg"][0], 0, KB, 256 * s, 256),
                               by_rows(A["ev_ffn_wu"][0], 0, KB, 256 * s, 256)), (up_mm, 2 * s + 2))
            ada_between("up", s)
        DOWNC = [(0, 8), (8, 8), (16, 6)]
        for n in range(2):
            for c, (k0, nk) in enumerate(DOWNC):
                chunk("down", (nk, 512), by_rows(A["ev_ffn_wd"][0], k0 * P, nk, 512 * n, 512), (down_mm, 3 * n + c + 1))
        for c in range(6):
            chunk("qkv", (KB, 512), by_rows(A["od_w_qkv"][0], 0, KB, 512 * c, 512), (qkv_mm, 4 * c + 4))
        for n in range(2):
            chunk("out1", (KB, 512), by_rows(A["od_w_out"][0], 0, KB, 512 * n, 512), (out_mm, 8 + 2 * n + 2))

        def slot(i, shape):
            v = BIG[:, (i % RING) * SLOT:(i % RING) * SLOT + shape[0] * shape[1]]
            return v.rearrange("p (k n) -> p k n", k=shape[0])

        loads_before = [0] * RING
        counts = []
        for i, (shape, source, _) in enumerate(stream):
            loads_before[i % RING] += 1 if shape else 2
            counts.append(16 * loads_before[i % RING])

        def wait_chunk(eng, i):
            eng.wait_ge(arrived[i % RING], counts[i])
            return slot(i, stream[i][0] or (KB, 512))

        NUP, NDN = FFE // 512, FFE // 512
        NEC = 2 * NUP + NDN
        assert NEC % RING_E == 0
        gu_mm, dn_mm = sem("gate_up_mm"), sem("expert_down_mm")

        s_const, s_rows, s_x, s_bias, s_misc = (sem(n) for n in ("const_in", "rows_in", "x_in", "ada_b_in", "misc_in"))
        rows_zero, st_zero = sem("rows_zeroed"), sem("padding_zeroed")
        sm_tr, sm_cols, st_ready = sem("small_transposed"), sem("small_columns"), sem("silu_c_ready")
        mod_rows, ada_tr, mod_cols, gb_mm = sem("mod_rows"), sem("ada_transposed"), sem("mod_columns"), sem("gate_rows_mm")
        norm_sd, norm_rstd, xn_ready, norm_tr, norm_ev = (sem(n) for n in (
            "norm_sd", "norm_rstd", "xn_ready", "norm_transposed", "norm_evacuated"))
        cin_ready, conv_done, win_ev = sem("conv_input"), sem("conv_done"), sem("win_used")
        tok_ev = sem("tok_evacuated")
        dve_seq, act_seq, pool_seq = sem("dve_seq"), sem("act_seq"), sem("pool_seq")
        m_sd, m_rstd, m_nrm, m_tr, m_trev = (sem(n) for n in ("mla_sd", "mla_rstd", "mla_normed", "mla_transposed",
                                                              "mla_latents"))
        mproj_ev, rot_mm, rot_ev = sem("mproj_evacuated"), sem("rot_mm"), sem("rope_done")
        att_s, att_max, att_p, att_pn, att_tr, att_pt, att_o, att_oe = (sem(n) for n in (
            "scores_mm", "scores_max", "probs_ready", "probs_normed", "probs_transposed", "probs_t_ready", "pv_mm",
            "pv_evacuated"))
        bias_in, bias_ok = [sem(f"rpb_in{i}") for i in range(4)], sem("bias_masked")
        l2_sq, l2_ss, l2_sd, l2_r, l2_bc, l2_ok, l2_tr, l2_ev = (sem(n) for n in (
            "l2_squares", "l2_sums", "l2_sd", "l2_rstd", "l2_broadcast", "l2_scaled", "kv_transposed", "kv_tokens"))
        dirs = range(2)

        def both(d, n):
            return 2 * (n - 1) + d + 1

        g_gU, g_seg, g_exp, g_msk, g_kk, g_A, g_At, g_AT, g_D1, g_E1 = (sem(n) for n in (
            "gU", "seg_mm", "decay", "decay_masked", "kk_mm", "A_ready", "A_transposed", "AT_ready", "inverse1", "inverse1_t"))
        g_LT, g_M1, g_M1e, g_PQ, g_DE, g_eg, g_sm, g_vec, g_wT, g_wTe, g_vn, g_vne, g_o, g_oe, g_S = (sem(n) for n in (
            "level_masked", "M1_mm", "M1_ready", "update_mm", "inverse", "sums_exp", "sums_mm", "kbe_kg_vb", "wT_mm",
            "wT_ready", "vnew_mm", "vnew_ready", "o_mm", "o_ready", "S_ready"))
        gb_ready, go_tr, go_ev, go_sd, go_r, go_n = (sem(n) for n in ("g_beta", "o_transposed", "o_columns", "o_sd",
                                                                "o_rstd", "o_gated"))
        out_ev = sem("out_added")
        up_silu, up_ev = sem("up_silu"), sem("up_ready")
        down_ev = sem("down_added")
        qkv_ev = [sem(f"qkv_evacuated{i}") for i in range(2)]
        rt_mm, rt_ev, rk_mm, rt_ok, rt_tab = (sem(n) for n in ("router_mm", "router_read", "rank_mm", "chosen",
                                                              "wave_tables"))
        e_sel, e_gmm, e_gev, e_tr, e_trev = (sem(n) for n in ("sel_ready", "gather_mm", "gathered", "sel_transposed",
                                                             "sel_t_ready"))
        e_silu, e_h, e_htr, e_htev, e_y, e_sc, e_add, e_zero = (sem(n) for n in (
            "expert_silu", "expert_h", "h_transposed", "h_columns", "y_ready", "scatter_mm", "scatter_added", "hidden_cleared"))
        s_out = sem("out_stored")
        go_sum, gz_ready = sem("o_sum"), sem("z_by_gain")
        bias_zero, cin_zero, conv_ev, tok_z = sem("ada_b_zeroed"), sem("conv_padding_zeroed"), sem("conv_evacuated"), sem("z_ready")
        sp_in, sp_ln, go_ss, s_fg = sem("softplus_in"), sem("softplus_ln"), sem("o_sums"), sem("final_gain_in")
        ge_ready, rt_d, rt_e, fin_x = sem("expert_gate_rows"), sem("logit_difference"), sem("logit_exp"), sem("final_x")
        fin_sd, fin_r, fin_n, fin_ok = sem("final_sd"), sem("final_rstd"), sem("final_normed"), sem("final_ready")

        block = ctx.enter_context(nc.Block())

        @block.sync
        def _(sp):
            for i, (shape, source, _) in enumerate(stream):
                if i >= RING:
                    sp.wait_ge(*stream[i - RING][2])
                if shape:
                    sp.dma_start(slot(i, shape), source).then_inc(arrived[i % RING], 16)
                else:
                    for half in range(2):
                        sp.dma_start(slot(i, (KB, 512))[:, :, 256 * half:256 * half + 256],
                                     source[half]).then_inc(arrived[i % RING], 16)

            begin(sp, None, "natt")
            rpb = A["od_rpb"]
            for j in range(2 * H_C):
                h, qt = j // 2, j % 2
                if j >= 4:
                    sp.wait_ge(att_s, len(M_ITEMS) + j - 3)
                for r in range(2):
                    at = h * RPB_R * RPB_C + (WIN_R - 1 - (2 * qt + r)) * RPB_C + WIN_C - GRID_W
                    src = bass.AP(tensor=rpb.tensor, offset=at, ap=[[1, GRID_W], [RPB_C, ROWS], [1, GRID_W]])
                    sp.dma_start(BM[64 * r:64 * r + 64, j % 4, :].rearrange("p (a b) -> p a b", a=ROWS),
                                 src).then_inc(bias_in[j % 4], 16)

            wg, wu = (A[n].rearrange("o e (k p) n -> (o e) p k n", p=P) for n in ("od_exp_wg", "od_exp_wu"))
            wd = A["od_exp_wd"].rearrange("o e (k p) n -> (o e) p k n", p=P)

            def wave_loads(w, e, first):
                for i in range(NEC):
                    if i >= RING_E:
                        j = i - RING_E
                        if j < 2 * NUP:
                            sp.wait_ge(gu_mm, NUP * w + j // 2 + 1)
                        else:
                            sp.wait_ge(dn_mm, NDN * w + j - 2 * NUP + 1)
                    elif first and i == RING:
                        begin(sp, None, "out1")
                    elif first and i < RING:
                        sp.wait_ge(*stream[-RING:][(i - len(stream)) % RING][2])
                    elif not first:
                        sp.wait_ge(dn_mm, NDN * w + i - RING_E + 1)
                    dst = BIG[:, (i % RING_E) * SLOT:(i % RING_E) * SLOT + SLOT]
                    if i < 2 * NUP:
                        src = (wg, wu)[i % 2][e, :, :, 512 * (i // 2):512 * (i // 2) + 512]
                        sp.dma_start(dst.rearrange("p (k n) -> p k n", k=KB), src).then_inc(arrived_e[i % RING_E], 16)
                    else:
                        j = 4 * (i - 2 * NUP)
                        sp.dma_start(dst.rearrange("p (k n) -> p k n", k=4),
                                     wd[e, :, j:j + 4, :]).then_inc(arrived_e[i % RING_E], 16)

            wave_loads(0, 0, True)
            with sp.Fori(1, E) as w:
                wave_loads(w, w, False)
            sp.wait_ge(rt_tab, 2)
            waves = sp.value_load(RI[0:1, 0:1], min_val=E, max_val=WAVES)
            with sp.If(waves > E):
                with sp.Fori(E, waves) as w:
                    e = sp.value_load(RI[0:1, bass.ds(w - E + 1, 1)], min_val=0, max_val=E - 1)
                    wave_loads(w, e, False)

            sp.wait_ge(fin_ok, 2)
            sp.dma_start(out[0].rearrange("(t p) n -> p t n", p=P), X[:, 0:2, :]).then_inc(s_out, 16)
            sp.wait_ge(s_out, 16)

        @block.gpsimd
        def _(pool):
            def seq(ins, count=[0]):
                count[0] += 1
                ins.then_inc(pool_seq, 1)
                pool.wait_ge(pool_seq, count[0])

            pool.memset(ROWSB[:, :], 0.0).then_inc(rows_zero, 1)
            pool.memset(ST[:, :, :], 0.0).then_inc(st_zero, 1)
            pool.memset(ONE[:, :], 1.0).then_inc(done["pool"], 1)

            begin(pool, "pool", "gdn")

            def heads(m):
                return CM[:, m, :].rearrange("p (a b) -> p a b", a=1).to_broadcast([P, 4, P])

            def gU(s, d):
                b, t = DIR[d], TILE_OF[d][s]
                if s:
                    pool.wait_ge(g_seg, both(d, s))
                for h in range(4):
                    last = pool.tensor_scalar(b["gU"][:, h, :], CM[:, UP if d == 0 else LO, :],
                                              GB8[:, t, 0, 4 * d + h:4 * d + h + 1], None, ALU.mult)
                last.then_inc(g_gU, 1)

            for d in dirs:
                gU(0, d)
            for s in range(NT):
                for d in dirs:
                    b = DIR[d]
                    pool.wait_ge(g_exp, both(d, s + 1))
                    pool.tensor_tensor(b["dec"], b["dec"], heads(SLO if d == 0 else SUP), ALU.mult)
                    pool.tensor_tensor(b["decT"], b["decT"], heads(UP if d == 0 else LO), ALU.mult).then_inc(g_msk, 1)
                for d in dirs:
                    b = DIR[d]
                    pool.wait_ge(g_A, both(d, s + 1))
                    if s:
                        pool.wait_ge(g_vn, both(d, s))
                    seq(pool.tensor_tensor(b["Dm"], b["A"], heads(LEV), ALU.mult))
                    pool.tensor_tensor(b["Dm"], heads(IDENT), b["Dm"], ALU.subtract).then_inc(g_D1, 1)
                for n in range(1, LEVELS):
                    for d in dirs:
                        b = DIR[d]
                        if n == 1:
                            pool.wait_ge(g_AT, both(d, s + 1))
                            if s:
                                pool.wait_ge(g_M1, both(d, (LEVELS - 1) * s))
                        else:
                            pool.wait_ge(g_M1, both(d, (LEVELS - 1) * s + n - 1))
                        pool.tensor_tensor(b["LT"], b["AT"], heads(LEV + n), ALU.mult).then_inc(g_LT, 1)
                for d in dirs:
                    if s + 1 < NT:
                        gU(s + 1, d)
            gain = GG[:, :].rearrange("p (a n) -> p a n", a=1).to_broadcast([P, 4, P])
            for t in range(NT):
                z = ZS[:, t, :].rearrange("p (h n) -> p h n", h=4)
                pool.tensor_tensor(z, z, gain, ALU.mult).then_inc(gz_ready, 1)
            pool.wait_ge(gz_ready, NT)
            pool.wait_ge(g_LT, both(1, (LEVELS - 1) * NT))
            pool.nop().then_inc(done["pool"], 1)

            begin(pool, "pool", "natt")
            for j in range(2 * H_C):
                pool.wait_ge(bias_in[j % 4], 32 * (j // 4 + 1))
                v = BM[:, j % 4, :].rearrange("p (a b) -> p a b", a=ROWS)
                m = WM[:, :].rearrange("p (a b) -> p a b", a=1).to_broadcast([P, ROWS, GRID_W])
                pool.tensor_tensor(v, v, m, ALU.add).then_inc(bias_ok, 1)
            pool.wait_ge(bias_ok, 2 * H_C)
            pool.nop().then_inc(done["pool"], 1)

        @block.scalar
        def _(act):
            def seq(ins, count=[0]):
                count[0] += 1
                ins.then_inc(act_seq, 1)
                act.wait_ge(act_seq, count[0])

            def everywhere(ap, n):
                return bass.AP(tensor=ap.tensor, offset=0, ap=[[0, P], [1, n]])

            def load_ada_b(l):
                rows = A["ada_b"][l:l + 1, :].rearrange("o (g c n) -> o g c n", g=3, c=4)
                for c in range(4):
                    for r in range(2):
                        act.dma_start(BADD[32 * c + r:32 * c + r + 1, :, :], rows[:, :, c, :]).then_inc(s_bias, 16)

            def squares(n, sem, value, bank):
                for i in range(n):
                    act.wait_ge(sem, value(i))
                    seq(act.activation(PS[:, bank:bank + 2, :].rearrange("p a b -> p (a b)"), X[:, i, :], ACT.Square,
                                       accum_out=SS[:, i:i + 1]))
                act.activation(SS[:, 8:8 + n], SS[:, 0:n], ACT.Sqrt, bias=EPSC[:, 0:1], scale=1.0 / D).then_inc(norm_sd, 1)

            act.wait_ge(rows_zero, 1)
            act.dma_start(ROWSB[0:KB, :], A["c"].rearrange("o (k n) -> (o k) n", n=P)).then_inc(s_rows, 16)
            act.dma_start(ROWSB[KB:2 * KB, :], A["c_ctx"].rearrange("(k n) -> k n", n=P)).then_inc(s_rows, 16)
            act.dma_start(ROWSB[R_NG:R_NG + 4 * KB, :],
                          A["norm_g"].rearrange("l w (k n) -> (l w k) n", n=P)).then_inc(s_rows, 16)
            act.dma_start(ROWSB[R_CONV:R_CONV + 12 * TAPS, :],
                          A["ev_conv_w"].rearrange("o j (b n) -> (o j b) n", n=P)).then_inc(s_rows, 16)
            act.dma_start(ROWSB[R_QG:R_QG + 3, :],
                          A["ev_q_norm_g"].rearrange("o (k n) -> (o k) n", n=P)).then_inc(s_rows, 16)
            act.dma_start(ROWSB[R_KVG:R_KVG + 2, :],
                          A["ev_kv_norm_g"].rearrange("o (k n) -> (o k) n", n=P)).then_inc(s_rows, 16)
            act.dma_start(CM[:, :, :].rearrange("p a b -> p (a b)"), A["masks"]).then_inc(s_const, 16)
            act.dma_start(X[:, 0:2, :], A["x"][0].rearrange("(t p) n -> p t n", p=P)).then_inc(s_x, 16)
            act.dma_start(X[:, 2:4, :], A["ctx"][0].rearrange("(t p) n -> p t n", p=P)).then_inc(s_x, 16)
            act.dma_start(CS[NOPE:NOPE + ROPE, :, :], A["rope"]).then_inc(s_misc, 16)
            act.dma_start(WM[:, :], A["window"]).then_inc(s_misc, 16)
            act.dma_start(DTB[:, 0, :], everywhere(A["ev_dt_bias"], 8)).then_inc(s_misc, 16)
            act.dma_start(DTB[:, 1, :], everywhere(A["ev_a_log"], 8)).then_inc(s_misc, 16)
            act.dma_start(GG[:, :], everywhere(A["ev_gdn_norm_g"], P)).then_inc(s_misc, 16)
            act.dma_start(RW[:, :, :], A["od_router"][0].rearrange("(k p) n -> p k n", p=P)).then_inc(s_misc, 16)
            act.wait_ge(st_zero, 1)
            act.wait_ge(bias_zero, 1)
            load_ada_b(0)
            squares(NT, s_x, lambda i: 32, 0)
            act.wait_ge(sm_cols, 1)
            act.activation(ST[:, :, 0:2], SM[:, 0:2 * KB].rearrange("p (r k) -> p k r", r=2),
                           ACT.Silu).then_inc(done["act"], 1)

            def norm(stage, n, nt0, xn):
                begin(act, "act", stage)
                act.wait_ge(norm_rstd, ("norm0", "norm1", "norm2", "norm3").index(stage) + 1)
                for i in range(n):
                    if i >= 2:
                        act.wait_ge(norm_tr, nt0 + i - 1)
                    last = act.activation(xn(i), X[:, i, :], ACT.Copy, scale=SS[:, 16 + i:17 + i])
                    last.then_inc(xn_ready, 1)
                act.wait_ge(xn_ready, nt0 + n)
                act.nop().then_inc(done["act"], 1)

            act.wait_ge(s_misc, 96)
            act.activation(EA[:, :], DTB[:, 1, :], ACT.Exp).then_inc(done["act"], 1)

            norm("norm0", NT, 0, lambda i: XN[:, i % 2, :])

            begin(act, "act", "win")
            act.wait_ge(cin_zero, 1)

            def conv_in(b):
                act.wait_ge(win_mm, b + 1)
                if b >= 2:
                    act.wait_ge(conv_done, b - 1)
                act.activation(CIN[:, b % 2, :, 2:2 + L], PS[:, b % 4, :].rearrange("p (a t) -> p a t", a=2),
                               ACT.Copy).then_inc(cin_ready, 1)

            def conv_out(b):
                act.wait_ge(conv_done, b + 1)
                return act.activation(qkvT[:, b, :], CACC[:, b % 2, :], ACT.Silu)

            conv_in(0)
            for b in range(12):
                if b < 11:
                    conv_in(b + 1)
                conv_out(b).then_inc(conv_ev if b < 11 else done["act"], 1)

            begin(act, "act", "tok")
            for t in range(NT):
                act.wait_ge(tok_mm, t + 1)
                act.activation(ZS[:, t, :], PS[:, t % 4, :], ACT.Silu).then_inc(tok_z, 1)
            act.wait_ge(tok_z, NT)
            act.nop().then_inc(done["act"], 1)

            begin(act, "act", "mproj")
            for t in range(NT):
                seq(act.activation(PM[:, 0, 0:QR], P2[:, t, CQ0:CQ0 + QR], ACT.Square, accum_out=SS[:, t:t + 1]))
                seq(act.activation(PM[:, 0, 0:KVR], P2[:, t, CKV0:CKV0 + KVR], ACT.Square,
                                   accum_out=SS[:, 4 + t:5 + t]))
            act.activation(SS[:, 8:12], SS[:, 0:4], ACT.Sqrt, bias=EPSC[:, 0:1], scale=1.0 / QR).then_inc(m_sd, 1)
            act.activation(SS[:, 12:16], SS[:, 4:8], ACT.Sqrt, bias=EPSC[:, 0:1], scale=1.0 / KVR).then_inc(m_sd, 1)
            act.wait_ge(sp_in, 1)
            seq(act.activation(GB8[:, :, 0, :], GB8[:, :, 2, :], ACT.Abs))
            seq(act.activation(GB8[:, :, 0, :], GB8[:, :, 0, :], ACT.Exp, scale=-1.0))
            act.activation(GB8[:, :, 0, :], GB8[:, :, 0, :], ACT.Ln, bias=ONE[:, 0:1]).then_inc(sp_ln, 1)
            act.activation(GB8[:, :, 1, :], P2[:, :, 8:16], ACT.Sigmoid).then_inc(sp_ln, 1)
            for j in range(2 * H_B + NT):
                act.wait_ge(mproj_mm, j + 1)
                if j < H_B:
                    to, of = QT[0:QD, j, :], PS[0:QD, j % 4, :]
                elif j < 2 * H_B:
                    to, of = KT[0:NOPE, j - H_B, :], PS[0:NOPE, j % 4, :]
                else:
                    to, of = VB[:, j - 2 * H_B, :], PS[:, j % 4, :]
                act.activation(to, of, ACT.Copy).then_inc(mproj_ev, 1)
            act.wait_ge(mproj_ev, 2 * H_B + NT)
            act.nop().then_inc(done["act"], 1)

            def attention(items, base, pm, pt, scale):
                def exp(j):
                    n = items[j][2]
                    act.wait_ge(att_max, base + j + 1)
                    if j >= 3:
                        act.wait_ge(att_tr, base + j - 2)
                    act.activation(pm[:, j % 3, 0:n * P], PS[:, j % 3, 0:n * P], ACT.Exp, bias=RT[:, j % 4:j % 4 + 1],
                                   scale=scale, accum_out=RT[:, 8 + j % 4:9 + j % 4]).then_inc(att_p, 1)

                for i in range(len(items) + 2):
                    if i < len(items):
                        exp(i)
                    j = i - 2
                    if j < 0:
                        continue
                    act.wait_ge(att_tr, base + j + 1)
                    if j >= 2:
                        act.wait_ge(att_o, base + j - 1)
                    n = items[j][2]
                    act.activation(pt[:, j % 2, 0:n, :],
                                   PS[:, 3 + j % 2, 0:n * P].rearrange("p (a b) -> p a b", a=n),
                                   ACT.Copy).then_inc(att_pt, 1)
                act.wait_ge(att_pt, base + len(items))
                act.nop().then_inc(done["act"], 1)

            begin(act, "act", "matt")
            attention(M_ITEMS, 0, PM, PT, QD ** -0.5)

            begin(act, "act", "l2")
            for b in range(8):
                if b >= 2:
                    act.wait_ge(l2_ss, b - 1)
                act.activation(SQ[:, b % 2, :], qkvT[:, b, :], ACT.Square).then_inc(l2_sq, 1)
            act.wait_ge(l2_ss, 8)
            act.activation(SS[:, 0:16], PS[:, 0, 0:16], ACT.Sqrt, bias=EPSC[:, 1:2], scale=float(DK)).then_inc(l2_sd, 1)
            act.activation(SS[:, 16:32], PS[:, 0, 16:32], ACT.Sqrt, bias=EPSC[:, 0:1]).then_inc(l2_sd, 1)
            for i in range(8):
                act.wait_ge(l2_tr, i + 1)
                act.activation((KTOK, VTOK)[i % 2][:, i // 2, :], PS[:, 6 + i % 2, :], ACT.Copy).then_inc(l2_ev, 1)
            act.wait_ge(l2_ev, 8)
            act.nop().then_inc(done["act"], 1)

            begin(act, "act", "gdn")
            for s in range(NT):
                for d in dirs:
                    b, B = DIR[d], 4 * d
                    act.wait_ge(g_seg, both(d, s + 1))
                    act.activation(b["decT"], PS[:, B, :], ACT.Exp)
                    act.activation(b["dec"], PS[:, B + 1, :], ACT.Exp).then_inc(g_exp, 1)
                    act.wait_ge(g_sm, both(d, s + 1))
                    act.activation(EG[:, d, :], PS[:, B + 2, 0:12], ACT.Exp).then_inc(g_eg, 1)
                for d in dirs:
                    b, B = DIR[d], 4 * d
                    act.wait_ge(g_At, both(d, s + 1))
                    act.activation(b["AT"], PS[:, B, :], ACT.Copy).then_inc(g_AT, 1)
                for n in range(1, LEVELS):
                    for d in dirs:
                        b, B = DIR[d], 4 * d
                        act.wait_ge(g_M1, both(d, (LEVELS - 1) * s + n))
                        act.activation(b["dec"], PS[:, B + 1, :], ACT.Copy).then_inc(g_M1e, 1)
                for d in dirs:
                    b, B = DIR[d], 4 * d
                    act.wait_ge(g_wT, both(d, s + 1))
                    act.activation(b["Dm"], PS[:, B + 1, :], ACT.Copy, scale=-1.0).then_inc(g_wTe, 1)
                for d in dirs:
                    b, B = DIR[d], 4 * d
                    act.wait_ge(g_vn, both(d, s + 1))
                    act.activation(b["A"], PS[:, B, :], ACT.Copy).then_inc(g_vne, 1)
            for d in dirs:
                act.wait_ge(g_vne, both(d, NT))
            act.nop().then_inc(done["act"], 1)

            begin(act, "act", "gout")
            for t in range(NT):
                act.wait_ge(go_sum, t + 1)
                for h in range(4):
                    seq(act.activation(PS[:, 4, 0:DK], OD[:, 0, t, h * DK:h * DK + DK], ACT.Square,
                                       accum_out=SS[:, 4 * t + h:4 * t + h + 1]))
            act.activation(SS[:, 16:32], SS[:, 0:16], ACT.Sqrt, bias=EPSC[:, 0:1], scale=1.0 / DK).then_inc(go_sd, 1)
            for t in range(NT):
                act.wait_ge(go_tr, t + 1)
                last = act.activation(mixT[:, 0:4, t * P:t * P + P], PS[:, t, :].rearrange("p (h n) -> p h n", h=4),
                                      ACT.Copy)
                last.then_inc(go_ev if t < NT - 1 else done["act"], 1)

            def gate_rows(stage, k, to, n):
                begin(act, "act", stage)
                act.wait_ge(gb_mm, k + 1)
                for r in range(n):
                    for c in range(2):
                        last = act.activation(to[:, r, 512 * c:512 * c + 512], PS[:, 4 + 2 * r + c, :], ACT.Copy)
                last.then_inc(gb_ready, 1)
                act.wait_ge(gb_ready, k + 1)

            gate_rows("out0", 0, GB, 2)
            squares(NT, out_ev, lambda i: NT + i + 1, 4)
            act.nop().then_inc(done["act"], 1)
            norm("norm1", NT, 4, lambda i: XN[:, i % 2, :])

            gate_rows("up", 1, GB, 2)
            act.wait_ge(bias_zero, 2)
            load_ada_b(1)
            act.dma_start(FG, everywhere(A["final_norm_g"], D)).then_inc(s_fg, 16)
            for f in range(FF // P):
                act.wait_ge(up_mm, f + 1)
                if f >= 2:
                    act.wait_ge(up_ev, f - 1)
                act.activation(SG[:, f % 2, :], PS[:, 2 * (f % 2), :], ACT.Silu).then_inc(up_silu, 1)
            act.wait_ge(up_silu, FF // P)
            act.nop().then_inc(done["act"], 1)

            begin(act, "act", "down")
            squares(NT, down_ev, lambda i: NT + i + 1, 0)
            act.nop().then_inc(done["act"], 1)

            norm("norm2", NT, 8, lambda i: XN[:, i % 2, :])

            begin(act, "act", "qkv")
            for i in range(0, 24, 2):
                act.wait_ge(qkv_mm, i + 1)
                to, of = qkv_place(i)
                act.activation(to, of, ACT.Copy).then_inc(qkv_ev[0], 1)
            act.wait_ge(qkv_ev[0], 12)
            act.nop().then_inc(done["act"], 1)

            begin(act, "act", "natt")
            attention(N_ITEMS, len(M_ITEMS), PC, PCT, DH ** -0.5)

            gate_rows("out1", 2, GB, 1)
            squares(2, out_ev, lambda i: 2 * NT + 2 + i + 1, 6)
            act.nop().then_inc(done["act"], 1)
            norm("norm3", 2, 12, lambda i: X[:, 2 + i, :])

            begin(act, "act", "route")
            act.wait_ge(gb_mm, 4)
            for c in range(2):
                last = act.activation(GE[:, 512 * c:512 * c + 512], PS[:, 4 + c, :], ACT.Copy)
            last.then_inc(ge_ready, 1)
            act.wait_ge(rt_d, 1)
            act.activation(RTB[:, 80:82], RTB[:, 82:84], ACT.Exp).then_inc(rt_e, 1)
            act.wait_ge(rt_e, 1)
            act.wait_ge(ge_ready, 1)
            act.nop().then_inc(done["act"], 1)

            begin(act, "act", "moe")
            act.wait_ge(e_zero, 1)
            waves = act.value_load(RI[0:1, 0:1], min_val=E, max_val=WAVES)
            with act.Fori(0, waves) as w:
                more = act.value_load(RIB[0:1, bass.ds(w, 1)], min_val=0, max_val=1)
                act.wait_ge(e_tr, w + 1)
                act.activation(SELT, PS[:, 6, 0:2 * P].rearrange("p (a b) -> p a b", a=2), ACT.Copy).then_inc(e_trev, 1)

                def silu(s):
                    act.wait_ge(gu_mm, NUP * w + s + 1)
                    if s >= 2:
                        act.wait_ge(e_h, NUP * w + s - 1)
                    act.activation(SEB[s % 2][64:P, :], PS[0:64, 2 + s % 2, :], ACT.Silu)
                    act.activation(SE[64:P, s % 2, :], PS[0:64, s % 2, :], ACT.Silu).then_inc(e_silu, 1)

                silu(0)
                for s in range(NUP):
                    if s < NUP - 1:
                        silu(s + 1)
                    act.wait_ge(e_htr, NUP * w + s + 1)
                    act.activation(HET[:, 4 * s:4 * s + 4, :], PS[:, 4 + s % 2, :].rearrange("p (a b) -> p a b", a=4),
                                   ACT.Copy).then_inc(e_htev, 1)
                act.wait_ge(rt_tab, 2)
                act.wait_ge(dn_mm, NDN * w + NDN)

                def take_y(bank, r0):
                    for n in range(2):
                        last = act.activation(YE[r0:r0 + 64, 0, 512 * n:512 * n + 512],
                                              PS[64 * n:64 * n + 64, bank, :], ACT.Copy)
                    return last

                with act.If(more > 0):
                    take_y(7, 64)
                take_y(6, 0).then_inc(e_y, 1)
            act.nop().then_inc(done["act"], 1)

            act.wait_ge(fin_x, 2)
            for i in range(2):
                seq(act.activation(QB[:, 0:D], X[:, i, :], ACT.Square, accum_out=SS[:, i:i + 1]))
            act.activation(SS[:, 8:10], SS[:, 0:2], ACT.Sqrt, bias=EPSC[:, 0:1], scale=1.0 / D).then_inc(fin_sd, 1)

        @block.vector
        def _(dve):
            def seq(ins, count=[0]):
                count[0] += 1
                ins.then_inc(dve_seq, 1)
                dve.wait_ge(dve_seq, count[0])

            def end(ins):
                ins.then_inc(done["dve"], 1)

            dve.memset(EPSC[:, 0:1], EPS)
            dve.memset(EPSC[:, 1:2], EPS * DK)
            dve.memset(BADD, 0.0).then_inc(bias_zero, 1)
            dve.wait_ge(sm_tr, 1)
            dve.tensor_copy(SM[:, :], PS[:, 7, 0:P]).then_inc(sm_cols, 1)
            dve.wait_ge(sm_cols, 1)
            dve.nop().then_inc(done["dve"], 1)

            def ada_rows(l, g):
                dve.wait_ge(ada_mm, 12 * l + 4 * g + 4)
                dve.tensor_tensor(MOD[:, g, :], PS[:, 4 + g, :], BADD[:, g, :], ALU.add).then_inc(mod_rows, 1)

            def ada_columns(l, g):
                dve.wait_ge(ada_tr, 3 * l + g + 1)
                v = PS[:, 4 + g, :].rearrange("p (j c q) -> p j c q", j=4, c=4)
                seq(dve.tensor_copy(MT[:, g, :, :, :], v[:, :, :, 0:2]))

            def ada_norm(l, which):
                sh, sc = ((0, 0), (0, 2)) if which == 0 else ((1, 2), (2, 0))
                ng = SM[:, R_NG + (2 * l + which) * KB:R_NG + (2 * l + which + 1) * KB]
                for r in range(2):
                    for c in range(2):
                        to = slice(4 * c, 4 * c + 4)
                        dve.scalar_tensor_tensor(AB[:, which, r, 0, to], MT[:, sc[0], :, sc[1] + c, r], 1.0,
                                                 ng[:, to], ALU.add, ALU.mult)
                        last = dve.tensor_copy(AB[:, which, r, 1, to], MT[:, sh[0], :, sh[1] + c, r])
                return last

            def norm(stage, n, nt0, l, which, dst):
                idx = ("norm0", "norm1", "norm2", "norm3").index(stage)
                begin(dve, "dve", stage)
                dve.wait_ge(norm_sd, idx + 1)
                dve.reciprocal(SS[:, 16:16 + n], SS[:, 8:8 + n]).then_inc(norm_rstd, 1)
                for i in range(n):
                    dve.wait_ge(norm_tr, nt0 + i + 1)
                    for k in range(KB):
                        r = i // 2
                        last = dve.tensor_scalar(dst[:, k, i * P:i * P + P],
                                                 PS[:, 2 * (i % 2) + k // 4, (k % 4) * P:(k % 4) * P + P],
                                                 AB[:, which, r, 0, k:k + 1], AB[:, which, r, 1, k:k + 1],
                                                 ALU.mult, ALU.add)
                    last.then_inc(norm_ev if i < n - 1 else done["dve"], 1)

            begin(dve, "dve", "ada0")
            dve.wait_ge(s_bias, 128)
            ada_rows(0, 0)
            ada_columns(0, 0)
            end(ada_norm(0, 0))
            norm("norm0", NT, 0, 0, 0, hT)

            begin(dve, "dve", "win")
            dve.memset(CIN, 0.0).then_inc(cin_zero, 1)
            for b in range(12):
                dve.wait_ge(cin_ready, b + 1)
                if b >= 2:
                    dve.wait_ge(conv_ev, b - 1)
                acc = CACC[:, b % 2, :].rearrange("p (a t) -> p a t", a=2)
                for j in range(TAPS):
                    w = SM[:, R_CONV + 12 * j + b:R_CONV + 12 * j + b + 1]
                    of = CIN[:, b % 2, :, j:j + L]
                    if j == 0:
                        seq(dve.tensor_scalar(acc, of, w, None, ALU.mult))
                    else:
                        ins = dve.scalar_tensor_tensor(acc, of, w, acc, ALU.mult, ALU.add)
                        if j < TAPS - 1:
                            seq(ins)
                ins.then_inc(conv_done, 1)
            dve.wait_ge(conv_done, 12)
            dve.nop().then_inc(done["dve"], 1)

            begin(dve, "dve", "tok")
            for j in range(NT, 3 * NT):
                dve.wait_ge(tok_mm, j + 1)
                c, t = j // NT - 1, j % NT
                dve.tensor_copy(P2[:, t, c * (REST // 2):(c + 1) * (REST // 2)],
                                PS[:, j % 4, 0:REST // 2]).then_inc(tok_ev, 1)
            for g in (1, 2):
                ada_rows(0, g)
            for g in (1, 2):
                ada_columns(0, g)
            end(ada_norm(0, 1))

            begin(dve, "dve", "mproj")
            dve.wait_ge(s_misc, 96)
            dt = DTB[:, 0:1, :].to_broadcast([P, NT, 8])
            dve.tensor_tensor(GB8[:, :, 2, :], P2[:, :, 0:8], dt, ALU.add).then_inc(sp_in, 1)
            dve.wait_ge(m_sd, 2)
            seq(dve.reciprocal(SS[:, 16:24], SS[:, 8:16]))
            for t in range(NT):
                v = P2[:, t, CQ0:CQ0 + QR]
                dve.tensor_scalar(v, v, SS[:, 16 + t:17 + t], None, ALU.mult)
                v = P2[:, t, CKV0:CKV0 + KVR]
                last = dve.tensor_scalar(v, v, SS[:, 20 + t:21 + t], None, ALU.mult)
            last.then_inc(m_nrm, 1)
            for k in range(3):
                dve.wait_ge(m_tr, k + 1)
                dve.tensor_scalar(CQT[:, k, :], PS[:, k, :], SM[:, R_QG + k:R_QG + k + 1], None,
                                  ALU.mult).then_inc(m_trev, 1)
            for k in range(2):
                dve.wait_ge(m_tr, k + 4)
                dve.tensor_scalar(CKVT[:, k, :], PS[:, 3 + k, :], SM[:, R_KVG + k:R_KVG + k + 1], None,
                                  ALU.mult).then_inc(m_trev, 1)
            dve.wait_ge(m_tr, 6)
            dve.tensor_copy(KT[NOPE:QD, 0, :], PS[NOPE:QD, 5, :]).then_inc(m_trev, 1)
            dve.wait_ge(sp_ln, 2)
            seq(dve.scalar_tensor_tensor(GB8[:, :, 2, :], GB8[:, :, 2, :], 0.0, GB8[:, :, 0, :], ALU.max, ALU.add))
            ea = EA[:, 0:1, :].to_broadcast([P, NT, 8])
            seq(dve.scalar_tensor_tensor(GB8[:, :, 0, :], GB8[:, :, 2, :], -1.0, ea, ALU.mult, ALU.mult))
            rs = slice(NOPE, QD)
            for j in range(H_B + 1):
                dve.wait_ge(rot_mm, j + 1)
                v = (QT[rs, j, 0:L] if j < H_B else KT[rs, 0, 0:L])
                seq(dve.tensor_tensor(RTMP[rs, j % 2, :], PS[rs, 4 + j % 2, 0:L], CS[rs, 1, :], ALU.mult))
                seq(dve.tensor_tensor(v, v, CS[rs, 0, :], ALU.mult))
                ins = dve.tensor_tensor(v, v, RTMP[rs, j % 2, :], ALU.add)
                ins.then_inc(rot_ev, 1)
            dve.wait_ge(rot_ev, H_B + 1)
            for h in range(1, H_B):
                last = dve.tensor_copy(KT[rs, h, :], KT[rs, 0, :])
            end(last)

            def attention(items, base, pm, out_of, scale):
                def largest(j):
                    n = items[j][2]
                    dve.wait_ge(att_s, base + j + 1)
                    seq(dve.tensor_reduce(RT[:, 4 + j % 4:5 + j % 4], PS[:, j % 3, 0:n * P], AX.X, ALU.max))
                    dve.tensor_scalar(RT[:, j % 4:j % 4 + 1], RT[:, 4 + j % 4:5 + j % 4], -scale, None,
                                      ALU.mult).then_inc(att_max, 1)

                def normalise(j):
                    dve.wait_ge(att_p, base + j + 1)
                    seq(dve.reciprocal(RT[:, 12 + j % 4:13 + j % 4], RT[:, 8 + j % 4:9 + j % 4]))
                    v = pm[:, j % 3, 0:items[j][2] * P]
                    dve.tensor_scalar(v, v, RT[:, 12 + j % 4:13 + j % 4], None, ALU.mult).then_inc(att_pn, 1)

                def take_out(j):
                    dve.wait_ge(att_o, base + j + 1)
                    r0 = 64 * (items[j][0] % 2)
                    dve.tensor_copy(out_of(j), PS[r0:r0 + 64, 5 + j % 2, 0:P]).then_inc(att_oe, 1)

                for i in range(len(items) + 4):
                    if i < len(items):
                        largest(i)
                    if 0 <= i - 1 < len(items):
                        normalise(i - 1)
                    if i - 4 >= 0:
                        take_out(i - 4)
                dve.wait_ge(att_oe, base + len(items))
                dve.nop().then_inc(done["dve"], 1)

            begin(dve, "dve", "matt")

            def out_of(j):
                h, t, _ = M_ITEMS[j]
                return YB[64 * (h % 2):64 * (h % 2) + 64, h // 2, t * P:t * P + P]

            attention(M_ITEMS, 0, PM, out_of, QD ** -0.5)

            begin(dve, "dve", "l2")
            for d in dirs:
                dve.memset(DIR[d]["S"], 0.0)
            dve.wait_ge(l2_sd, 2)
            dve.reciprocal(SS[:, 32:64], SS[:, 0:32]).then_inc(l2_r, 1)
            for b in range(8):
                dve.wait_ge(l2_bc, b + 1)
                dve.tensor_tensor(qkvT[:, b, :], qkvT[:, b, :], PS[:, 2 + b % 4, :], ALU.mult).then_inc(l2_ok, 1)
            dve.wait_ge(l2_ok, 8)
            dve.nop().then_inc(done["dve"], 1)

            begin(dve, "dve", "gdn")

            def heads(m):
                return CM[:, m, :].rearrange("p (a b) -> p a b", a=1).to_broadcast([P, 4, P])

            def vectors(s, d):
                b, t = DIR[d], TILE_OF[d][s]
                dve.wait_ge(g_eg, both(d, s + 1))
                be = RT[:, 8 + 4 * d:12 + 4 * d]
                seq(dve.tensor_tensor(be, GB8[:, t, 1, 4 * d:4 * d + 4], EG[:, d, 0:4], ALU.mult))
                for h in range(4):
                    kk, vv = KTOK[:, t, h * DK:h * DK + DK], VTOK[:, t, h * DK:h * DK + DK]
                    dve.tensor_scalar(b["kbe"][:, h, :], kk, be[:, h:h + 1], None, ALU.mult)
                    dve.tensor_scalar(b["kg"][:, h, :], kk, EG[:, d, 4 + h:5 + h], None, ALU.mult)
                    last = dve.tensor_scalar(b["vb"][:, h, :], vv, GB8[:, t, 1, 4 * d + h:4 * d + h + 1], None,
                                             ALU.mult)
                last.then_inc(g_vec, 1)

            for s in range(NT):
                for d in dirs:
                    b, B, t = DIR[d], 4 * d, TILE_OF[d][s]
                    dve.wait_ge(g_kk, both(d, s + 1))
                    dve.wait_ge(g_msk, both(d, s + 1))
                    for h in range(4):
                        beta = GB8[:, t, 1, 4 * d + h:4 * d + h + 1]
                        dve.scalar_tensor_tensor(b["A"][:, h, :], PS[:, B + 3, h * P:h * P + P], beta,
                                                 b["dec"][:, h, :], ALU.mult, ALU.mult)
                    dve.tensor_tensor(b["decT"], PS[:, B, :].rearrange("p (h n) -> p h n", h=4), b["decT"],
                                      ALU.mult).then_inc(g_A, 1)
                for d in dirs:
                    b = DIR[d]
                    dve.wait_ge(g_AT, both(d, s + 1))
                    seq(dve.tensor_tensor(b["Em"], b["AT"], heads(LEV), ALU.mult))
                    dve.tensor_tensor(b["Em"], heads(IDENT), b["Em"], ALU.subtract).then_inc(g_E1, 1)
                for n in range(1, LEVELS):
                    for d in dirs:
                        b, B = DIR[d], 4 * d
                        dve.wait_ge(g_PQ, both(d, (LEVELS - 1) * s + n))
                        if n < LEVELS - 1:
                            dve.tensor_tensor(b["Dm"], b["Dm"], PS[:, B + 2, :].rearrange("p (h n) -> p h n", h=4),
                                              ALU.subtract)
                        dve.tensor_tensor(b["Em"], b["Em"], PS[:, B + 3, :].rearrange("p (h n) -> p h n", h=4),
                                          ALU.subtract).then_inc(g_DE, 1)
                    if n <= 2:
                        vectors(s, n - 1)
                for d in dirs:
                    b, B, t = DIR[d], 4 * d, TILE_OF[d][s]
                    dve.wait_ge(g_o, both(d, s + 1))
                    seq(dve.tensor_copy(OD[:, d, t, :], PS[:, B + 3, :]))
                    for h in range(4):
                        hs = slice(h * DK, h * DK + DK)
                        dve.scalar_tensor_tensor(OD[:, d, t, hs], PS[:, B + 2, hs], EG[:, d, h:h + 1],
                                                 OD[:, d, t, hs], ALU.mult, ALU.add)
                        last = dve.scalar_tensor_tensor(b["S"][:, h, :], b["S"][:, h, :], EG[:, d, 8 + h:9 + h],
                                                        PS[:, B + 1, hs], ALU.mult, ALU.add)
                    last.then_inc(g_S, 1)
            for d in dirs:
                dve.wait_ge(g_S, both(d, NT))
            dve.nop().then_inc(done["dve"], 1)

            begin(dve, "dve", "gout")
            for t in range(NT):
                dve.tensor_tensor(OD[:, 0, t, :], OD[:, 0, t, :], OD[:, 1, t, :], ALU.add).then_inc(go_sum, 1)
            dve.wait_ge(go_sd, 1)
            seq(dve.reciprocal(SS[:, 32:48], SS[:, 16:32]))
            for t in range(NT):
                for h in range(4):
                    hs = slice(h * DK, h * DK + DK)
                    last = dve.scalar_tensor_tensor(OD[:, 0, t, hs], OD[:, 0, t, hs],
                                                    SS[:, 32 + 4 * t + h:33 + 4 * t + h], ZS[:, t, hs], ALU.mult, ALU.mult)
                last.then_inc(go_n, 1)
            dve.wait_ge(go_n, NT)
            dve.nop().then_inc(done["dve"], 1)

            def add_out(stage, base, nt):
                begin(dve, "dve", stage)
                dve.wait_ge(gb_ready, 1 if stage == "out0" else 3)
                for i in range(2 * nt):
                    n, t = i // nt, i % nt
                    cols = slice(512 * n, 512 * n + 512)
                    dve.wait_ge(out_mm, base + i + 1)
                    seq(dve.tensor_tensor(ZS[:, i % 2, :], PS[:, i % 4, :], GB[:, t // 2, cols], ALU.mult))
                    dve.tensor_tensor(X[:, t, cols], X[:, t, cols], ZS[:, i % 2, :], ALU.add).then_inc(out_ev, 1)
                dve.wait_ge(out_ev, base + 2 * nt)
                dve.nop().then_inc(done["dve"], 1)

            add_out("out0", 0, NT)
            norm("norm1", NT, 4, 0, 1, hT)

            begin(dve, "dve", "up")
            dve.memset(BADD, 0.0).then_inc(bias_zero, 1)
            for f in range(FF // P):
                dve.wait_ge(up_silu, f + 1)
                dve.tensor_tensor(H2T[:, f, :], SG[:, f % 2, :], PS[:, 2 * (f % 2) + 1, :], ALU.mult).then_inc(up_ev, 1)
            dve.wait_ge(s_bias, 256)
            for g in range(3):
                ada_rows(1, g)
            for g in range(3):
                ada_columns(1, g)
            ada_norm(1, 0)
            end(ada_norm(1, 1))

            begin(dve, "dve", "down")
            for n in range(2):
                dve.wait_ge(down_mm, 3 * n + 3)
                for t in range(NT):
                    cols = slice(512 * n, 512 * n + 512)
                    seq(dve.tensor_tensor(ZS[:, t % 2, :], PS[:, 4 * n + t, :], GB[:, t // 2, cols], ALU.mult))
                    dve.tensor_tensor(X[:, t, cols], X[:, t, cols], ZS[:, t % 2, :], ALU.add).then_inc(down_ev, 1)
            dve.wait_ge(down_ev, 2 * NT)
            dve.nop().then_inc(done["dve"], 1)

            norm("norm2", NT, 8, 1, 0, hT)

            begin(dve, "dve", "qkv")
            for i in range(1, 24, 2):
                dve.wait_ge(qkv_mm, i + 1)
                to, of = qkv_place(i)
                dve.tensor_copy(to, of).then_inc(qkv_ev[1], 1)
            dve.wait_ge(qkv_ev[1], 12)
            dve.nop().then_inc(done["dve"], 1)

            begin(dve, "dve", "natt")

            def out_of(j):
                h, t, _ = N_ITEMS[j]
                return OC[64 * (h % 2):64 * (h % 2) + 64, h // 2, t * P:t * P + P]

            attention(N_ITEMS, len(M_ITEMS), PC, out_of, DH ** -0.5)

            add_out("out1", 2 * NT, 2)
            norm("norm3", 2, 12, 1, 1, fT)

            begin(dve, "dve", "route")

            def r8(at, n=2):
                return RTB[:, at:at + 8 * n].rearrange("p (t e) -> p t e", t=n)

            LG, PK1, PK2, TMP, WT, PRIO = r8(0), r8(16), r8(32), r8(48), r8(64), RTB[:, 96:104]
            M1, M2 = RTB[:, 84:86], RTB[:, 86:88]
            dve.wait_ge(rt_mm, 1)
            seq(dve.tensor_copy(LG, PS[:, 0, 0:16].rearrange("p (t e) -> p t e", t=2)))
            seq(dve.tensor_scalar(PRIO, CM[:, IOTA, 0:8], -1.0, 8.0, ALU.mult, ALU.add))

            def pick(mx, pk):
                seq(dve.tensor_reduce(mx, LG, AX.X, ALU.max))
                for t in range(2):
                    seq(dve.scalar_tensor_tensor(TMP[:, t, :], LG[:, t, :], mx[:, t:t + 1], PRIO, ALU.is_equal, ALU.mult))
                seq(dve.tensor_reduce(RTB[:, 88:90], TMP, AX.X, ALU.max))
                for t in range(2):
                    seq(dve.tensor_scalar(pk[:, t, :], TMP[:, t, :], RTB[:, 88 + t:89 + t], None, ALU.is_equal))

            pick(M1, PK1)
            seq(dve.scalar_tensor_tensor(LG, PK1, -3e38, LG, ALU.mult, ALU.add))
            pick(M2, PK2)
            dve.tensor_tensor(RTB[:, 82:84], M2, M1, ALU.subtract).then_inc(rt_d, 1)
            seq(dve.tensor_tensor(SELM[:, :, :], PK1, PK2, ALU.add))
            dve.nop().then_inc(rt_ev, 1)
            dve.wait_ge(rt_e, 1)
            G1, G2 = RTB[:, 90:92], RTB[:, 92:94]
            seq(dve.tensor_scalar(G1, RTB[:, 80:82], 1.0, None, ALU.add))
            seq(dve.reciprocal(G1, G1))
            seq(dve.tensor_tensor(G2, G1, RTB[:, 80:82], ALU.mult))
            for t in range(2):
                seq(dve.tensor_scalar(TMP[:, t, :], PK1[:, t, :], G1[:, t:t + 1], None, ALU.mult))
                seq(dve.scalar_tensor_tensor(WT[:, t, :], PK2[:, t, :], G2[:, t:t + 1], TMP[:, t, :], ALU.mult, ALU.add))
            dve.wait_ge(rk_mm, 1)
            RK = r8(0)
            for t in range(2):
                seq(dve.scalar_tensor_tensor(RK[:, t, :], PS[:, 1, 8 * t:8 * t + 8], 1.0, SELM[:, t, :], ALU.add,
                                             ALU.mult))
            seq(dve.tensor_scalar(RK, RK, -1.0, None, ALU.add))
            OV, ORD, OH = RTB[:, 104:112], RTB[:, 112:120], RTB[:, 120:128]
            seq(dve.tensor_scalar(OV, PS[:, 1, 16:24], float(P), None, ALU.is_gt))
            seq(dve.memset(ORD, 0.0))
            for e in range(1, E):
                seq(dve.tensor_tensor(ORD[:, e:e + 1], ORD[:, e - 1:e], OV[:, e - 1:e], ALU.add))
            for t in range(2):
                seq(dve.tensor_copy(WR[:, t, 0:E], RK[:, t, :]))
                seq(dve.tensor_copy(WG[:, t, 0:E], WT[:, t, :]))
            seq(dve.tensor_reduce(RF[:, 0:1], OV, AX.X, ALU.add))
            seq(dve.tensor_scalar(RF[:, 0:1], RF[:, 0:1], float(E), None, ALU.add))
            for j in range(WAVES - E):
                seq(dve.scalar_tensor_tensor(OH, ORD, float(j), OV, ALU.is_equal, ALU.mult))
                seq(dve.tensor_tensor(PRIO, OH, CM[:, IOTA, 0:8], ALU.mult))
                seq(dve.tensor_reduce(RF[:, 1 + j:2 + j], PRIO, AX.X, ALU.add))
                for t in range(2):
                    seq(dve.scalar_tensor_tensor(PRIO, RK[:, t, :], float(1 - P), OH, ALU.add, ALU.mult))
                    seq(dve.tensor_reduce(WR[:, t, E + j:E + j + 1], PRIO, AX.X, ALU.add))
                    seq(dve.tensor_scalar(WR[:, t, E + j:E + j + 1], WR[:, t, E + j:E + j + 1], -1.0, None, ALU.add))
                    seq(dve.tensor_tensor(PRIO, WT[:, t, :], OH, ALU.mult))
                    seq(dve.tensor_reduce(WG[:, t, E + j:E + j + 1], PRIO, AX.X, ALU.add))
            seq(dve.tensor_scalar(RFB[:, 0:E], PS[:, 1, 16:24], float(P // 2), None, ALU.is_gt))
            seq(dve.tensor_scalar(OV, PS[:, 1, 16:24], float(P + P // 2), None, ALU.is_gt))
            for j in range(WAVES - E):
                seq(dve.scalar_tensor_tensor(OH, ORD, float(j), OV, ALU.is_equal, ALU.mult))
                seq(dve.tensor_reduce(RFB[:, E + j:E + j + 1], OH, AX.X, ALU.add))
            dve.tensor_copy(RIB[:, :], RFB[:, :]).then_inc(rt_tab, 1)
            dve.tensor_copy(RI[:, 0:4], RF[:, 0:4]).then_inc(rt_tab, 1)
            dve.wait_ge(rt_tab, 2)
            dve.nop().then_inc(done["dve"], 1)

            begin(dve, "dve", "moe")
            waves = dve.value_load(RI[0:1, 0:1], min_val=E, max_val=WAVES)
            dve.memset(YE, 0.0)
            dve.memset(HE, 0.0).then_inc(e_zero, 1)
            dve.memset(ACC, 0.0).then_inc(e_add, 4)
            dve.wait_ge(e_add, 4)
            with dve.Fori(0, waves) as w:
                for t in range(2):
                    dve.tensor_scalar(SEL[:, t, :], CM[:, IOTA, :], WR[:, t, bass.ds(w, 1)], None, ALU.is_equal)
                    last = dve.tensor_scalar(SEL[:, 2 + t, :], CM[:, IOTA, :], WR[:, t, bass.ds(w, 1)],
                                             WG[:, t, bass.ds(w, 1)], ALU.is_equal, ALU.mult)
                last.then_inc(e_sel, 1)
                for half in range(2):
                    dve.wait_ge(e_gmm, 2 * w + half + 1)
                    for k in range(4 * half, 4 * half + 4):
                        last = dve.tensor_scalar(XG[:, k, :], PS[:, 4 + half, (k % 4) * P:(k % 4) * P + P],
                                                 AB[:, 1, 0, 0, k:k + 1], AB[:, 1, 0, 1, k:k + 1], ALU.mult, ALU.add)
                    last.then_inc(e_gev, 1)
                for s in range(NUP):
                    dve.wait_ge(e_silu, NUP * w + s + 1)
                    if s >= 2:
                        dve.wait_ge(e_htr, NUP * w + s - 1)
                    dve.tensor_tensor(HE[64:P, s % 2, :], SEB[s % 2][64:P, :], PS[64:P, 2 + s % 2, :], ALU.mult)
                    dve.tensor_tensor(HE[0:64, s % 2, :], SE[64:P, s % 2, :], PS[64:P, s % 2, :],
                                      ALU.mult).then_inc(e_h, 1)
                for i in range(4):
                    dve.wait_ge(e_sc, 4 * w + i + 1)
                    v = ACC[:, i // 2, 512 * (i % 2):512 * (i % 2) + 512]
                    dve.tensor_tensor(v, v, PS[:, i, :], ALU.add).then_inc(e_add, 1)
            dve.wait_ge(e_add, 4 * waves + 4)
            for t in range(2):
                seq(dve.tensor_tensor(ACC[:, t, :], ACC[:, t, :], GE, ALU.mult))
                seq(dve.tensor_tensor(X[:, t, :], X[:, t, :], ACC[:, t, :], ALU.add))
                dve.nop().then_inc(fin_x, 1)

            dve.wait_ge(fin_sd, 1)
            seq(dve.reciprocal(SS[:, 16:18], SS[:, 8:10]))
            dve.wait_ge(s_fg, 16)
            for t in range(2):
                dve.scalar_tensor_tensor(X[:, t, :], X[:, t, :], SS[:, 16 + t:17 + t], FG, ALU.mult,
                                         ALU.mult).then_inc(fin_ok, 1)

        @block.tensor
        def _(pe):
            mm = pe.matmul

            def end():
                pe.nop().then_inc(done["pe"], 1)

            def ident(n=P):
                return CM[0:n, IDENT, 0:n]

            pe.wait_ge(s_rows, 96)
            pe.wait_ge(s_const, 16)
            pe.transpose(PS[:, 7, 0:P], ROWSB[:, :], ident()).then_inc(sm_tr, 1)
            pe.wait_ge(sm_tr, 1)
            end()

            def ada_products(l, i):
                g, q = i // 4, i % 4
                w = wait_chunk(pe, first[f"ada{l}_{i}"])
                for k in range(2):
                    for c in range(4):
                        last = mm(PS[32 * c:32 * c + 32, 4 + g, :], ST[:, 2 * q + k, :],
                                  w[:, k, 512 * c:512 * c + 512], start=(q + k == 0), stop=(q == 3 and k == 1),
                                  tile_position=(0, 32 * c))
                last.then_inc(ada_mm, 1)

            def ada_between(stage, n):
                l, which = ADA_IN.get((stage, n), (0, ()))
                for i in which:
                    ada_products(l, i)

            def ada_columns(l, g):
                pe.wait_ge(mod_rows, 3 * l + g + 1)
                for j in range(4):
                    last = pe.transpose(PS[:, 4 + g, j * P:j * P + P], MOD[:, g, j * P:j * P + P], ident())
                last.then_inc(ada_tr, 1)

            evbase = [0]

            def norm(stage, n, nt0, xn):
                begin(pe, "pe", stage)
                for i in range(n):
                    pe.wait_ge(xn_ready, nt0 + i + 1)
                    if i >= 2:
                        pe.wait_ge(norm_ev, evbase[0] + i - 1)
                    for k in range(KB):
                        last = pe.transpose(PS[:, 2 * (i % 2) + k // 4, (k % 4) * P:(k % 4) * P + P],
                                            xn(i)[:, k * P:k * P + P], ident())
                    last.then_inc(norm_tr, 1)
                evbase[0] += n - 1
                pe.wait_ge(norm_tr, nt0 + n)
                end()

            begin(pe, "pe", "ada0")
            for i in range(4):
                ada_products(0, i)
            ada_columns(0, 0)
            pe.wait_ge(ada_tr, 1)
            end()
            norm("norm0", NT, 0, lambda i: XN[:, i % 2, :])

            begin(pe, "pe", "win")
            for b in range(12):
                w = wait_chunk(pe, first[f"win{b // 4}"])
                if b >= 4:
                    pe.wait_ge(cin_ready, b - 3)
                for k in range(KB):
                    last = mm(PS[:, b % 4, :], w[:, k, (b % 4) * P:(b % 4) * P + P], hT[:, k, :],
                              start=(k == 0), stop=(k == KB - 1))
                last.then_inc(win_mm, 1)
                if b % 4 == 3:
                    ada_between("win", b // 4)
            pe.wait_ge(win_mm, 12)
            end()

            begin(pe, "pe", "tok")
            for j in range(3 * NT):
                c, t = j // NT, j % NT
                n = TOKC[c][1]
                w = wait_chunk(pe, first[f"tok{c}"])
                if 4 <= j < 8:
                    pe.wait_ge(tok_z, j - 3)
                elif j >= 8:
                    pe.wait_ge(tok_ev, j - 7)
                for k in range(KB):
                    last = mm(PS[:, j % 4, 0:n], hT[:, k, t * P:t * P + P], w[:, k, :],
                              start=(k == 0), stop=(k == KB - 1))
                last.then_inc(tok_mm, 1)
                if t == NT - 1:
                    ada_between("tok", c)
            ada_columns(0, 1)
            ada_columns(0, 2)
            pe.wait_ge(ada_tr, 3)
            end()

            begin(pe, "pe", "mproj")
            pe.wait_ge(m_nrm, 1)
            for k in range(6):
                c0 = (CQ0 + P * k) if k < 3 else (CKV0 + P * (k - 3)) if k < 5 else KR0 - NOPE
                n = P if k < 5 else QD
                for t in range(NT):
                    last = pe.transpose(PS[0:n, k, t * P:t * P + P], P2[:, t, c0:c0 + n], ident())
                last.then_inc(m_tr, 1)
            pe.wait_ge(m_trev, 6)
            for j in range(2 * H_B + NT):
                if j >= 4:
                    pe.wait_ge(mproj_ev, j - 3)
                if j < H_B:
                    w = wait_chunk(pe, first["mproj"])
                    for k in range(3):
                        last = mm(PS[0:QD, j % 4, :], w[:, k, j * QD:j * QD + QD], CQT[:, k, :],
                                  start=(k == 0), stop=(k == 2))
                elif j < 2 * H_B:
                    w = wait_chunk(pe, first["mproj"] + 1)
                    h = j - H_B
                    for k in range(2):
                        last = mm(PS[0:NOPE, j % 4, :], w[:, k, h * P:h * P + NOPE], CKVT[:, k, :],
                                  start=(k == 0), stop=(k == 1))
                else:
                    t = j - 2 * H_B
                    for k in range(2):
                        wv = w[:, k, :].rearrange("p (h n) -> p h n", h=H_B)[:, :, NOPE:NOPE + DV]
                        last = mm(PS[:, j % 4, :], CKVT[:, k, t * P:t * P + P], wv, start=(k == 0), stop=(k == 1))
                last.then_inc(mproj_mm, 1)
            pe.wait_ge(mproj_ev, H_B + 1)
            for j in range(H_B + 1):
                if j >= 2:
                    pe.wait_ge(rot_ev, j - 1)
                of = QT[0:QD, j, 0:L] if j < H_B else KT[0:QD, 0, 0:L]
                mm(PS[0:QD, 4 + j % 2, 0:L], CM[0:QD, ROT, 0:QD], of, start=True, stop=True).then_inc(rot_mm, 1)
            pe.wait_ge(rot_mm, H_B + 1)
            end()

            def attention(items, base, pm, pt, scores, pv):
                for i in range(len(items) + 3):
                    if i < len(items):
                        if i >= 3:
                            pe.wait_ge(att_p, base + i - 2)
                        scores(i).then_inc(att_s, 1)
                    j = i - 2
                    if 0 <= j < len(items):
                        pe.wait_ge(att_pn, base + j + 1)
                        if j >= 2:
                            pe.wait_ge(att_pt, base + j - 1)
                        for c in range(items[j][2]):
                            last = pe.transpose(PS[:, 3 + j % 2, c * P:c * P + P], pm[:, j % 3, c * P:c * P + P], ident())
                        last.then_inc(att_tr, 1)
                    j = i - 3
                    if 0 <= j:
                        h, t, n = items[j]
                        pe.wait_ge(att_pt, base + j + 1)
                        if j >= 2:
                            pe.wait_ge(att_oe, base + j - 1)
                        r0 = 64 * (h % 2)
                        for c in range(n):
                            last = mm(PS[r0:r0 + 64, 5 + j % 2, 0:P], pv(h, c, n), pt[:, j % 2, c, :], start=(c == 0),
                                      stop=(c == n - 1))
                        last.then_inc(att_o, 1)
                pe.wait_ge(att_o, base + len(items))
                end()

            begin(pe, "pe", "matt")

            def scores(j):
                h, t, n = M_ITEMS[j]
                return mm(PS[:, j % 3, 0:n * P], QT[0:QD, h, t * P:t * P + P], KT[0:QD, h, T - n * P:T],
                          start=True, stop=True)

            attention(M_ITEMS, 0, PM, PT, scores, lambda h, i, n: VB[:, NT - n + i, h * DV:h * DV + DV])

            begin(pe, "pe", "l2")
            for b in range(8):
                pe.wait_ge(l2_sq, b + 1)
                for t in range(NT):
                    last = mm(PS[:, 0, 4 * b + t:4 * b + t + 1], SQ[:, b % 2, t * P:t * P + P], ONE[:, 0:1],
                              start=True, stop=True)
                last.then_inc(l2_ss, 1)
            pe.wait_ge(l2_r, 1)
            for b in range(8):
                if b >= 4:
                    pe.wait_ge(l2_ok, b - 3)
                for t in range(NT):
                    last = mm(PS[:, 2 + b % 4, t * P:t * P + P],
                              SS[:, 32 + 4 * b + t:33 + 4 * b + t].to_broadcast([P, P]), ident(), start=True, stop=True)
                last.then_inc(l2_bc, 1)
            pe.wait_ge(l2_ok, 8)
            for i in range(8):
                if i >= 2:
                    pe.wait_ge(l2_ev, i - 1)
                for h in range(4):
                    last = pe.transpose(PS[:, 6 + i % 2, h * P:h * P + P],
                                        qkvT[:, 4 + 4 * (i % 2) + h, (i // 2) * P:(i // 2) * P + P], ident())
                last.then_inc(l2_tr, 1)
            pe.wait_ge(l2_tr, 8)
            end()

            begin(pe, "pe", "gdn")
            hh = range(4)
            for s in range(NT):
                for d in dirs:
                    b, B, t = DIR[d], 4 * d, TILE_OF[d][s]
                    tc = slice(t * P, t * P + P)
                    upto, after = CM[:, UP if d == 0 else LO, :], CM[:, SLO if d == 0 else SUP, :]
                    pe.wait_ge(g_gU, both(d, s + 1))
                    if s:
                        pe.wait_ge(g_S, both(d, s))
                    mm(PS[:, B, :], after, b["gU"].rearrange("p h n -> p (h n)"), start=True, stop=True)
                    for h in hh:
                        last = mm(PS[:, B + 1, h * P:h * P + P], b["gU"][:, h, :], after, start=True, stop=True)
                    last.then_inc(g_seg, 1)
                    g = GB8[:, t, 0, 4 * d:4 * d + 4]
                    mm(PS[:, B + 2, 0:4], upto, g, start=True, stop=True)
                    mm(PS[:, B + 2, 4:8], after, g, start=True, stop=True)
                    mm(PS[:, B + 2, 8:12], ONE[:, :], g, start=True, stop=True).then_inc(g_sm, 1)
                    for h in hh:
                        mm(PS[:, B + 3, h * P:h * P + P], qkvT[:, 4 + h, tc], qkvT[:, 4 + h, tc], start=True, stop=True)
                for d in dirs:
                    B, t = 4 * d, TILE_OF[d][s]
                    tc = slice(t * P, t * P + P)
                    pe.wait_ge(g_exp, both(d, s + 1))
                    for h in hh:
                        last = mm(PS[:, B, h * P:h * P + P], qkvT[:, 4 + h, tc], qkvT[:, h, tc], start=True, stop=True)
                    last.then_inc(g_kk, 1)
                for d in dirs:
                    b, B = DIR[d], 4 * d
                    pe.wait_ge(g_A, both(d, s + 1))
                    for h in hh:
                        last = pe.transpose(PS[:, B, h * P:h * P + P], b["A"][:, h, :], ident())
                    last.then_inc(g_At, 1)
                for n in range(1, LEVELS):
                    at = (LEVELS - 1) * s + n
                    for d in dirs:
                        b, B = DIR[d], 4 * d
                        pe.wait_ge(g_LT, both(d, at))
                        if n == 1:
                            pe.wait_ge(g_D1, both(d, s + 1))
                            pe.wait_ge(g_eg, both(d, s + 1))
                        else:
                            pe.wait_ge(g_DE, both(d, at - 1))
                        for h in hh:
                            last = mm(PS[:, B + 1, h * P:h * P + P], b["LT"][:, h, :], b["Dm"][:, h, :],
                                      start=True, stop=True)
                        last.then_inc(g_M1, 1)
                    for d in dirs:
                        b, B = DIR[d], 4 * d
                        pe.wait_ge(g_M1e, both(d, at))
                        if n == 1:
                            pe.wait_ge(g_E1, both(d, s + 1))
                        for h in hh:
                            if n < LEVELS - 1:
                                mm(PS[:, B + 2, h * P:h * P + P], b["Em"][:, h, :], b["dec"][:, h, :],
                                   start=True, stop=True)
                            last = mm(PS[:, B + 3, h * P:h * P + P], b["dec"][:, h, :], b["Em"][:, h, :],
                                      start=True, stop=True)
                        last.then_inc(g_PQ, 1)
                for d in dirs:
                    b, B = DIR[d], 4 * d
                    pe.wait_ge(g_DE, both(d, (LEVELS - 1) * (s + 1)))
                    pe.wait_ge(g_vec, both(d, s + 1))
                    for h in hh:
                        last = mm(PS[:, B + 1, h * P:h * P + P], b["kbe"][:, h, :], b["Em"][:, h, :],
                                  start=True, stop=True)
                    last.then_inc(g_wT, 1)
                for d in dirs:
                    b, B, t = DIR[d], 4 * d, TILE_OF[d][s]
                    pe.wait_ge(g_wTe, both(d, s + 1))
                    for h in hh:
                        mm(PS[:, B, h * P:h * P + P], b["Em"][:, h, :], b["vb"][:, h, :], start=True, stop=False)
                        last = mm(PS[:, B, h * P:h * P + P], b["Dm"][:, h, :], b["S"][:, h, :], start=False, stop=True)
                    last.then_inc(g_vn, 1)
                    for h in hh:
                        mm(PS[:, B + 2, h * P:h * P + P], qkvT[:, h, t * P:t * P + P], b["S"][:, h, :],
                           start=True, stop=True)
                for d in dirs:
                    b, B = DIR[d], 4 * d
                    pe.wait_ge(g_vne, both(d, s + 1))
                    for h in hh:
                        mm(PS[:, B + 3, h * P:h * P + P], b["decT"][:, h, :], b["A"][:, h, :], start=True, stop=True)
                    for h in hh:
                        last = mm(PS[:, B + 1, h * P:h * P + P], b["kg"][:, h, :], b["A"][:, h, :],
                                  start=True, stop=True)
                    last.then_inc(g_o, 1)
            for d in dirs:
                pe.wait_ge(g_o, both(d, NT))
            end()

            begin(pe, "pe", "gout")
            for t in range(NT):
                pe.wait_ge(go_n, t + 1)
                for h in range(4):
                    last = pe.transpose(PS[:, t, h * P:h * P + P], OD[:, 0, t, h * P:h * P + P], ident())
                last.then_inc(go_tr, 1)
            pe.wait_ge(go_tr, NT)
            end()

            def gate_rows(g, c0, n):
                for r in range(n):
                    for c in range(2):
                        q = 32 * (c0 + c) + r
                        last = mm(PS[:, 4 + 2 * r + c, :], ident()[:, q:q + 1].to_broadcast([P, P]), MOD[:, g, :],
                                  start=True, stop=True)
                last.then_inc(gb_mm, 1)

            def project(stage, base, nt, lhs):
                begin(pe, "pe", stage)
                gate_rows(1, 0, nt // 2)
                for i in range(2 * nt):
                    n, t = i // nt, i % nt
                    w = wait_chunk(pe, first[stage] + n)
                    if i >= 4:
                        pe.wait_ge(out_ev, base + i - 3)
                    for k in range(KB):
                        last = mm(PS[:, i % 4, :], lhs(k, t), w[:, k, :], start=(k == 0), stop=(k == KB - 1))
                    last.then_inc(out_mm, 1)
                pe.wait_ge(out_mm, base + 2 * nt)
                end()

            project("out0", 0, NT, lambda k, t: (mixT[:, k, t * P:t * P + P] if k < 4 else YB[:, k - 4, t * P:t * P + P]))
            norm("norm1", NT, 4, lambda i: XN[:, i % 2, :])

            begin(pe, "pe", "up")
            gate_rows(2, 2, 2)
            for f in range(FF // P):
                w = wait_chunk(pe, first[f"up{f // 2}"])
                if f >= 2:
                    pe.wait_ge(up_ev, f - 1)
                for u in range(2):
                    for k in range(KB):
                        c0 = 256 * u + P * (f % 2)
                        last = mm(PS[:, 2 * (f % 2) + u, :], w[:, k, c0:c0 + P], hT[:, k, :],
                                  start=(k == 0), stop=(k == KB - 1))
                last.then_inc(up_mm, 1)
                if f == 1:
                    pe.wait_ge(gb_ready, 2)
                if f % 2:
                    ada_between("up", f // 2)
            for g in range(3):
                ada_columns(1, g)
            pe.wait_ge(ada_tr, 6)
            end()

            begin(pe, "pe", "down")
            for n in range(2):
                for c, (k0, nk) in enumerate(DOWNC):
                    w = wait_chunk(pe, first["down"] + 3 * n + c)
                    for k in range(nk):
                        for t in range(NT):
                            last = mm(PS[:, 4 * n + t, :], H2T[:, k0 + k, t * P:t * P + P], w[:, k, :],
                                      start=(k0 + k == 0), stop=(k0 + k == FF // P - 1))
                    last.then_inc(down_mm, 1)
            pe.wait_ge(down_mm, 6)
            end()

            norm("norm2", NT, 8, lambda i: XN[:, i % 2, :])

            begin(pe, "pe", "qkv")
            for i in range(24):
                w = wait_chunk(pe, first["qkv"] + i // 4)
                if i >= 4:
                    pe.wait_ge(qkv_ev[i % 2], (i - 4) // 2 + 1)
                for k in range(KB):
                    blk = slice((i % 4) * P, (i % 4) * P + P)
                    if i < 8:
                        last = mm(PS[:, i % 4, 0:L], w[:, k, blk], hT[:, k, 0:L], start=(k == 0), stop=(k == KB - 1))
                    elif i < 16:
                        last = mm(PS[:, i % 4, :], w[:, k, blk], hT[:, k, :], start=(k == 0), stop=(k == KB - 1))
                    else:
                        last = mm(PS[:, i % 4, :], hT[:, k, blk], w[:, k, :], start=(k == 0), stop=(k == KB - 1))
                last.then_inc(qkv_mm, 1)
            pe.wait_ge(qkv_mm, 24)
            end()

            begin(pe, "pe", "natt")

            def scores(j):
                h, t, n = N_ITEMS[j]
                rs = slice(64 * (h % 2), 64 * (h % 2) + 64)
                mm(PS[:, j % 3, :], QC[rs, h // 2, t * P:t * P + P], KC[rs, h // 2, :], start=True, stop=False)
                pe.wait_ge(bias_ok, j + 1)
                return mm(PS[:, j % 3, 0:L], CM[:, FLIP, :], BM[:, j % 4, :], start=False, stop=True)

            attention(N_ITEMS, len(M_ITEMS), PC, PCT, scores, lambda h, i, n: VC[:, i, h * DH:h * DH + DH])

            project("out1", 2 * NT, 2, lambda k, t: OC[:, k, t * P:t * P + P])
            norm("norm3", 2, 12, lambda i: X[:, 2 + i, :])

            begin(pe, "pe", "route")
            for t in range(2):
                for k in range(KB):
                    last = mm(PS[:, 0, 8 * t:8 * t + 8], fT[:, k, t * P:t * P + P], RW[:, k, :], start=(k == 0),
                              stop=(k == KB - 1))
            last.then_inc(rt_mm, 1)
            gate_rows(2, 2, 1)
            pe.wait_ge(rt_ev, 1)
            mm(PS[:, 1, 0:8], CM[:, SUP, :], SELM[:, 0, :], start=True, stop=True)
            mm(PS[:, 1, 8:16], CM[:, SUP, :], SELM[:, 1, :], start=True, stop=False)
            mm(PS[:, 1, 8:16], ONE[:, :], SELM[:, 0, :], start=False, stop=True)
            mm(PS[:, 1, 16:24], ONE[:, :], SELM[:, 0, :], start=True, stop=False)
            mm(PS[:, 1, 16:24], ONE[:, :], SELM[:, 1, :], start=False, stop=True).then_inc(rk_mm, 1)
            pe.wait_ge(rk_mm, 1)
            end()

            begin(pe, "pe", "moe")
            waves = pe.value_load(RI[0:1, 0:1], min_val=E, max_val=WAVES)

            def arrive(w, i):
                pe.wait_ge(arrived_e[i % RING_E], (16 * (NEC // RING_E)) * w + 16 * (i // RING_E + 1))
                return BIG[:, (i % RING_E) * SLOT:(i % RING_E) * SLOT + SLOT]

            with pe.Fori(0, waves) as w:
                more = pe.value_load(RIB[0:1, bass.ds(w, 1)], min_val=0, max_val=1)
                pe.wait_ge(e_sel, w + 1)
                for k in range(KB):
                    for t in range(2):
                        last = mm(PS[:, 4 + k // 4, (k % 4) * P:(k % 4) * P + P], X[:, 2 + t, k * P:k * P + P],
                                  SEL[:, t, :], start=(t == 0), stop=(t == 1))
                    if k % 4 == 3:
                        last.then_inc(e_gmm, 1)
                for t in range(2):
                    last = pe.transpose(PS[:, 6, t * P:t * P + P], SEL[:, 2 + t, :], ident())
                last.then_inc(e_tr, 1)

                def columns(s):
                    pe.wait_ge(e_h, NUP * w + s + 1)
                    if s >= 2:
                        pe.wait_ge(e_htev, NUP * w + s - 1)
                    for j in range(4):
                        last = pe.transpose(PS[:, 4 + s % 2, j * P:j * P + P], HE[:, s % 2, j * P:j * P + P], ident())
                    last.then_inc(e_htr, 1)

                pe.wait_ge(e_gev, 2 * w + 2)
                pe.wait_ge(e_add, 4 * w + 4)
                for s in range(NUP):
                    wgu = [arrive(w, 2 * s + u).rearrange("p (k n) -> p k n", k=KB) for u in range(2)]
                    if s >= 2:
                        pe.wait_ge(e_h, NUP * w + s - 1)

                    def gate_up(bank, c0):
                        for k in range(KB):
                            for u in range(2):
                                last = mm(PS[64 * u:64 * u + 64, bank, :], XG[:, k, c0:c0 + 64], wgu[u][:, k, :],
                                          start=(k == 0), stop=(k == KB - 1))
                        return last

                    with pe.If(more > 0):
                        gate_up(2 + s % 2, 64)
                    gate_up(s % 2, 0).then_inc(gu_mm, 1)
                    if s:
                        columns(s - 1)
                columns(NUP - 1)
                pe.wait_ge(e_trev, w + 1)
                for i in range(NDN):
                    slot_e = arrive(w, 2 * NUP + i).rearrange("p (k n) -> p k n", k=4)
                    pe.wait_ge(e_htev, NUP * w + i + 1)

                    def down(bank, c0):
                        for k in range(4):
                            for n in range(2):
                                last = mm(PS[64 * n:64 * n + 64, bank, :], HET[:, 4 * i + k, c0:c0 + 64],
                                          slot_e[:, k, 512 * n:512 * n + 512], start=(i + k == 0),
                                          stop=(i == NDN - 1 and k == 3))
                        return last

                    with pe.If(more > 0):
                        down(7, 64)
                    down(6, 0).then_inc(dn_mm, 1)
                pe.wait_ge(e_y, w + 1)
                for t in range(2):
                    for n in range(2):
                        mm(PS[:, 2 * t + n, :], SELT[:, t, :], YE[:, 0, 512 * n:512 * n + 512], start=True,
                           stop=True).then_inc(e_sc, 1)



_CONSTS = ("masks", "rope", "window")
_INS = ("x", "c", "ctx", "c_ctx", "ada_w", "ada_b", "norm_g", "ev_w_in", "ev_conv_w", "ev_a_log", "ev_dt_bias",
        "ev_gdn_norm_g", "ev_q_norm_g", "ev_w_uq", "ev_kv_norm_g", "ev_w_ukv", "ev_w_out", "ev_ffn_wg", "ev_ffn_wu",
        "ev_ffn_wd", "od_w_qkv", "od_rpb", "od_w_out", "od_router", "od_exp_wg", "od_exp_wu", "od_exp_wd",
        "final_norm_g")


def kernel(**inputs):
    import concourse.bacc as bacc
    from concourse.bass_utils import run_bass_kernel_spmd

    nc = bacc.Bacc("TRN2", target_bir_lowering=False, num_devices=1)
    arrays, A = {}, {}
    for name, a in list(zip(_CONSTS, constants())) + [(n, inputs[n]) for n in _INS]:
        a = np.ascontiguousarray(a)
        arrays[f"in_{name}"] = a
        A[name] = nc.dram_tensor(f"in_{name}", a.shape, mybir.dt.from_np(a.dtype), kind="ExternalInput").ap()
    out = nc.dram_tensor("out", (1, L, D), mybir.dt.float32, kind="ExternalOutput").ap()
    build(nc, A, out)
    r = run_bass_kernel_spmd(nc, [arrays], core_ids=[0])
    return r.results[0]["out"]
```

```python
import math
from contextlib import ExitStack

import concourse.bass as bass
import numpy as np
from concourse import mybir

P = 128
D = 1024
KB = D // P
L = 256
NT = 2 * L // P
T = 2 * L
EPS = 1e-6
H_A, DK = 4, 128
TAPS = 5
H_B, NOPE, ROPE, DV = 8, 64, 32, 64
QR, KVR = 384, 256
QD = NOPE + ROPE
H_C, DH = 16, 64
GRID_W, WIN_C, WIN_R = 64, 16, 8
RPB_R, RPB_C = 2 * WIN_R - 1, 2 * WIN_C - 1
ROWS = L // GRID_W
FF = 2816
E, FFE = 8, 3584
QKV_A = 3 * H_A * DK
Z0 = QKV_A
AB0 = Z0 + H_A * DK
IN_DIM = AB0 + 16 + QR + KVR + ROPE
REST = IN_DIM - AB0
CQ0, CKV0, KR0 = 16, 16 + QR, 16 + QR + KVR
SLOT = 4096
RING, RING_E = 3, 7
LEVELS = 7
IDENT, UP, LO, SLO, SUP, LEV, ROT, IOTA, FLIP = 0, 1, 2, 3, 4, 5, 5 + LEVELS, 6 + LEVELS, 7 + LEVELS
N_CONST = 8 + LEVELS
R_C, R_NG, R_CONV, R_QG, R_KVG = 0, 16, 48, 108, 111
WAVES = E + 3

STAGES = ["prep", "ada0", "norm0", "win", "tok", "mproj", "matt", "l2", "gdn", "gout", "out0", "norm1", "up",
          "down", "norm2", "qkv", "natt", "out1", "norm3", "route", "moe", "final"]
WORKS = {
    "pe": set(STAGES) - {"moe", "final"},
    "act": set(STAGES) - {"final"},
    "dve": set(STAGES) - {"moe", "final"},
    "pool": {"prep", "gdn", "natt"},
}


def constants():
    i = np.arange(P)
    m = np.zeros((P, N_CONST, P), np.float32)
    r, c = i[:, None], i[None, :]
    m[:, IDENT] = r == c
    m[:, UP] = r <= c
    m[:, LO] = r >= c
    m[:, SLO] = r > c
    m[:, SUP] = r < c
    for n in range(LEVELS):
        m[:, LEV + n] = (r >> (n + 1) == c >> (n + 1)) & (r >> n != c >> n)
    q = ROPE // 4
    for a in range(q):
        for half in (0, 2 * q):
            m[NOPE + half + q + a, ROT, NOPE + half + a] = -1.0
            m[NOPE + half + a, ROT, NOPE + half + q + a] = 1.0
    m[:, IOTA] = c
    m[:, FLIP] = ((r // GRID_W == c // GRID_W) & (r % GRID_W == GRID_W - 1 - c % GRID_W)) * float(DH) ** 0.5
    t = np.arange(L)
    inv = np.float32(10000.0) ** (-np.arange(0, ROPE // 2, 2, dtype=np.float32) / np.float32(ROPE // 2))
    ar = (t // GRID_W).astype(np.float32)[:, None] * inv[None]
    ac = (t % GRID_W).astype(np.float32)[:, None] * inv[None]
    ang = np.concatenate([ar, ar, ac, ac], axis=-1)
    rope = np.stack([np.cos(ang).T, np.sin(ang).T], axis=1).astype(np.float32)
    col = GRID_W - 1 - i % GRID_W
    first = np.clip(col - WIN_C // 2, 0, GRID_W - WIN_C)[:, None]
    key = np.arange(GRID_W)[None]
    window = np.where((key >= first) & (key < first + WIN_C), 0.0, -1e30).astype(np.float32)
    return m.reshape(P, -1), rope, window


def build(nc, A, out):
    f32, i32, f32r = mybir.dt.float32, mybir.dt.int32, mybir.dt.float32r
    ALU, ACT, AX = mybir.AluOpType, mybir.ActivationFunctionType, mybir.AxisListType

    ctx = ExitStack()
    with ctx:
        parts_of = {}

        def sb(name, shape, dt=f32, parts=()):
            at = -(-nc.sbuf_base // 32) * 32
            t = ctx.enter_context(nc.sbuf_tensor(name, shape, dt))
            parts_of[name] = [(a, b, nc.alloc_sbuf_tensor_at(f"{name}_parts{a}", [P, b - a], f32r, offset=at + 4 * a))
                              for a, b in parts]
            return t

        def sem(name):
            return ctx.enter_context(nc.semaphore(name))

        BIG = sb("BIG", [P, RING_E * SLOT],
                 parts=[(i * SLOT, (i + 1) * SLOT) for i in range(RING)] + [(RING * SLOT, RING_E * SLOT)])
        HB = sb("HB", [P, KB * T], parts=[(0, KB * T)])
        QB = sb("QB", [P, 12 * T], parts=[(0, KB * T)])
        X = sb("X", [P, NT, D])
        ZS = sb("ZS", [P, NT, 512], parts=[(0, NT * 512)])
        YB = sb("YB", [P, 4, T], parts=[(0, 4 * T)])
        CM = sb("CM", [P, N_CONST, P])
        CS = sb("CS", [P, 2, L])
        WM = sb("WM", [P, GRID_W])
        MOD = sb("MOD", [P, 3, 512])
        MT = sb("MT", [P, 3, 4, 4, 2])
        AB = sb("AB", [P, 2, 2, 2, KB])
        ROWSB = sb("ROWSB", [P, P])
        SM = sb("SM", [P, P])
        ST = sb("ST", [P, KB, 32])
        DTB = sb("DTB", [P, 2, 8])
        GG = sb("GG", [P, P])
        ONE = sb("ONE", [P, P])
        SS = sb("SS", [P, 64])
        RT = sb("RT", [P, 64])
        GB8 = sb("GB8", [P, NT, 3, 8])
        EG = sb("EG", [P, 2, 12])
        RW = sb("RW", [P, KB, E])
        EPSC = sb("EPSC", [P, 2])
        EA = sb("EA", [P, 1, 8])
        SELM = sb("SELM", [P, 2, E])
        WR = sb("WR", [P, 2, WAVES])
        WG = sb("WG", [P, 2, WAVES])
        RF = sb("RF", [P, 4])
        RI = sb("RI", [P, 4], i32)
        RFB = sb("RFB", [P, WAVES])
        RIB = sb("RIB", [P, WAVES], i32)

        hT = HB[:, :].rearrange("p (k t) -> p k t", t=T)
        qkvT = QB[:, :].rearrange("p (b t) -> p b t", t=T)
        mixT = QB[:, 0:KB * T].rearrange("p (b t) -> p b t", t=T)
        XN = QB[:, 0:2 * D].rearrange("p (a n) -> p a n", a=2)
        GB = QB[:, KB * T:KB * T + 2 * D].rearrange("p (r n) -> p r n", r=2)
        AR = BIG[:, RING * SLOT:]

        class Cut:
            def __init__(self, region, at=0):
                self.region, self.at = region, at

            def __call__(self, *shape):
                n = int(np.prod(shape))
                v = self.region[:, self.at:self.at + n]
                self.at += n
                if len(shape) == 2:
                    v = v.rearrange("p (a b) -> p a b", a=shape[0])
                if len(shape) == 3:
                    v = v.rearrange("p (a b c) -> p a b c", a=shape[0], b=shape[1])
                return v

        cut = Cut(AR, (RING_E - RING) * SLOT - 3 * 512)
        BADD = cut(3, 512)
        cut = Cut(AR)
        CIN = cut(2, 2, L + TAPS - 1)
        CACC = cut(2, T)
        cut = Cut(AR)
        P2 = cut(NT, REST)
        CQT = cut(3, T)
        CKVT = cut(2, T)
        QT = cut(H_B, T)
        KT = cut(H_B, T)
        VB = cut(NT, H_B * DV)
        cut = Cut(HB)
        PM = cut(3, T)
        PT = cut(2, 4, P)
        RTMP = cut(2, L)
        cut = Cut(AR)
        KTOK = cut(NT, 4 * DK)
        VTOK = cut(NT, 4 * DK)
        DIR = [{n: cut(4, P) for n in ("gU", "dec", "decT", "A", "AT", "Dm", "Em", "kbe", "kg", "vb", "S", "LT")}
               for _ in range(2)]
        OD = HB[:, :].rearrange("p (d t n) -> p d t n", d=2, t=NT)
        SQ = HB[:, 0:2 * T].rearrange("p (a t) -> p a t", a=2)
        cut = Cut(AR)
        H2T = cut(FF // P, T)
        SG = cut(2, T)
        HHIGH = cut(2, 2, T)
        cut = Cut(AR)
        QC = cut(KB, L)
        KC = cut(KB, T)
        VC = cut(NT, D)
        PC = cut(3, T)
        PCT = cut(2, 4, P)
        BM = cut(4, L)
        OC = HB[:, 0:KB * L].rearrange("p (k t) -> p k t", t=L)
        cut = Cut(QB)
        XG = cut(KB, P)
        HE = cut(2, 512)
        HET = cut(FFE // P, P)
        SEB = [QB[:, cut.at:cut.at + 512], ZS[:, 3, :]]
        cut = Cut(HB, KB * L)
        SE = cut(2, 512)
        YE = cut(1, D)
        fT = HB[:, 0:KB * L].rearrange("p (k t) -> p k t", t=L)
        SEL = ZS[:, 0, :].rearrange("p (a b) -> p a b", a=4)
        SELT = ZS[:, 1, 0:2 * P].rearrange("p (a b) -> p a b", a=2)
        RTB = ZS[:, 2, :]
        FG = YB[:, 0:2, :].rearrange("p a b -> p (a b)")
        GE = YB[:, 2:4, :].rearrange("p a b -> p (a b)")
        ACC = HB[:, 0:2 * D].rearrange("p (t n) -> p t n", t=2)

        WH = {"win": AR[:, 4096:4096 + SLOT], "up": QB[:, 0:SLOT], "qkv": AR[:, 10240:10240 + SLOT]}
        win_high = AR[:, 8192:8192 + KB * T].rearrange("p (a k t) -> p a k t", a=2, t=T)
        HIGH = {"win": [win_high[:, a] for a in range(2)], "up": [ZS[:, :, :], YB[:, :, :]]}

        def r12(ap):
            first_, end_, t = next(r for r in parts_of[ap.tensor.name] if r[0] <= ap.offset < r[1])
            return bass.AP(tensor=t, offset=ap.offset - first_, ap=[[end_ - first_, P]] + [list(d) for d in ap.ap[1:]])

        TILE_OF = [[2, 3, 0, 1], [3, 2, 1, 0]]
        M_ITEMS = [(h, t, 4 if t < 2 else 2) for h in range(H_B) for t in range(NT)]
        N_ITEMS = [(h, t, 4) for h in range(H_C) for t in range(2)]

        PS = ctx.enter_context(nc.psum_tensor("PS", [P, 8, 512], f32))

        done = {e: sem(f"{e}_stage_done") for e in WORKS}

        def qkv_place(i):
            if i < 8:
                return QC[:, i, :], PS[:, i % 4, 0:L]
            if i < 16:
                return KC[:, i - 8, :], PS[:, i % 4, :]
            return VC[:, i % 4, 512 * (i // 20):512 * (i // 20) + 512], PS[:, i % 4, :]

        def begin(eng, me, stage):
            for e in WORKS:
                n = sum(s in WORKS[e] for s in STAGES[:STAGES.index(stage)])
                if e != me and n:
                    eng.wait_ge(done[e], n)

        arrived = [sem(f"weights_arrived{i}") for i in range(RING)]
        arrived_e = [sem(f"expert_weights_arrived{i}") for i in range(RING_E)]
        ada_mm, win_mm, tok_mm, mproj_mm = sem("ada_mm"), sem("win_mm"), sem("tok_mm"), sem("mproj_mm")
        out_mm, up_mm, down_mm, qkv_mm = sem("out_mm"), sem("up_mm"), sem("down_mm"), sem("qkv_mm")
        stream = []

        def by_rows(w, r0, nb, c0, nc_):
            return w[r0:r0 + nb * P, c0:c0 + nc_].rearrange("(k p) n -> p k n", p=P)

        first = {}

        def chunk(key, shape, source, free):
            first.setdefault(key, len(stream))
            stream.append((shape, source, free))

        def ada_chunk(l, i):
            g, q = i // 4, i % 4
            chunk(f"ada{l}_{i}", (2, 2048), by_rows(A["ada_w"][l], 256 * q, 2, 2048 * g, 2048), (ada_mm, 12 * l + i + 1))

        ADA_IN = {("win", 0): (0, (4,)), ("win", 1): (0, (5,)), ("win", 2): (0, (6,)), ("tok", 0): (0, (7,)),
                  ("tok", 1): (0, (8,)), ("tok", 2): (0, (9, 10, 11))}
        ADA_IN |= {("up", n): (1, (n + 1,)) for n in range(-1, FF // 256)}

        def ada_between(stage, n):
            l, which = ADA_IN.get((stage, n), (0, ()))
            for i in which:
                ada_chunk(l, i)

        for i in range(4):
            ada_chunk(0, i)
        w_in = A["ev_w_in"][0]
        for c in range(3):
            chunk(f"win{c}", (KB, 512), by_rows(w_in, 0, KB, 512 * c, 512), (win_mm, 4 * c + 4))
            ada_between("win", c)
        TOKC = [(Z0, 512), (AB0, REST // 2), (AB0 + REST // 2, REST // 2)]
        for c, (c0, n) in enumerate(TOKC):
            chunk(f"tok{c}", (KB, n), by_rows(w_in, 0, KB, c0, n), (tok_mm, 4 * c + 4))
            ada_between("tok", c)
        chunk("mproj", (3, H_B * QD), by_rows(A["ev_w_uq"][0], 0, 3, 0, H_B * QD), (mproj_mm, H_B))
        chunk("mproj", (2, H_B * 128), by_rows(A["ev_w_ukv"][0], 0, 2, 0, H_B * 128), (mproj_mm, 2 * H_B + NT))
        for n in range(2):
            chunk("out0", (KB, 512), by_rows(A["ev_w_out"][0], 0, KB, 512 * n, 512), (out_mm, 4 * n + 4))
        ada_between("up", -1)
        for s in range(FF // 256):
            chunk(f"up{s}", None, (by_rows(A["ev_ffn_wg"][0], 0, KB, 256 * s, 256),
                               by_rows(A["ev_ffn_wu"][0], 0, KB, 256 * s, 256)), (up_mm, 2 * s + 2))
            ada_between("up", s)
        NDOWN = FF // P // 2
        for c in range(0, NDOWN, 2):
            nk = min(4, 2 * (NDOWN - c))
            chunk("down", (nk, D), by_rows(A["ev_ffn_wd"][0], 2 * c * P, nk, 0, D),
                  (down_mm, c + 2 if c + 2 < NDOWN else NDOWN + 7))
        for c in range(6):
            chunk("qkv", (KB, 512), by_rows(A["od_w_qkv"][0], 0, KB, 512 * c, 512), (qkv_mm, 4 * c + 4))
        for n in range(2):
            chunk("out1", (KB, 512), by_rows(A["od_w_out"][0], 0, KB, 512 * n, 512), (out_mm, 8 + 2 * n + 2))

        def slot(i, shape):
            v = BIG[:, (i % RING) * SLOT:(i % RING) * SLOT + shape[0] * shape[1]]
            return v.rearrange("p (k n) -> p k n", k=shape[0])

        loads_before = [0] * RING
        counts = []
        for i, (shape, source, _) in enumerate(stream):
            loads_before[i % RING] += 1 if shape else 2
            counts.append(16 * loads_before[i % RING])

        def wait_chunk(eng, i):
            eng.wait_ge(arrived[i % RING], counts[i])
            return slot(i, stream[i][0] or (KB, 512))

        half_mm, split_h, split_l, norm_high = sem("half_chunk_mm"), sem("weights_high"), sem("weights_low"), sem("norm_high")
        units, unit_of = [], {}
        halves = [0]

        def unit(key, stage, at, c, view, free):
            unit_of[key] = len(units)
            w = view(slot(c, stream[c][0] or (KB, 512)))
            high = WH[stage][:, (at % 2) * (SLOT // 2):(at % 2) * (SLOT // 2) + int(np.prod(w.shape[1:]))]
            if len(w.shape) == 4:
                high = high.rearrange("p (k u n) -> p k u n", k=w.shape[1], u=w.shape[2])
            else:
                high = high.rearrange("p (k n) -> p k n", k=w.shape[1])
            before = units[-2][-1] if at >= (3 if stage == "up" else 2) else None
            units.append((c, w, high, before, free))

        def unit_halves(key, stage, at, c, free):
            halves[0] += 1
            unit((key, 0), stage, at, c, lambda w: w[:, 0:4, :], (half_mm, halves[0]))
            unit((key, 1), stage, at + 1, c, lambda w: w[:, 4:8, :], free)

        for j in range(6):
            unit(("win", j), "win", j, first[f"win{j // 2}"], lambda w: w[:, :, 256 * (j % 2):256 * (j % 2) + 256],
                 (win_mm, 2 * j + 2))
        for c in range(3):
            unit_halves(f"tok{c}", "win", 6 + 2 * c, first[f"tok{c}"], (tok_mm, 4 * c + 4))
        for n in range(2):
            unit_halves(f"out0{n}", "win", 2 * n, first["out0"] + n, (out_mm, 4 * n + 4))
        for f in range(FF // P):
            unit(("up", f), "up", f + 1, first[f"up{f // 2}"],
                 lambda w: w.rearrange("p k (u f n) -> p k u f n", u=2, f=2)[:, :, :, f % 2, :], (up_mm, f + 1))
        for j in range(NDOWN):
            unit(("down", j), "up", FF // P + 1 + j, first["down"] + j // 2, lambda w: w[:, 2 * (j % 2):2 * (j % 2) + 2, :],
                 (down_mm, j + 1 if j + 1 < NDOWN else NDOWN + 7))
        for j in range(8):
            unit(("qkv", j), "qkv", j, first["qkv"] + j // 2, lambda w: w[:, :, 256 * (j % 2):256 * (j % 2) + 256],
                 (qkv_mm, 2 * j + 2))
        for c in (4, 5):
            unit_halves(f"qkv{c}", "qkv", 2 * c, first["qkv"] + c, (qkv_mm, 4 * c + 4))

        def unit_parts(eng, key):
            u = unit_of[key]
            eng.wait_ge(split_l, u + 1)
            _, w, high, _, _ = units[u]
            return r12(high), r12(w)

        NUP, NDN = FFE // 512, FFE // 512
        NEC = 2 * NUP + NDN
        assert NEC % RING_E == 0
        gu_mm, dn_mm = sem("gate_up_mm"), sem("expert_down_mm")

        s_const, s_rows, s_x, s_bias, s_misc = (sem(n) for n in ("const_in", "rows_in", "x_in", "ada_b_in", "misc_in"))
        rows_zero, st_zero = sem("rows_zeroed"), sem("padding_zeroed")
        sm_tr, sm_cols = sem("small_transposed"), sem("small_columns")
        mod_rows, ada_tr, gb_mm = sem("mod_rows"), sem("ada_transposed"), sem("gate_rows_mm")
        norm_sd, norm_rstd, xn_ready, norm_tr, norm_ev = (sem(n) for n in (
            "norm_sd", "norm_rstd", "xn_ready", "norm_transposed", "norm_evacuated"))
        cin_ready, conv_done = sem("conv_input"), sem("conv_done")
        tok_ev = sem("tok_evacuated")
        dve_seq, act_seq, pool_seq = sem("dve_seq"), sem("act_seq"), sem("pool_seq")
        m_sd, m_nrm, m_tr, m_trev = (sem(n) for n in ("mla_sd", "mla_normed", "mla_transposed",
                                                              "mla_latents"))
        mproj_ev, rot_mm, rot_ev = sem("mproj_evacuated"), sem("rot_mm"), sem("rope_done")
        att_s, att_max, att_p, att_pn, att_tr, att_pt, att_o, att_oe = (sem(n) for n in (
            "scores_mm", "scores_max", "probs_ready", "probs_normed", "probs_transposed", "probs_t_ready", "pv_mm",
            "pv_evacuated"))
        bias_in, bias_ok = [sem(f"rpb_in{i}") for i in range(4)], sem("bias_masked")
        l2_sq, l2_ss, l2_sd, l2_r, l2_bc, l2_ok, l2_tr, l2_ev = (sem(n) for n in (
            "l2_squares", "l2_sums", "l2_sd", "l2_rstd", "l2_broadcast", "l2_scaled", "kv_transposed", "kv_tokens"))
        dirs = range(2)

        def both(d, n):
            return 2 * (n - 1) + d + 1

        g_gU, g_seg, g_exp, g_msk, g_kk, g_A, g_At, g_AT, g_D1, g_E1 = (sem(n) for n in (
            "gU", "seg_mm", "decay", "decay_masked", "kk_mm", "A_ready", "A_transposed", "AT_ready", "inverse1", "inverse1_t"))
        g_LT, g_M1, g_M1e, g_PQ, g_DE, g_eg, g_sm, g_vec, g_wT, g_wTe, g_vn, g_vne, g_o, g_S = (sem(n) for n in (
            "level_masked", "M1_mm", "M1_ready", "update_mm", "inverse", "sums_exp", "sums_mm", "kbe_kg_vb", "wT_mm",
            "wT_ready", "vnew_mm", "vnew_ready", "o_mm", "S_ready"))
        gb_ready, go_tr, go_ev, go_sd, go_n = (sem(n) for n in ("gate_rows_ready", "o_transposed", "o_columns", "o_sd",
                                                                "o_gated"))
        o_high, o_low = sem("mixed_high"), sem("mixed_low")
        h2_high, h2_low = sem("hidden_high"), sem("hidden_low")
        out_ev = sem("out_added")
        up_silu, up_ev = sem("up_silu"), sem("up_ready")
        down_ev = sem("down_added")
        qkv_ev = [sem(f"qkv_evacuated{i}") for i in range(2)]
        rt_mm, rt_ev, rk_mm, rt_tab = (sem(n) for n in ("router_mm", "router_read", "rank_mm",
                                                              "wave_tables"))
        e_sel, e_gmm, e_gev, e_tr, e_trev = (sem(n) for n in ("sel_ready", "gather_mm", "gathered", "sel_transposed",
                                                             "sel_t_ready"))
        e_silu, e_h, e_htr, e_htev, e_y, e_sc, e_add, e_zero = (sem(n) for n in (
            "expert_silu", "expert_h", "h_transposed", "h_columns", "y_ready", "scatter_mm", "scatter_added", "hidden_cleared"))
        s_out = sem("out_stored")
        go_sum, gz_ready = sem("o_sum"), sem("z_by_gain")
        bias_zero, cin_zero, conv_ev, tok_z = sem("ada_b_zeroed"), sem("conv_padding_zeroed"), sem("conv_evacuated"), sem("z_ready")
        sp_in, sp_ln, s_fg = sem("softplus_in"), sem("softplus_ln"), sem("final_gain_in")
        ge_ready, rt_d, rt_e, fin_x = sem("expert_gate_rows"), sem("logit_difference"), sem("logit_exp"), sem("final_x")
        fin_sd, fin_ok = sem("final_sd"), sem("final_ready")

        block = ctx.enter_context(nc.Block())

        @block.sync
        def _(sp):
            for i, (shape, source, _) in enumerate(stream):
                if i >= RING:
                    sp.wait_ge(*stream[i - RING][2])
                if shape:
                    sp.dma_start(slot(i, shape), source).then_inc(arrived[i % RING], 16)
                else:
                    for half in range(2):
                        sp.dma_start(slot(i, (KB, 512))[:, :, 256 * half:256 * half + 256],
                                     source[half]).then_inc(arrived[i % RING], 16)

            begin(sp, None, "natt")
            rpb = A["od_rpb"]
            for j in range(2 * H_C):
                h, qt = j // 2, j % 2
                if j >= 4:
                    sp.wait_ge(att_s, len(M_ITEMS) + j - 3)
                for r in range(2):
                    at = h * RPB_R * RPB_C + (WIN_R - 1 - (2 * qt + r)) * RPB_C + WIN_C - GRID_W
                    src = bass.AP(tensor=rpb.tensor, offset=at, ap=[[1, GRID_W], [RPB_C, ROWS], [1, GRID_W]])
                    sp.dma_start(BM[64 * r:64 * r + 64, j % 4, :].rearrange("p (a b) -> p a b", a=ROWS),
                                 src).then_inc(bias_in[j % 4], 16)

            wg, wu = (A[n].rearrange("o e (k p) n -> (o e) p k n", p=P) for n in ("od_exp_wg", "od_exp_wu"))
            wd = A["od_exp_wd"].rearrange("o e (k p) n -> (o e) p k n", p=P)

            def wave_loads(w, e, first):
                for i in range(NEC):
                    if i >= RING_E:
                        j = i - RING_E
                        if j < 2 * NUP:
                            sp.wait_ge(gu_mm, NUP * w + j // 2 + 1)
                        else:
                            sp.wait_ge(dn_mm, NDN * w + j - 2 * NUP + 1)
                    elif first and i == RING:
                        begin(sp, None, "out1")
                    elif first and i < RING:
                        sp.wait_ge(*stream[-RING:][(i - len(stream)) % RING][2])
                    elif not first:
                        sp.wait_ge(dn_mm, NDN * w + i - RING_E + 1)
                    dst = BIG[:, (i % RING_E) * SLOT:(i % RING_E) * SLOT + SLOT]
                    if i < 2 * NUP:
                        src = (wg, wu)[i % 2][e, :, :, 512 * (i // 2):512 * (i // 2) + 512]
                        sp.dma_start(dst.rearrange("p (k n) -> p k n", k=KB), src).then_inc(arrived_e[i % RING_E], 16)
                    else:
                        j = 4 * (i - 2 * NUP)
                        sp.dma_start(dst.rearrange("p (k n) -> p k n", k=4),
                                     wd[e, :, j:j + 4, :]).then_inc(arrived_e[i % RING_E], 16)

            wave_loads(0, 0, True)
            with sp.Fori(1, E) as w:
                wave_loads(w, w, False)
            sp.wait_ge(rt_tab, 2)
            waves = sp.value_load(RI[0:1, 0:1], min_val=E, max_val=WAVES)
            with sp.If(waves > E):
                with sp.Fori(E, waves) as w:
                    e = sp.value_load(RI[0:1, bass.ds(w - E + 1, 1)], min_val=0, max_val=E - 1)
                    wave_loads(w, e, False)

            sp.wait_ge(fin_ok, 2)
            sp.dma_start(out[0].rearrange("(t p) n -> p t n", p=P), X[:, 0:2, :]).then_inc(s_out, 16)
            sp.wait_ge(s_out, 16)

        @block.gpsimd
        def _(pool):
            def seq(ins, count=[0]):
                count[0] += 1
                ins.then_inc(pool_seq, 1)
                pool.wait_ge(pool_seq, count[0])

            pool.memset(ROWSB[:, :], 0.0).then_inc(rows_zero, 1)
            pool.memset(ST[:, :, :], 0.0).then_inc(st_zero, 1)
            pool.memset(ONE[:, :], 1.0).then_inc(done["pool"], 1)

            def make_low(keys):
                for key in keys:
                    u = unit_of[key]
                    _, w, high, _, _ = units[u]
                    pool.wait_ge(split_h, u + 1)
                    pool.tensor_tensor(r12(w), w, r12(high), ALU.subtract).then_inc(split_l, 1)

            make_low([("win", j) for j in range(6)] + [(f"tok{c}", h) for c in range(3) for h in range(2)])

            begin(pool, "pool", "gdn")

            def heads(m):
                return CM[:, m, :].rearrange("p (a b) -> p a b", a=1).to_broadcast([P, 4, P])

            def gU(s, d):
                b, t = DIR[d], TILE_OF[d][s]
                if s:
                    pool.wait_ge(g_seg, both(d, s))
                for h in range(4):
                    last = pool.tensor_scalar(b["gU"][:, h, :], CM[:, UP if d == 0 else LO, :],
                                              GB8[:, t, 0, 4 * d + h:4 * d + h + 1], None, ALU.mult)
                last.then_inc(g_gU, 1)

            for d in dirs:
                gU(0, d)
            for s in range(NT):
                for d in dirs:
                    b = DIR[d]
                    pool.wait_ge(g_exp, both(d, s + 1))
                    pool.tensor_tensor(b["dec"], b["dec"], heads(SLO if d == 0 else SUP), ALU.mult)
                    pool.tensor_tensor(b["decT"], b["decT"], heads(UP if d == 0 else LO), ALU.mult).then_inc(g_msk, 1)
                for d in dirs:
                    b = DIR[d]
                    pool.wait_ge(g_A, both(d, s + 1))
                    if s:
                        pool.wait_ge(g_vn, both(d, s))
                    seq(pool.tensor_tensor(b["Dm"], b["A"], heads(LEV), ALU.mult))
                    pool.tensor_tensor(b["Dm"], heads(IDENT), b["Dm"], ALU.subtract).then_inc(g_D1, 1)
                for n in range(1, LEVELS):
                    for d in dirs:
                        b = DIR[d]
                        if n == 1:
                            pool.wait_ge(g_AT, both(d, s + 1))
                            if s:
                                pool.wait_ge(g_M1, both(d, (LEVELS - 1) * s))
                        else:
                            pool.wait_ge(g_M1, both(d, (LEVELS - 1) * s + n - 1))
                        pool.tensor_tensor(b["LT"], b["AT"], heads(LEV + n), ALU.mult).then_inc(g_LT, 1)
                for d in dirs:
                    if s + 1 < NT:
                        gU(s + 1, d)
            gain = GG[:, :].rearrange("p (a n) -> p a n", a=1).to_broadcast([P, 4, P])
            for t in range(NT):
                z = ZS[:, t, :].rearrange("p (h n) -> p h n", h=4)
                pool.tensor_tensor(z, z, gain, ALU.mult).then_inc(gz_ready, 1)
            pool.wait_ge(gz_ready, NT)
            pool.wait_ge(g_LT, both(1, (LEVELS - 1) * NT))
            pool.nop().then_inc(done["pool"], 1)

            make_low([(f"out0{n}", half) for n in range(2) for half in range(2)])
            make_low([("up", f) for f in range(FF // P)] + [("down", j) for j in range(NDOWN)] +
                     [("qkv", j) for j in range(8)] +
                     [(f"qkv{c}", h) for c in (4, 5) for h in range(2)])

            begin(pool, "pool", "natt")
            for j in range(2 * H_C):
                pool.wait_ge(bias_in[j % 4], 32 * (j // 4 + 1))
                v = BM[:, j % 4, :].rearrange("p (a b) -> p a b", a=ROWS)
                m = WM[:, :].rearrange("p (a b) -> p a b", a=1).to_broadcast([P, ROWS, GRID_W])
                pool.tensor_tensor(v, v, m, ALU.add).then_inc(bias_ok, 1)
            pool.wait_ge(bias_ok, 2 * H_C)
            pool.nop().then_inc(done["pool"], 1)

        @block.scalar
        def _(act):
            def seq(ins, count=[0]):
                count[0] += 1
                ins.then_inc(act_seq, 1)
                act.wait_ge(act_seq, count[0])

            def everywhere(ap, n):
                return bass.AP(tensor=ap.tensor, offset=0, ap=[[0, P], [1, n]])

            def load_ada_b(l):
                rows = A["ada_b"][l:l + 1, :].rearrange("o (g c n) -> o g c n", g=3, c=4)
                for c in range(4):
                    for r in range(2):
                        act.dma_start(BADD[32 * c + r:32 * c + r + 1, :, :], rows[:, :, c, :]).then_inc(s_bias, 16)

            def squares(n, sem, value, bank):
                for i in range(n):
                    act.wait_ge(sem, value(i))
                    seq(act.activation(PS[:, bank:bank + 2, :].rearrange("p a b -> p (a b)"), X[:, i, :], ACT.Square,
                                       accum_out=SS[:, i:i + 1]))
                act.activation(SS[:, 8:8 + n], SS[:, 0:n], ACT.Sqrt, bias=EPSC[:, 0:1], scale=1.0 / D).then_inc(norm_sd, 1)

            act.wait_ge(rows_zero, 1)
            act.dma_start(ROWSB[0:KB, :], A["c"].rearrange("o (k n) -> (o k) n", n=P)).then_inc(s_rows, 16)
            act.dma_start(ROWSB[KB:2 * KB, :], A["c_ctx"].rearrange("(k n) -> k n", n=P)).then_inc(s_rows, 16)
            act.dma_start(ROWSB[R_NG:R_NG + 4 * KB, :],
                          A["norm_g"].rearrange("l w (k n) -> (l w k) n", n=P)).then_inc(s_rows, 16)
            act.dma_start(ROWSB[R_CONV:R_CONV + 12 * TAPS, :],
                          A["ev_conv_w"].rearrange("o j (b n) -> (o j b) n", n=P)).then_inc(s_rows, 16)
            act.dma_start(ROWSB[R_QG:R_QG + 3, :],
                          A["ev_q_norm_g"].rearrange("o (k n) -> (o k) n", n=P)).then_inc(s_rows, 16)
            act.dma_start(ROWSB[R_KVG:R_KVG + 2, :],
                          A["ev_kv_norm_g"].rearrange("o (k n) -> (o k) n", n=P)).then_inc(s_rows, 16)
            act.dma_start(CM[:, :, :].rearrange("p a b -> p (a b)"), A["masks"]).then_inc(s_const, 16)
            act.dma_start(X[:, 0:2, :], A["x"][0].rearrange("(t p) n -> p t n", p=P)).then_inc(s_x, 16)
            act.dma_start(X[:, 2:4, :], A["ctx"][0].rearrange("(t p) n -> p t n", p=P)).then_inc(s_x, 16)
            act.dma_start(CS[NOPE:NOPE + ROPE, :, :], A["rope"]).then_inc(s_misc, 16)
            act.dma_start(WM[:, :], A["window"]).then_inc(s_misc, 16)
            act.dma_start(DTB[:, 0, :], everywhere(A["ev_dt_bias"], 8)).then_inc(s_misc, 16)
            act.dma_start(DTB[:, 1, :], everywhere(A["ev_a_log"], 8)).then_inc(s_misc, 16)
            act.dma_start(GG[:, :], everywhere(A["ev_gdn_norm_g"], P)).then_inc(s_misc, 16)
            act.dma_start(RW[:, :, :], A["od_router"][0].rearrange("(k p) n -> p k n", p=P)).then_inc(s_misc, 16)
            act.wait_ge(st_zero, 1)
            act.wait_ge(bias_zero, 1)
            load_ada_b(0)
            squares(NT, s_x, lambda i: 32, 0)
            act.wait_ge(sm_cols, 1)
            act.activation(ST[:, :, 0:2], SM[:, 0:2 * KB].rearrange("p (r k) -> p k r", r=2),
                           ACT.Silu).then_inc(done["act"], 1)

            def x_high(i, nt0, nxt):
                act.wait_ge(norm_ev, nt0 + i + 1)
                tile = slice(i * P, i * P + P)
                for a, high in enumerate(HIGH["win" if nxt == "win" else "up"]):
                    act.activation(r12(high[:, :, tile]), hT[:, 4 * a:4 * a + 4, tile], ACT.Copy).then_inc(norm_high, 1)

            def make_high(*key):
                u = unit_of[key]
                c, w, high, before, _ = units[u]
                wait_chunk(act, c)
                if before:
                    act.wait_ge(*before)
                act.activation(r12(high), w, ACT.Copy).then_inc(split_h, 1)

            def norm(stage, n, nt0, xn, nxt=None):
                begin(act, "act", stage)
                act.wait_ge(norm_rstd, ("norm0", "norm1", "norm2", "norm3").index(stage) + 1)
                for i in range(n):
                    if i >= 2:
                        act.wait_ge(norm_tr, nt0 + i - 1)
                    act.activation(xn(i), X[:, i, :], ACT.Copy, scale=SS[:, 16 + i:17 + i]).then_inc(xn_ready, 1)
                    if nxt and i == 1:
                        make_high(nxt, 0)
                    if nxt and i >= 2:
                        x_high(i - 2, nt0, nxt)
                if nxt:
                    x_high(n - 2, nt0, nxt)
                    x_high(n - 1, nt0, nxt)
                    act.wait_ge(norm_high, 2 * (nt0 + n))
                act.wait_ge(xn_ready, nt0 + n)
                act.nop().then_inc(done["act"], 1)

            act.wait_ge(s_misc, 96)
            act.activation(EA[:, :], DTB[:, 1, :], ACT.Exp).then_inc(done["act"], 1)

            norm("norm0", NT, 0, lambda i: XN[:, i % 2, :], "win")

            begin(act, "act", "win")
            act.wait_ge(cin_zero, 1)

            def conv_in(b):
                act.wait_ge(win_mm, b + 1)
                if b >= 2:
                    act.wait_ge(conv_done, b - 1)
                act.activation(CIN[:, b % 2, :, 2:2 + L], PS[:, b % 4, :].rearrange("p (a t) -> p a t", a=2),
                               ACT.Copy).then_inc(cin_ready, 1)

            def conv_out(b):
                act.wait_ge(conv_done, b + 1)
                return act.activation(qkvT[:, b, :], CACC[:, b % 2, :], ACT.Silu)

            make_high("win", 1)
            conv_in(0)
            for b in range(12):
                if b < 11:
                    conv_in(b + 1)
                if b % 2 == 0:
                    j = b // 2 + 2
                    make_high(*(("win", j) if j < 6 else ("tok0", j - 6)))
                conv_out(b).then_inc(conv_ev if b < 11 else done["act"], 1)

            begin(act, "act", "tok")
            make_high("tok1", 0)
            for t in range(NT):
                act.wait_ge(tok_mm, t + 1)
                act.activation(ZS[:, t, :], PS[:, t % 4, :], ACT.Silu).then_inc(tok_z, 1)
            make_high("tok1", 1)
            make_high("tok2", 0)
            make_high("tok2", 1)
            act.wait_ge(tok_z, NT)
            act.nop().then_inc(done["act"], 1)

            begin(act, "act", "mproj")
            for t in range(NT):
                seq(act.activation(PM[:, 0, 0:QR], P2[:, t, CQ0:CQ0 + QR], ACT.Square, accum_out=SS[:, t:t + 1]))
                seq(act.activation(PM[:, 0, 0:KVR], P2[:, t, CKV0:CKV0 + KVR], ACT.Square,
                                   accum_out=SS[:, 4 + t:5 + t]))
            act.activation(SS[:, 8:12], SS[:, 0:4], ACT.Sqrt, bias=EPSC[:, 0:1], scale=1.0 / QR).then_inc(m_sd, 1)
            act.activation(SS[:, 12:16], SS[:, 4:8], ACT.Sqrt, bias=EPSC[:, 0:1], scale=1.0 / KVR).then_inc(m_sd, 1)
            act.wait_ge(sp_in, 1)
            seq(act.activation(GB8[:, :, 0, :], GB8[:, :, 2, :], ACT.Abs))
            seq(act.activation(GB8[:, :, 0, :], GB8[:, :, 0, :], ACT.Exp, scale=-1.0))
            act.activation(GB8[:, :, 0, :], GB8[:, :, 0, :], ACT.Ln, bias=ONE[:, 0:1]).then_inc(sp_ln, 1)
            act.activation(GB8[:, :, 1, :], P2[:, :, 8:16], ACT.Sigmoid).then_inc(sp_ln, 1)
            for j in range(2 * H_B + NT):
                act.wait_ge(mproj_mm, j + 1)
                if j < H_B:
                    to, of = QT[0:QD, j, :], PS[0:QD, j % 4, :]
                elif j < 2 * H_B:
                    to, of = KT[0:NOPE, j - H_B, :], PS[0:NOPE, j % 4, :]
                else:
                    to, of = VB[:, j - 2 * H_B, :], PS[:, j % 4, :]
                act.activation(to, of, ACT.Copy).then_inc(mproj_ev, 1)
            act.wait_ge(mproj_ev, 2 * H_B + NT)
            act.nop().then_inc(done["act"], 1)

            def attention(items, base, pm, pt, scale):
                def exp(j):
                    n = items[j][2]
                    act.wait_ge(att_max, base + j + 1)
                    if j >= 3:
                        act.wait_ge(att_tr, base + j - 2)
                    act.activation(pm[:, j % 3, 0:n * P], PS[:, j % 3, 0:n * P], ACT.Exp, bias=RT[:, j % 4:j % 4 + 1],
                                   scale=scale, accum_out=RT[:, 8 + j % 4:9 + j % 4]).then_inc(att_p, 1)

                for i in range(len(items) + 2):
                    if i < len(items):
                        exp(i)
                    j = i - 2
                    if j < 0:
                        continue
                    act.wait_ge(att_tr, base + j + 1)
                    if j >= 2:
                        act.wait_ge(att_o, base + j - 1)
                    n = items[j][2]
                    act.activation(pt[:, j % 2, 0:n, :],
                                   PS[:, 3 + j % 2, 0:n * P].rearrange("p (a b) -> p a b", a=n),
                                   ACT.Copy).then_inc(att_pt, 1)
                act.wait_ge(att_pt, base + len(items))
                act.nop().then_inc(done["act"], 1)

            begin(act, "act", "matt")
            attention(M_ITEMS, 0, PM, PT, QD ** -0.5)

            begin(act, "act", "l2")
            for b in range(8):
                if b >= 2:
                    act.wait_ge(l2_ss, b - 1)
                act.activation(SQ[:, b % 2, :], qkvT[:, b, :], ACT.Square).then_inc(l2_sq, 1)
            act.wait_ge(l2_ss, 8)
            act.activation(SS[:, 0:16], PS[:, 0, 0:16], ACT.Sqrt, bias=EPSC[:, 1:2], scale=float(DK)).then_inc(l2_sd, 1)
            act.activation(SS[:, 16:32], PS[:, 0, 16:32], ACT.Sqrt, bias=EPSC[:, 0:1]).then_inc(l2_sd, 1)
            for i in range(8):
                act.wait_ge(l2_tr, i + 1)
                act.activation((KTOK, VTOK)[i % 2][:, i // 2, :], PS[:, 6 + i % 2, :], ACT.Copy).then_inc(l2_ev, 1)
            act.wait_ge(l2_ev, 8)
            act.nop().then_inc(done["act"], 1)

            begin(act, "act", "gdn")
            for s in range(NT):
                for d in dirs:
                    b, B = DIR[d], 4 * d
                    act.wait_ge(g_seg, both(d, s + 1))
                    act.activation(b["decT"], PS[:, B, :], ACT.Exp)
                    act.activation(b["dec"], PS[:, B + 1, :], ACT.Exp).then_inc(g_exp, 1)
                    act.wait_ge(g_sm, both(d, s + 1))
                    act.activation(EG[:, d, :], PS[:, B + 2, 0:12], ACT.Exp).then_inc(g_eg, 1)
                for d in dirs:
                    b, B = DIR[d], 4 * d
                    act.wait_ge(g_At, both(d, s + 1))
                    act.activation(b["AT"], PS[:, B, :], ACT.Copy).then_inc(g_AT, 1)
                for n in range(1, LEVELS):
                    for d in dirs:
                        b, B = DIR[d], 4 * d
                        act.wait_ge(g_M1, both(d, (LEVELS - 1) * s + n))
                        act.activation(b["dec"], PS[:, B + 1, :], ACT.Copy).then_inc(g_M1e, 1)
                for d in dirs:
                    b, B = DIR[d], 4 * d
                    act.wait_ge(g_wT, both(d, s + 1))
                    act.activation(b["Dm"], PS[:, B + 1, :], ACT.Copy, scale=-1.0).then_inc(g_wTe, 1)
                for d in dirs:
                    b, B = DIR[d], 4 * d
                    act.wait_ge(g_vn, both(d, s + 1))
                    act.activation(b["A"], PS[:, B, :], ACT.Copy).then_inc(g_vne, 1)
            for d in dirs:
                act.wait_ge(g_vne, both(d, NT))
            act.nop().then_inc(done["act"], 1)

            begin(act, "act", "gout")
            for t in range(NT):
                act.wait_ge(go_sum, t + 1)
                for h in range(4):
                    seq(act.activation(PS[:, 4, 0:DK], OD[:, 0, t, h * DK:h * DK + DK], ACT.Square,
                                       accum_out=SS[:, 4 * t + h:4 * t + h + 1]))
            act.activation(SS[:, 16:32], SS[:, 0:16], ACT.Sqrt, bias=EPSC[:, 0:1], scale=1.0 / DK).then_inc(go_sd, 1)
            for t in range(NT):
                act.wait_ge(go_tr, t + 1)
                last = act.activation(mixT[:, 0:4, t * P:t * P + P], PS[:, t, :].rearrange("p (h n) -> p h n", h=4),
                                      ACT.Copy)
                last.then_inc(go_ev, 1)
                if t == 0:
                    make_high("out00", 0)
            for t in range(NT):
                tile = slice(t * P, t * P + P)
                act.wait_ge(go_ev, t + 1)
                act.activation(r12(HIGH["win"][0][:, :, tile]), mixT[:, 0:4, tile], ACT.Copy).then_inc(o_high, 1)
            act.activation(r12(HIGH["win"][1]), YB[:, :, :], ACT.Copy).then_inc(o_high, 1)
            make_high("out00", 1)
            act.wait_ge(o_high, NT + 1)
            act.nop().then_inc(done["act"], 1)

            def gate_rows(stage, k, to, n):
                begin(act, "act", stage)
                act.wait_ge(gb_mm, k + 1)
                for r in range(n):
                    for c in range(2):
                        last = act.activation(to[:, r, 512 * c:512 * c + 512], PS[:, 4 + 2 * r + c, :], ACT.Copy)
                last.then_inc(gb_ready, 1)
                act.wait_ge(gb_ready, k + 1)

            gate_rows("out0", 0, GB, 2)
            for half in range(2):
                make_high("out01", half)
            squares(NT, out_ev, lambda i: NT + i + 1, 4)
            act.nop().then_inc(done["act"], 1)
            norm("norm1", NT, 4, lambda i: XN[:, i % 2, :], "up")

            gate_rows("up", 1, GB, 2)
            make_high("up", 1)
            act.wait_ge(bias_zero, 2)
            load_ada_b(1)
            for f in range(FF // P):
                act.wait_ge(up_mm, f + 1)
                if f >= 2:
                    act.wait_ge(up_ev, f - 1)
                act.activation(SG[:, f % 2, :], PS[:, 2 * (f % 2), :], ACT.Silu).then_inc(up_silu, 1)
                if f + 2 < FF // P:
                    make_high("up", f + 2)

            def hidden_high(j):
                act.wait_ge(up_ev, 2 * j + 2)
                if j >= 2:
                    act.wait_ge(down_mm, j - 1)
                act.activation(r12(HHIGH[:, j % 2]), H2T[:, 2 * j:2 * j + 2, :], ACT.Copy).then_inc(h2_high, 1)

            for j in range(2):
                make_high("down", j)
                hidden_high(j)
            act.wait_ge(h2_high, 2)
            act.wait_ge(up_silu, FF // P)
            act.nop().then_inc(done["act"], 1)

            begin(act, "act", "down")
            for j in range(2, NDOWN):
                make_high("down", j)
                hidden_high(j)
            squares(NT, down_ev, lambda i: NT + i + 1, 0)
            act.nop().then_inc(done["act"], 1)

            norm("norm2", NT, 8, lambda i: XN[:, i % 2, :], "qkv")

            begin(act, "act", "qkv")
            make_high("qkv", 1)
            after = {2 * j: [("qkv", j + 2)] for j in range(6)}
            after |= {12: [("qkv4", 0)], 14: [("qkv4", 1), ("qkv5", 0)], 18: [("qkv5", 1)]}
            for i in range(0, 24, 2):
                act.wait_ge(qkv_mm, i + 1)
                to, of = qkv_place(i)
                act.activation(to, of, ACT.Copy).then_inc(qkv_ev[0], 1)
                for key in after.get(i, ()):
                    make_high(*key)
            act.wait_ge(qkv_ev[0], 12)
            act.nop().then_inc(done["act"], 1)

            begin(act, "act", "natt")
            act.dma_start(FG, everywhere(A["final_norm_g"], D)).then_inc(s_fg, 16)
            attention(N_ITEMS, len(M_ITEMS), PC, PCT, DH ** -0.5)

            gate_rows("out1", 2, GB, 1)
            squares(2, out_ev, lambda i: 2 * NT + 2 + i + 1, 6)
            act.nop().then_inc(done["act"], 1)
            norm("norm3", 2, 12, lambda i: X[:, 2 + i, :])

            begin(act, "act", "route")
            act.wait_ge(gb_mm, 4)
            for c in range(2):
                last = act.activation(GE[:, 512 * c:512 * c + 512], PS[:, 4 + c, :], ACT.Copy)
            last.then_inc(ge_ready, 1)
            act.wait_ge(rt_d, 1)
            act.activation(RTB[:, 80:82], RTB[:, 82:84], ACT.Exp).then_inc(rt_e, 1)
            act.wait_ge(rt_e, 1)
            act.wait_ge(ge_ready, 1)
            act.nop().then_inc(done["act"], 1)

            begin(act, "act", "moe")
            act.wait_ge(e_zero, 1)
            waves = act.value_load(RI[0:1, 0:1], min_val=E, max_val=WAVES)
            with act.Fori(0, waves) as w:
                more = act.value_load(RIB[0:1, bass.ds(w, 1)], min_val=0, max_val=1)
                act.wait_ge(e_tr, w + 1)
                act.activation(SELT, PS[:, 6, 0:2 * P].rearrange("p (a b) -> p a b", a=2), ACT.Copy).then_inc(e_trev, 1)

                def silu(s):
                    act.wait_ge(gu_mm, NUP * w + s + 1)
                    if s >= 2:
                        act.wait_ge(e_h, NUP * w + s - 1)
                    act.activation(SEB[s % 2][64:P, :], PS[0:64, 2 + s % 2, :], ACT.Silu)
                    act.activation(SE[64:P, s % 2, :], PS[0:64, s % 2, :], ACT.Silu).then_inc(e_silu, 1)

                silu(0)
                for s in range(NUP):
                    if s < NUP - 1:
                        silu(s + 1)
                    act.wait_ge(e_htr, NUP * w + s + 1)
                    act.activation(HET[:, 4 * s:4 * s + 4, :], PS[:, 4 + s % 2, :].rearrange("p (a b) -> p a b", a=4),
                                   ACT.Copy).then_inc(e_htev, 1)
                act.wait_ge(rt_tab, 2)
                act.wait_ge(dn_mm, NDN * w + NDN)

                def take_y(bank, r0):
                    for n in range(2):
                        last = act.activation(YE[r0:r0 + 64, 0, 512 * n:512 * n + 512],
                                              PS[64 * n:64 * n + 64, bank, :], ACT.Copy)
                    return last

                with act.If(more > 0):
                    take_y(7, 64)
                take_y(6, 0).then_inc(e_y, 1)
            act.nop().then_inc(done["act"], 1)

            act.wait_ge(fin_x, 2)
            for i in range(2):
                seq(act.activation(QB[:, 0:D], X[:, i, :], ACT.Square, accum_out=SS[:, i:i + 1]))
            act.activation(SS[:, 8:10], SS[:, 0:2], ACT.Sqrt, bias=EPSC[:, 0:1], scale=1.0 / D).then_inc(fin_sd, 1)

        @block.vector
        def _(dve):
            def seq(ins, count=[0]):
                count[0] += 1
                ins.then_inc(dve_seq, 1)
                dve.wait_ge(dve_seq, count[0])

            def end(ins):
                ins.then_inc(done["dve"], 1)

            dve.memset(EPSC[:, 0:1], EPS)
            dve.memset(EPSC[:, 1:2], EPS * DK)
            dve.memset(BADD, 0.0).then_inc(bias_zero, 1)
            dve.wait_ge(sm_tr, 1)
            dve.tensor_copy(SM[:, :], PS[:, 7, 0:P]).then_inc(sm_cols, 1)
            dve.wait_ge(sm_cols, 1)
            dve.nop().then_inc(done["dve"], 1)

            def ada_rows(l, g):
                dve.wait_ge(ada_mm, 12 * l + 4 * g + 4)
                dve.tensor_tensor(MOD[:, g, :], PS[:, 4 + g, :], BADD[:, g, :], ALU.add).then_inc(mod_rows, 1)

            def ada_columns(l, g):
                dve.wait_ge(ada_tr, 3 * l + g + 1)
                v = PS[:, 4 + g, :].rearrange("p (j c q) -> p j c q", j=4, c=4)
                seq(dve.tensor_copy(MT[:, g, :, :, :], v[:, :, :, 0:2]))

            def ada_norm(l, which):
                sh, sc = ((0, 0), (0, 2)) if which == 0 else ((1, 2), (2, 0))
                ng = SM[:, R_NG + (2 * l + which) * KB:R_NG + (2 * l + which + 1) * KB]
                for r in range(2):
                    for c in range(2):
                        to = slice(4 * c, 4 * c + 4)
                        dve.scalar_tensor_tensor(AB[:, which, r, 0, to], MT[:, sc[0], :, sc[1] + c, r], 1.0,
                                                 ng[:, to], ALU.add, ALU.mult)
                        last = dve.tensor_copy(AB[:, which, r, 1, to], MT[:, sh[0], :, sh[1] + c, r])
                return last

            def x_low(i, nt0, high):
                tile = slice(i * P, i * P + P)
                for a in range(2):
                    dve.wait_ge(norm_high, 2 * (nt0 + i) + a + 1)
                    v = hT[:, 4 * a:4 * a + 4, tile]
                    last = dve.tensor_tensor(r12(v), v, r12(high[a][:, :, tile]), ALU.subtract)
                if i == NT - 1:
                    seq(last)

            def norm(stage, n, nt0, l, which, dst, high=None):
                idx = ("norm0", "norm1", "norm2", "norm3").index(stage)
                begin(dve, "dve", stage)
                dve.wait_ge(norm_sd, idx + 1)
                dve.reciprocal(SS[:, 16:16 + n], SS[:, 8:8 + n]).then_inc(norm_rstd, 1)
                for i in range(n):
                    dve.wait_ge(norm_tr, nt0 + i + 1)
                    for k in range(KB):
                        r = i // 2
                        last = dve.tensor_scalar(dst[:, k, i * P:i * P + P],
                                                 PS[:, 2 * (i % 2) + k // 4, (k % 4) * P:(k % 4) * P + P],
                                                 AB[:, which, r, 0, k:k + 1], AB[:, which, r, 1, k:k + 1],
                                                 ALU.mult, ALU.add)
                    last.then_inc(norm_ev, 1)
                    if high and i:
                        x_low(i - 1, nt0, high)
                if high:
                    x_low(n - 1, nt0, high)
                dve.wait_ge(norm_ev, nt0 + n)
                dve.nop().then_inc(done["dve"], 1)

            begin(dve, "dve", "ada0")
            dve.wait_ge(s_bias, 128)
            ada_rows(0, 0)
            ada_columns(0, 0)
            end(ada_norm(0, 0))
            norm("norm0", NT, 0, 0, 0, hT, HIGH["win"])

            begin(dve, "dve", "win")
            dve.memset(CIN, 0.0).then_inc(cin_zero, 1)
            for b in range(12):
                dve.wait_ge(cin_ready, b + 1)
                if b >= 2:
                    dve.wait_ge(conv_ev, b - 1)
                acc = CACC[:, b % 2, :].rearrange("p (a t) -> p a t", a=2)
                for j in range(TAPS):
                    w = SM[:, R_CONV + 12 * j + b:R_CONV + 12 * j + b + 1]
                    of = CIN[:, b % 2, :, j:j + L]
                    if j == 0:
                        seq(dve.tensor_scalar(acc, of, w, None, ALU.mult))
                    else:
                        ins = dve.scalar_tensor_tensor(acc, of, w, acc, ALU.mult, ALU.add)
                        if j < TAPS - 1:
                            seq(ins)
                ins.then_inc(conv_done, 1)
            dve.wait_ge(conv_done, 12)
            dve.nop().then_inc(done["dve"], 1)

            begin(dve, "dve", "tok")
            for j in range(NT, 3 * NT):
                dve.wait_ge(tok_mm, j + 1)
                c, t = j // NT - 1, j % NT
                dve.tensor_copy(P2[:, t, c * (REST // 2):(c + 1) * (REST // 2)],
                                PS[:, j % 4, 0:REST // 2]).then_inc(tok_ev, 1)
            for g in (1, 2):
                ada_rows(0, g)
            for g in (1, 2):
                ada_columns(0, g)
            end(ada_norm(0, 1))

            begin(dve, "dve", "mproj")
            dve.wait_ge(s_misc, 96)
            dt = DTB[:, 0:1, :].to_broadcast([P, NT, 8])
            dve.tensor_tensor(GB8[:, :, 2, :], P2[:, :, 0:8], dt, ALU.add).then_inc(sp_in, 1)
            dve.wait_ge(m_sd, 2)
            seq(dve.reciprocal(SS[:, 16:24], SS[:, 8:16]))
            for t in range(NT):
                v = P2[:, t, CQ0:CQ0 + QR]
                dve.tensor_scalar(v, v, SS[:, 16 + t:17 + t], None, ALU.mult)
                v = P2[:, t, CKV0:CKV0 + KVR]
                last = dve.tensor_scalar(v, v, SS[:, 20 + t:21 + t], None, ALU.mult)
            last.then_inc(m_nrm, 1)
            for k in range(3):
                dve.wait_ge(m_tr, k + 1)
                dve.tensor_scalar(CQT[:, k, :], PS[:, k, :], SM[:, R_QG + k:R_QG + k + 1], None,
                                  ALU.mult).then_inc(m_trev, 1)
            for k in range(2):
                dve.wait_ge(m_tr, k + 4)
                dve.tensor_scalar(CKVT[:, k, :], PS[:, 3 + k, :], SM[:, R_KVG + k:R_KVG + k + 1], None,
                                  ALU.mult).then_inc(m_trev, 1)
            dve.wait_ge(m_tr, 6)
            dve.tensor_copy(KT[NOPE:QD, 0, :], PS[NOPE:QD, 5, :]).then_inc(m_trev, 1)
            dve.wait_ge(sp_ln, 2)
            seq(dve.scalar_tensor_tensor(GB8[:, :, 2, :], GB8[:, :, 2, :], 0.0, GB8[:, :, 0, :], ALU.max, ALU.add))
            ea = EA[:, 0:1, :].to_broadcast([P, NT, 8])
            seq(dve.scalar_tensor_tensor(GB8[:, :, 0, :], GB8[:, :, 2, :], -1.0, ea, ALU.mult, ALU.mult))
            rs = slice(NOPE, QD)
            for j in range(H_B + 1):
                dve.wait_ge(rot_mm, j + 1)
                v = (QT[rs, j, 0:L] if j < H_B else KT[rs, 0, 0:L])
                seq(dve.tensor_tensor(RTMP[rs, j % 2, :], PS[rs, 4 + j % 2, 0:L], CS[rs, 1, :], ALU.mult))
                seq(dve.tensor_tensor(v, v, CS[rs, 0, :], ALU.mult))
                ins = dve.tensor_tensor(v, v, RTMP[rs, j % 2, :], ALU.add)
                ins.then_inc(rot_ev, 1)
            dve.wait_ge(rot_ev, H_B + 1)
            for h in range(1, H_B):
                last = dve.tensor_copy(KT[rs, h, :], KT[rs, 0, :])
            end(last)

            def attention(items, base, pm, out_of, scale):
                def largest(j):
                    n = items[j][2]
                    dve.wait_ge(att_s, base + j + 1)
                    seq(dve.tensor_reduce(RT[:, 4 + j % 4:5 + j % 4], PS[:, j % 3, 0:n * P], AX.X, ALU.max))
                    dve.tensor_scalar(RT[:, j % 4:j % 4 + 1], RT[:, 4 + j % 4:5 + j % 4], -scale, None,
                                      ALU.mult).then_inc(att_max, 1)

                def normalise(j):
                    dve.wait_ge(att_p, base + j + 1)
                    seq(dve.reciprocal(RT[:, 12 + j % 4:13 + j % 4], RT[:, 8 + j % 4:9 + j % 4]))
                    v = pm[:, j % 3, 0:items[j][2] * P]
                    dve.tensor_scalar(v, v, RT[:, 12 + j % 4:13 + j % 4], None, ALU.mult).then_inc(att_pn, 1)

                def take_out(j):
                    dve.wait_ge(att_o, base + j + 1)
                    r0 = 64 * (items[j][0] % 2)
                    dve.tensor_copy(out_of(j), PS[r0:r0 + 64, 5 + j % 2, 0:P]).then_inc(att_oe, 1)

                for i in range(len(items) + 4):
                    if i < len(items):
                        largest(i)
                    if 0 <= i - 1 < len(items):
                        normalise(i - 1)
                    if i - 4 >= 0:
                        take_out(i - 4)
                dve.wait_ge(att_oe, base + len(items))
                dve.nop().then_inc(done["dve"], 1)

            begin(dve, "dve", "matt")

            def out_of(j):
                h, t, _ = M_ITEMS[j]
                return YB[64 * (h % 2):64 * (h % 2) + 64, h // 2, t * P:t * P + P]

            attention(M_ITEMS, 0, PM, out_of, QD ** -0.5)

            begin(dve, "dve", "l2")
            for d in dirs:
                dve.memset(DIR[d]["S"], 0.0)
            dve.wait_ge(l2_sd, 2)
            dve.reciprocal(SS[:, 32:64], SS[:, 0:32]).then_inc(l2_r, 1)
            for b in range(8):
                dve.wait_ge(l2_bc, b + 1)
                dve.tensor_tensor(qkvT[:, b, :], qkvT[:, b, :], PS[:, 2 + b % 4, :], ALU.mult).then_inc(l2_ok, 1)
            dve.wait_ge(l2_ok, 8)
            dve.nop().then_inc(done["dve"], 1)

            begin(dve, "dve", "gdn")

            def heads(m):
                return CM[:, m, :].rearrange("p (a b) -> p a b", a=1).to_broadcast([P, 4, P])

            def vectors(s, d):
                b, t = DIR[d], TILE_OF[d][s]
                dve.wait_ge(g_eg, both(d, s + 1))
                be = RT[:, 8 + 4 * d:12 + 4 * d]
                seq(dve.tensor_tensor(be, GB8[:, t, 1, 4 * d:4 * d + 4], EG[:, d, 0:4], ALU.mult))
                for h in range(4):
                    kk, vv = KTOK[:, t, h * DK:h * DK + DK], VTOK[:, t, h * DK:h * DK + DK]
                    dve.tensor_scalar(b["kbe"][:, h, :], kk, be[:, h:h + 1], None, ALU.mult)
                    dve.tensor_scalar(b["kg"][:, h, :], kk, EG[:, d, 4 + h:5 + h], None, ALU.mult)
                    last = dve.tensor_scalar(b["vb"][:, h, :], vv, GB8[:, t, 1, 4 * d + h:4 * d + h + 1], None,
                                             ALU.mult)
                last.then_inc(g_vec, 1)

            for s in range(NT):
                for d in dirs:
                    b, B, t = DIR[d], 4 * d, TILE_OF[d][s]
                    dve.wait_ge(g_kk, both(d, s + 1))
                    dve.wait_ge(g_msk, both(d, s + 1))
                    for h in range(4):
                        beta = GB8[:, t, 1, 4 * d + h:4 * d + h + 1]
                        dve.scalar_tensor_tensor(b["A"][:, h, :], PS[:, B + 3, h * P:h * P + P], beta,
                                                 b["dec"][:, h, :], ALU.mult, ALU.mult)
                    dve.tensor_tensor(b["decT"], PS[:, B, :].rearrange("p (h n) -> p h n", h=4), b["decT"],
                                      ALU.mult).then_inc(g_A, 1)
                for d in dirs:
                    b = DIR[d]
                    dve.wait_ge(g_AT, both(d, s + 1))
                    seq(dve.tensor_tensor(b["Em"], b["AT"], heads(LEV), ALU.mult))
                    dve.tensor_tensor(b["Em"], heads(IDENT), b["Em"], ALU.subtract).then_inc(g_E1, 1)
                for n in range(1, LEVELS):
                    for d in dirs:
                        b, B = DIR[d], 4 * d
                        dve.wait_ge(g_PQ, both(d, (LEVELS - 1) * s + n))
                        if n < LEVELS - 1:
                            dve.tensor_tensor(b["Dm"], b["Dm"], PS[:, B + 2, :].rearrange("p (h n) -> p h n", h=4),
                                              ALU.subtract)
                        dve.tensor_tensor(b["Em"], b["Em"], PS[:, B + 3, :].rearrange("p (h n) -> p h n", h=4),
                                          ALU.subtract).then_inc(g_DE, 1)
                    if n <= 2:
                        vectors(s, n - 1)
                for d in dirs:
                    b, B, t = DIR[d], 4 * d, TILE_OF[d][s]
                    dve.wait_ge(g_o, both(d, s + 1))
                    seq(dve.tensor_copy(OD[:, d, t, :], PS[:, B + 3, :]))
                    for h in range(4):
                        hs = slice(h * DK, h * DK + DK)
                        dve.scalar_tensor_tensor(OD[:, d, t, hs], PS[:, B + 2, hs], EG[:, d, h:h + 1],
                                                 OD[:, d, t, hs], ALU.mult, ALU.add)
                        last = dve.scalar_tensor_tensor(b["S"][:, h, :], b["S"][:, h, :], EG[:, d, 8 + h:9 + h],
                                                        PS[:, B + 1, hs], ALU.mult, ALU.add)
                    last.then_inc(g_S, 1)
            for d in dirs:
                dve.wait_ge(g_S, both(d, NT))
            dve.nop().then_inc(done["dve"], 1)

            begin(dve, "dve", "gout")
            for t in range(NT):
                dve.tensor_tensor(OD[:, 0, t, :], OD[:, 0, t, :], OD[:, 1, t, :], ALU.add).then_inc(go_sum, 1)
            dve.wait_ge(go_sd, 1)
            seq(dve.reciprocal(SS[:, 32:48], SS[:, 16:32]))
            for t in range(NT):
                for h in range(4):
                    hs = slice(h * DK, h * DK + DK)
                    last = dve.scalar_tensor_tensor(OD[:, 0, t, hs], OD[:, 0, t, hs],
                                                    SS[:, 32 + 4 * t + h:33 + 4 * t + h], ZS[:, t, hs], ALU.mult, ALU.mult)
                last.then_inc(go_n, 1)
            for t in range(NT + 1):
                dve.wait_ge(o_high, t + 1)
                v, high = (mixT[:, 0:4, t * P:t * P + P], HIGH["win"][0][:, :, t * P:t * P + P]) if t < NT else \
                    (YB[:, :, :], HIGH["win"][1])
                dve.tensor_tensor(r12(v), v, r12(high), ALU.subtract).then_inc(o_low, 1)
            dve.wait_ge(o_low, NT + 1)
            dve.nop().then_inc(done["dve"], 1)

            def add_out(stage, base, nt):
                begin(dve, "dve", stage)
                dve.wait_ge(gb_ready, 1 if stage == "out0" else 3)
                for i in range(2 * nt):
                    n, t = i // nt, i % nt
                    cols = slice(512 * n, 512 * n + 512)
                    dve.wait_ge(out_mm, base + i + 1)
                    seq(dve.tensor_tensor(ZS[:, i % 2, :], PS[:, i % 4, :], GB[:, t // 2, cols], ALU.mult))
                    dve.tensor_tensor(X[:, t, cols], X[:, t, cols], ZS[:, i % 2, :], ALU.add).then_inc(out_ev, 1)
                dve.wait_ge(out_ev, base + 2 * nt)
                dve.nop().then_inc(done["dve"], 1)

            add_out("out0", 0, NT)
            norm("norm1", NT, 4, 0, 1, hT, HIGH["up"])

            begin(dve, "dve", "up")
            dve.memset(BADD, 0.0).then_inc(bias_zero, 1)
            for f in range(FF // P):
                dve.wait_ge(up_silu, f + 1)
                dve.tensor_tensor(H2T[:, f, :], SG[:, f % 2, :], PS[:, 2 * (f % 2) + 1, :], ALU.mult).then_inc(up_ev, 1)

            def hidden_low(j):
                dve.wait_ge(h2_high, j + 1)
                v = H2T[:, 2 * j:2 * j + 2, :]
                dve.tensor_tensor(r12(v), v, r12(HHIGH[:, j % 2]), ALU.subtract).then_inc(h2_low, 1)

            for j in range(2):
                hidden_low(j)
            dve.wait_ge(s_bias, 256)
            for g in range(3):
                ada_rows(1, g)
            for g in range(3):
                ada_columns(1, g)
            ada_norm(1, 0)
            end(ada_norm(1, 1))

            begin(dve, "dve", "down")
            for j in range(2, NDOWN):
                hidden_low(j)
            for n in range(2):
                for t in range(NT):
                    dve.wait_ge(down_mm, NDOWN + NT * n + t)
                    cols = slice(512 * n, 512 * n + 512)
                    seq(dve.tensor_tensor(ZS[:, t % 2, :], PS[:, 4 * n + t, :], GB[:, t // 2, cols], ALU.mult))
                    dve.tensor_tensor(X[:, t, cols], X[:, t, cols], ZS[:, t % 2, :], ALU.add).then_inc(down_ev, 1)
            dve.wait_ge(down_ev, 2 * NT)
            dve.nop().then_inc(done["dve"], 1)

            norm("norm2", NT, 8, 1, 0, hT, HIGH["up"])

            begin(dve, "dve", "qkv")
            for i in range(1, 24, 2):
                dve.wait_ge(qkv_mm, i + 1)
                to, of = qkv_place(i)
                dve.tensor_copy(to, of).then_inc(qkv_ev[1], 1)
            dve.wait_ge(qkv_ev[1], 12)
            dve.nop().then_inc(done["dve"], 1)

            begin(dve, "dve", "natt")

            def out_of(j):
                h, t, _ = N_ITEMS[j]
                return OC[64 * (h % 2):64 * (h % 2) + 64, h // 2, t * P:t * P + P]

            attention(N_ITEMS, len(M_ITEMS), PC, out_of, DH ** -0.5)

            add_out("out1", 2 * NT, 2)
            norm("norm3", 2, 12, 1, 1, fT)

            begin(dve, "dve", "route")

            def r8(at, n=2):
                return RTB[:, at:at + 8 * n].rearrange("p (t e) -> p t e", t=n)

            LG, PK1, PK2, TMP, WT, PRIO = r8(0), r8(16), r8(32), r8(48), r8(64), RTB[:, 96:104]
            M1, M2 = RTB[:, 84:86], RTB[:, 86:88]
            dve.wait_ge(rt_mm, 1)
            seq(dve.tensor_copy(LG, PS[:, 0, 0:16].rearrange("p (t e) -> p t e", t=2)))
            seq(dve.tensor_scalar(PRIO, CM[:, IOTA, 0:8], -1.0, 8.0, ALU.mult, ALU.add))

            def pick(mx, pk):
                seq(dve.tensor_reduce(mx, LG, AX.X, ALU.max))
                for t in range(2):
                    seq(dve.scalar_tensor_tensor(TMP[:, t, :], LG[:, t, :], mx[:, t:t + 1], PRIO, ALU.is_equal, ALU.mult))
                seq(dve.tensor_reduce(RTB[:, 88:90], TMP, AX.X, ALU.max))
                for t in range(2):
                    seq(dve.tensor_scalar(pk[:, t, :], TMP[:, t, :], RTB[:, 88 + t:89 + t], None, ALU.is_equal))

            pick(M1, PK1)
            seq(dve.scalar_tensor_tensor(LG, PK1, -3e38, LG, ALU.mult, ALU.add))
            pick(M2, PK2)
            dve.tensor_tensor(RTB[:, 82:84], M2, M1, ALU.subtract).then_inc(rt_d, 1)
            seq(dve.tensor_tensor(SELM[:, :, :], PK1, PK2, ALU.add))
            dve.nop().then_inc(rt_ev, 1)
            dve.wait_ge(rt_e, 1)
            G1, G2 = RTB[:, 90:92], RTB[:, 92:94]
            seq(dve.tensor_scalar(G1, RTB[:, 80:82], 1.0, None, ALU.add))
            seq(dve.reciprocal(G1, G1))
            seq(dve.tensor_tensor(G2, G1, RTB[:, 80:82], ALU.mult))
            for t in range(2):
                seq(dve.tensor_scalar(TMP[:, t, :], PK1[:, t, :], G1[:, t:t + 1], None, ALU.mult))
                seq(dve.scalar_tensor_tensor(WT[:, t, :], PK2[:, t, :], G2[:, t:t + 1], TMP[:, t, :], ALU.mult, ALU.add))
            dve.wait_ge(rk_mm, 1)
            RK = r8(0)
            for t in range(2):
                seq(dve.scalar_tensor_tensor(RK[:, t, :], PS[:, 1, 8 * t:8 * t + 8], 1.0, SELM[:, t, :], ALU.add,
                                             ALU.mult))
            seq(dve.tensor_scalar(RK, RK, -1.0, None, ALU.add))
            OV, ORD = RTB[:, 104:112], RTB[:, 112:120]
            seq(dve.tensor_scalar(OV, PS[:, 1, 16:24], float(P), None, ALU.is_gt))
            seq(dve.memset(ORD, 0.0))
            for e in range(1, E):
                seq(dve.tensor_tensor(ORD[:, e:e + 1], ORD[:, e - 1:e], OV[:, e - 1:e], ALU.add))
            for t in range(2):
                dve.tensor_copy(WR[:, t, 0:E], RK[:, t, :])
                dve.tensor_copy(WG[:, t, 0:E], WT[:, t, :])
            seq(dve.tensor_reduce(RF[:, 0:1], OV, AX.X, ALU.add))
            seq(dve.tensor_scalar(RF[:, 0:1], RF[:, 0:1], float(E), None, ALU.add))
            J = WAVES - E

            def by_expert(at):
                return RTB[:, at:at + 8 * J].rearrange("p (j e) -> p j e", j=J)

            def each(v):
                return v.rearrange("p (a e) -> p a e", a=1).to_broadcast([P, J, E])

            OH, EX, PR, PG = by_expert(128), by_expert(152), [by_expert(176 + 24 * t) for t in range(2)], \
                [by_expert(224 + 24 * t) for t in range(2)]
            for j in range(J):
                ins = dve.scalar_tensor_tensor(OH[:, j, :], ORD, float(j), OV, ALU.is_equal, ALU.mult)
            seq(ins)
            ins = dve.tensor_tensor(EX, OH, each(CM[:, IOTA, 0:8]), ALU.mult)
            for t in range(2):
                dve.scalar_tensor_tensor(PR[t], each(RK[:, t, :]), float(1 - P), OH, ALU.add, ALU.mult)
                ins = dve.tensor_tensor(PG[t], each(WT[:, t, :]), OH, ALU.mult)
            seq(ins)
            dve.tensor_reduce(RF[:, 1:1 + J], EX, AX.X, ALU.add)
            for t in range(2):
                dve.tensor_reduce(WG[:, t, E:WAVES], PG[t], AX.X, ALU.add)
                ins = dve.tensor_reduce(WR[:, t, E:WAVES], PR[t], AX.X, ALU.add)
            seq(ins)
            for t in range(2):
                dve.tensor_scalar(WR[:, t, E:WAVES], WR[:, t, E:WAVES], -1.0, None, ALU.add)
            seq(dve.tensor_scalar(RFB[:, 0:E], PS[:, 1, 16:24], float(P // 2), None, ALU.is_gt))
            seq(dve.tensor_scalar(OV, PS[:, 1, 16:24], float(P + P // 2), None, ALU.is_gt))
            for j in range(J):
                ins = dve.scalar_tensor_tensor(OH[:, j, :], ORD, float(j), OV, ALU.is_equal, ALU.mult)
            seq(ins)
            seq(dve.tensor_reduce(RFB[:, E:WAVES], OH, AX.X, ALU.add))
            dve.tensor_copy(RIB[:, :], RFB[:, :]).then_inc(rt_tab, 1)
            dve.tensor_copy(RI[:, 0:4], RF[:, 0:4]).then_inc(rt_tab, 1)
            dve.wait_ge(rt_tab, 2)
            dve.nop().then_inc(done["dve"], 1)

            begin(dve, "dve", "moe")
            waves = dve.value_load(RI[0:1, 0:1], min_val=E, max_val=WAVES)
            dve.memset(YE, 0.0)
            dve.memset(HE, 0.0).then_inc(e_zero, 1)
            dve.memset(ACC, 0.0).then_inc(e_add, 4)
            dve.wait_ge(e_add, 4)
            with dve.Fori(0, waves) as w:
                for t in range(2):
                    dve.tensor_scalar(SEL[:, t, :], CM[:, IOTA, :], WR[:, t, bass.ds(w, 1)], None, ALU.is_equal)
                    last = dve.tensor_scalar(SEL[:, 2 + t, :], CM[:, IOTA, :], WR[:, t, bass.ds(w, 1)],
                                             WG[:, t, bass.ds(w, 1)], ALU.is_equal, ALU.mult)
                last.then_inc(e_sel, 1)
                for half in range(2):
                    dve.wait_ge(e_gmm, 2 * w + half + 1)
                    for k in range(4 * half, 4 * half + 4):
                        last = dve.tensor_scalar(XG[:, k, :], PS[:, 4 + half, (k % 4) * P:(k % 4) * P + P],
                                                 AB[:, 1, 0, 0, k:k + 1], AB[:, 1, 0, 1, k:k + 1], ALU.mult, ALU.add)
                    last.then_inc(e_gev, 1)
                for s in range(NUP):
                    dve.wait_ge(e_silu, NUP * w + s + 1)
                    if s >= 2:
                        dve.wait_ge(e_htr, NUP * w + s - 1)
                    dve.tensor_tensor(HE[64:P, s % 2, :], SEB[s % 2][64:P, :], PS[64:P, 2 + s % 2, :], ALU.mult)
                    dve.tensor_tensor(HE[0:64, s % 2, :], SE[64:P, s % 2, :], PS[64:P, s % 2, :],
                                      ALU.mult).then_inc(e_h, 1)
                for i in range(4):
                    dve.wait_ge(e_sc, 4 * w + i + 1)
                    v = ACC[:, i // 2, 512 * (i % 2):512 * (i % 2) + 512]
                    dve.tensor_tensor(v, v, PS[:, i, :], ALU.add).then_inc(e_add, 1)
            dve.wait_ge(e_add, 4 * waves + 4)
            for t in range(2):
                seq(dve.tensor_tensor(ACC[:, t, :], ACC[:, t, :], GE, ALU.mult))
                seq(dve.tensor_tensor(X[:, t, :], X[:, t, :], ACC[:, t, :], ALU.add))
                dve.nop().then_inc(fin_x, 1)

            dve.wait_ge(fin_sd, 1)
            seq(dve.reciprocal(SS[:, 16:18], SS[:, 8:10]))
            dve.wait_ge(s_fg, 16)
            for t in range(2):
                dve.scalar_tensor_tensor(X[:, t, :], X[:, t, :], SS[:, 16 + t:17 + t], FG, ALU.mult,
                                         ALU.mult).then_inc(fin_ok, 1)

        @block.tensor
        def _(pe):
            mm = pe.matmul

            def end():
                pe.nop().then_inc(done["pe"], 1)

            def ident(n=P):
                return CM[0:n, IDENT, 0:n]

            pe.wait_ge(s_rows, 96)
            pe.wait_ge(s_const, 16)
            pe.transpose(PS[:, 7, 0:P], ROWSB[:, :], ident()).then_inc(sm_tr, 1)
            pe.wait_ge(sm_tr, 1)
            end()

            def ada_products(l, i):
                g, q = i // 4, i % 4
                w = wait_chunk(pe, first[f"ada{l}_{i}"])
                for k in range(2):
                    for c in range(4):
                        last = mm(PS[32 * c:32 * c + 32, 4 + g, :], ST[:, 2 * q + k, :],
                                  w[:, k, 512 * c:512 * c + 512], start=(q + k == 0), stop=(q == 3 and k == 1),
                                  tile_position=(0, 32 * c))
                last.then_inc(ada_mm, 1)

            def ada_between(stage, n):
                l, which = ADA_IN.get((stage, n), (0, ()))
                for i in which:
                    ada_products(l, i)

            def ada_columns(l, g):
                pe.wait_ge(mod_rows, 3 * l + g + 1)
                for j in range(4):
                    last = pe.transpose(PS[:, 4 + g, j * P:j * P + P], MOD[:, g, j * P:j * P + P], ident())
                last.then_inc(ada_tr, 1)

            def split_mm(to, parts, ks, n_k, **where):
                for k in ks:
                    (wh, wl), (mh, ml) = parts(k)
                    mm(to, wl, mh, start=(k == 0), stop=False)
                    mm(to, wh, ml, start=False, stop=False)
                    last = mm(to, wh, mh, start=False, stop=(k == n_k - 1))
                return last

            def x_parts(group, k, cols):
                return r12(HIGH[group][k // 4][:, k % 4, cols]), r12(hT[:, k, cols])

            def norm(stage, n, nt0, xn):
                begin(pe, "pe", stage)
                for i in range(n):
                    pe.wait_ge(xn_ready, nt0 + i + 1)
                    if i >= 2:
                        pe.wait_ge(norm_ev, nt0 + i - 1)
                    for k in range(KB):
                        last = pe.transpose(PS[:, 2 * (i % 2) + k // 4, (k % 4) * P:(k % 4) * P + P],
                                            xn(i)[:, k * P:k * P + P], ident())
                    last.then_inc(norm_tr, 1)
                pe.wait_ge(norm_tr, nt0 + n)
                end()

            begin(pe, "pe", "ada0")
            for i in range(4):
                ada_products(0, i)
            ada_columns(0, 0)
            pe.wait_ge(ada_tr, 1)
            end()
            norm("norm0", NT, 0, lambda i: XN[:, i % 2, :])

            begin(pe, "pe", "win")
            for b in range(12):
                high, low = unit_parts(pe, ("win", b // 2))
                if b >= 4:
                    pe.wait_ge(cin_ready, b - 3)
                blk = slice((b % 2) * P, (b % 2) * P + P)
                split_mm(PS[:, b % 4, :], lambda k: ((high[:, k, blk], low[:, k, blk]), x_parts("win", k, slice(0, T))),
                         range(KB), KB).then_inc(win_mm, 1)
                if b % 4 == 3:
                    ada_between("win", b // 4)
            pe.wait_ge(win_mm, 12)
            end()

            begin(pe, "pe", "tok")
            def by_tokens(key, x_of, n, free, done_mm):
                for half in range(2):
                    high, low = unit_parts(pe, (key, half))
                    for t in range(NT):
                        if half == 0 and free(t):
                            pe.wait_ge(*free(t))
                        last = split_mm(PS[:, t, 0:n],
                                        lambda k: (x_of(k, slice(t * P, t * P + P)),
                                                   (high[:, k % 4, :], low[:, k % 4, :])),
                                        range(4 * half, 4 * half + 4), KB)
                        if half:
                            last.then_inc(done_mm, 1)
                    if half == 0:
                        last.then_inc(half_mm, 1)

            for c in range(3):
                by_tokens(f"tok{c}", lambda k, cols: x_parts("win", k, cols), TOKC[c][1],
                          lambda t: (None, (tok_z, t + 1), (tok_ev, t + 1))[c], tok_mm)
                ada_between("tok", c)
            ada_columns(0, 1)
            ada_columns(0, 2)
            pe.wait_ge(ada_tr, 3)
            end()

            begin(pe, "pe", "mproj")
            pe.wait_ge(m_nrm, 1)
            for k in range(6):
                c0 = (CQ0 + P * k) if k < 3 else (CKV0 + P * (k - 3)) if k < 5 else KR0 - NOPE
                n = P if k < 5 else QD
                for t in range(NT):
                    last = pe.transpose(PS[0:n, k, t * P:t * P + P], P2[:, t, c0:c0 + n], ident())
                last.then_inc(m_tr, 1)
            pe.wait_ge(m_trev, 6)
            for j in range(2 * H_B + NT):
                if j >= 4:
                    pe.wait_ge(mproj_ev, j - 3)
                if j < H_B:
                    w = wait_chunk(pe, first["mproj"])
                    for k in range(3):
                        last = mm(PS[0:QD, j % 4, :], w[:, k, j * QD:j * QD + QD], CQT[:, k, :],
                                  start=(k == 0), stop=(k == 2))
                elif j < 2 * H_B:
                    w = wait_chunk(pe, first["mproj"] + 1)
                    h = j - H_B
                    for k in range(2):
                        last = mm(PS[0:NOPE, j % 4, :], w[:, k, h * P:h * P + NOPE], CKVT[:, k, :],
                                  start=(k == 0), stop=(k == 1))
                else:
                    t = j - 2 * H_B
                    for k in range(2):
                        wv = w[:, k, :].rearrange("p (h n) -> p h n", h=H_B)[:, :, NOPE:NOPE + DV]
                        last = mm(PS[:, j % 4, :], CKVT[:, k, t * P:t * P + P], wv, start=(k == 0), stop=(k == 1))
                last.then_inc(mproj_mm, 1)
            pe.wait_ge(mproj_ev, H_B + 1)
            for j in range(H_B + 1):
                if j >= 2:
                    pe.wait_ge(rot_ev, j - 1)
                of = QT[0:QD, j, 0:L] if j < H_B else KT[0:QD, 0, 0:L]
                mm(PS[0:QD, 4 + j % 2, 0:L], CM[0:QD, ROT, 0:QD], of, start=True, stop=True).then_inc(rot_mm, 1)
            pe.wait_ge(rot_mm, H_B + 1)
            end()

            def attention(items, base, pm, pt, scores, pv):
                for i in range(len(items) + 3):
                    if i < len(items):
                        if i >= 3:
                            pe.wait_ge(att_p, base + i - 2)
                        scores(i).then_inc(att_s, 1)
                    j = i - 2
                    if 0 <= j < len(items):
                        pe.wait_ge(att_pn, base + j + 1)
                        if j >= 2:
                            pe.wait_ge(att_pt, base + j - 1)
                        for c in range(items[j][2]):
                            last = pe.transpose(PS[:, 3 + j % 2, c * P:c * P + P], pm[:, j % 3, c * P:c * P + P], ident())
                        last.then_inc(att_tr, 1)
                    j = i - 3
                    if 0 <= j:
                        h, t, n = items[j]
                        pe.wait_ge(att_pt, base + j + 1)
                        if j >= 2:
                            pe.wait_ge(att_oe, base + j - 1)
                        r0 = 64 * (h % 2)
                        for c in range(n):
                            last = mm(PS[r0:r0 + 64, 5 + j % 2, 0:P], pv(h, c, n), pt[:, j % 2, c, :], start=(c == 0),
                                      stop=(c == n - 1))
                        last.then_inc(att_o, 1)
                pe.wait_ge(att_o, base + len(items))
                end()

            begin(pe, "pe", "matt")

            def scores(j):
                h, t, n = M_ITEMS[j]
                return mm(PS[:, j % 3, 0:n * P], QT[0:QD, h, t * P:t * P + P], KT[0:QD, h, T - n * P:T],
                          start=True, stop=True)

            attention(M_ITEMS, 0, PM, PT, scores, lambda h, i, n: VB[:, NT - n + i, h * DV:h * DV + DV])

            begin(pe, "pe", "l2")
            for b in range(8):
                pe.wait_ge(l2_sq, b + 1)
                for t in range(NT):
                    last = mm(PS[:, 0, 4 * b + t:4 * b + t + 1], SQ[:, b % 2, t * P:t * P + P], ONE[:, 0:1],
                              start=True, stop=True)
                last.then_inc(l2_ss, 1)
            pe.wait_ge(l2_r, 1)
            for b in range(8):
                if b >= 4:
                    pe.wait_ge(l2_ok, b - 3)
                for t in range(NT):
                    last = mm(PS[:, 2 + b % 4, t * P:t * P + P],
                              SS[:, 32 + 4 * b + t:33 + 4 * b + t].to_broadcast([P, P]), ident(), start=True, stop=True)
                last.then_inc(l2_bc, 1)
            pe.wait_ge(l2_ok, 8)
            for i in range(8):
                if i >= 2:
                    pe.wait_ge(l2_ev, i - 1)
                for h in range(4):
                    last = pe.transpose(PS[:, 6 + i % 2, h * P:h * P + P],
                                        qkvT[:, 4 + 4 * (i % 2) + h, (i // 2) * P:(i // 2) * P + P], ident())
                last.then_inc(l2_tr, 1)
            pe.wait_ge(l2_tr, 8)
            end()

            begin(pe, "pe", "gdn")
            hh = range(4)
            for s in range(NT):
                for d in dirs:
                    b, B, t = DIR[d], 4 * d, TILE_OF[d][s]
                    tc = slice(t * P, t * P + P)
                    upto, after = CM[:, UP if d == 0 else LO, :], CM[:, SLO if d == 0 else SUP, :]
                    pe.wait_ge(g_gU, both(d, s + 1))
                    if s:
                        pe.wait_ge(g_S, both(d, s))
                    mm(PS[:, B, :], after, b["gU"].rearrange("p h n -> p (h n)"), start=True, stop=True)
                    for h in hh:
                        last = mm(PS[:, B + 1, h * P:h * P + P], b["gU"][:, h, :], after, start=True, stop=True)
                    last.then_inc(g_seg, 1)
                    g = GB8[:, t, 0, 4 * d:4 * d + 4]
                    mm(PS[:, B + 2, 0:4], upto, g, start=True, stop=True)
                    mm(PS[:, B + 2, 4:8], after, g, start=True, stop=True)
                    mm(PS[:, B + 2, 8:12], ONE[:, :], g, start=True, stop=True).then_inc(g_sm, 1)
                    for h in hh:
                        mm(PS[:, B + 3, h * P:h * P + P], qkvT[:, 4 + h, tc], qkvT[:, 4 + h, tc], start=True, stop=True)
                for d in dirs:
                    B, t = 4 * d, TILE_OF[d][s]
                    tc = slice(t * P, t * P + P)
                    pe.wait_ge(g_exp, both(d, s + 1))
                    for h in hh:
                        last = mm(PS[:, B, h * P:h * P + P], qkvT[:, 4 + h, tc], qkvT[:, h, tc], start=True, stop=True)
                    last.then_inc(g_kk, 1)
                for d in dirs:
                    b, B = DIR[d], 4 * d
                    pe.wait_ge(g_A, both(d, s + 1))
                    for h in hh:
                        last = pe.transpose(PS[:, B, h * P:h * P + P], b["A"][:, h, :], ident())
                    last.then_inc(g_At, 1)
                for n in range(1, LEVELS):
                    at = (LEVELS - 1) * s + n
                    for d in dirs:
                        b, B = DIR[d], 4 * d
                        pe.wait_ge(g_LT, both(d, at))
                        if n == 1:
                            pe.wait_ge(g_D1, both(d, s + 1))
                            pe.wait_ge(g_eg, both(d, s + 1))
                        else:
                            pe.wait_ge(g_DE, both(d, at - 1))
                        for h in hh:
                            last = mm(PS[:, B + 1, h * P:h * P + P], b["LT"][:, h, :], b["Dm"][:, h, :],
                                      start=True, stop=True)
                        last.then_inc(g_M1, 1)
                    for d in dirs:
                        b, B = DIR[d], 4 * d
                        pe.wait_ge(g_M1e, both(d, at))
                        if n == 1:
                            pe.wait_ge(g_E1, both(d, s + 1))
                        for h in hh:
                            if n < LEVELS - 1:
                                mm(PS[:, B + 2, h * P:h * P + P], b["Em"][:, h, :], b["dec"][:, h, :],
                                   start=True, stop=True)
                            last = mm(PS[:, B + 3, h * P:h * P + P], b["dec"][:, h, :], b["Em"][:, h, :],
                                      start=True, stop=True)
                        last.then_inc(g_PQ, 1)
                for d in dirs:
                    b, B = DIR[d], 4 * d
                    pe.wait_ge(g_DE, both(d, (LEVELS - 1) * (s + 1)))
                    pe.wait_ge(g_vec, both(d, s + 1))
                    for h in hh:
                        last = mm(PS[:, B + 1, h * P:h * P + P], b["kbe"][:, h, :], b["Em"][:, h, :],
                                  start=True, stop=True)
                    last.then_inc(g_wT, 1)
                for d in dirs:
                    b, B, t = DIR[d], 4 * d, TILE_OF[d][s]
                    pe.wait_ge(g_wTe, both(d, s + 1))
                    for h in hh:
                        mm(PS[:, B, h * P:h * P + P], b["Em"][:, h, :], b["vb"][:, h, :], start=True, stop=False)
                        last = mm(PS[:, B, h * P:h * P + P], b["Dm"][:, h, :], b["S"][:, h, :], start=False, stop=True)
                    last.then_inc(g_vn, 1)
                    for h in hh:
                        mm(PS[:, B + 2, h * P:h * P + P], qkvT[:, h, t * P:t * P + P], b["S"][:, h, :],
                           start=True, stop=True)
                for d in dirs:
                    b, B = DIR[d], 4 * d
                    pe.wait_ge(g_vne, both(d, s + 1))
                    for h in hh:
                        mm(PS[:, B + 3, h * P:h * P + P], b["decT"][:, h, :], b["A"][:, h, :], start=True, stop=True)
                    for h in hh:
                        last = mm(PS[:, B + 1, h * P:h * P + P], b["kg"][:, h, :], b["A"][:, h, :],
                                  start=True, stop=True)
                    last.then_inc(g_o, 1)
            for d in dirs:
                pe.wait_ge(g_o, both(d, NT))
            end()

            begin(pe, "pe", "gout")
            for t in range(NT):
                pe.wait_ge(go_n, t + 1)
                for h in range(4):
                    last = pe.transpose(PS[:, t, h * P:h * P + P], OD[:, 0, t, h * P:h * P + P], ident())
                last.then_inc(go_tr, 1)
            pe.wait_ge(go_tr, NT)
            end()

            def gate_rows(g, c0, n):
                for r in range(n):
                    for c in range(2):
                        q = 32 * (c0 + c) + r
                        last = mm(PS[:, 4 + 2 * r + c, :], ident()[:, q:q + 1].to_broadcast([P, P]), MOD[:, g, :],
                                  start=True, stop=True)
                last.then_inc(gb_mm, 1)

            def project(stage, base, nt, lhs):
                begin(pe, "pe", stage)
                gate_rows(1, 0, nt // 2)
                for i in range(2 * nt):
                    n, t = i // nt, i % nt
                    w = wait_chunk(pe, first[stage] + n)
                    if i >= 4:
                        pe.wait_ge(out_ev, base + i - 3)
                    for k in range(KB):
                        last = mm(PS[:, i % 4, :], lhs(k, t), w[:, k, :], start=(k == 0), stop=(k == KB - 1))
                    last.then_inc(out_mm, 1)
                pe.wait_ge(out_mm, base + 2 * nt)
                end()

            begin(pe, "pe", "out0")
            gate_rows(1, 0, 2)

            def mixed_parts(k, cols):
                low = mixT[:, k, cols] if k < 4 else YB[:, k - 4, cols]
                return r12(HIGH["win"][k // 4][:, k % 4, cols]), r12(low)

            for n in range(2):
                by_tokens(f"out0{n}", mixed_parts, 512, lambda t: (out_ev, t + 1) if n else None, out_mm)
            pe.wait_ge(out_mm, 2 * NT)
            end()
            norm("norm1", NT, 4, lambda i: XN[:, i % 2, :])

            begin(pe, "pe", "up")
            gate_rows(2, 2, 2)
            pe.wait_ge(gb_ready, 2)
            ada_between("up", -1)
            for f in range(FF // P):
                high, low = unit_parts(pe, ("up", f))
                if f >= 2:
                    pe.wait_ge(up_ev, f - 1)
                for u in range(2):
                    last = split_mm(PS[:, 2 * (f % 2) + u, :],
                                    lambda k: ((high[:, k, u, :], low[:, k, u, :]), x_parts("up", k, slice(0, T))),
                                    range(KB), KB)
                last.then_inc(up_mm, 1)
                if f % 2:
                    ada_between("up", f // 2)
            for g in range(3):
                ada_columns(1, g)
            pe.wait_ge(ada_tr, 6)
            end()

            begin(pe, "pe", "down")
            for j in range(NDOWN):
                high, low = unit_parts(pe, ("down", j))
                pe.wait_ge(h2_low, j + 1)
                for n in range(2):
                    for t in range(NT):
                        tile, cols = slice(t * P, t * P + P), slice(512 * n, 512 * n + 512)
                        last = split_mm(PS[:, 4 * n + t, :],
                                        lambda k: ((r12(HHIGH[:, j % 2, k % 2, tile]), r12(H2T[:, k, tile])),
                                                   (high[:, k % 2, cols], low[:, k % 2, cols])),
                                        range(2 * j, 2 * j + 2), FF // P)
                        if j == NDOWN - 1:
                            last.then_inc(down_mm, 1)
                if j < NDOWN - 1:
                    last.then_inc(down_mm, 1)
            pe.wait_ge(down_mm, NDOWN + 7)
            end()

            norm("norm2", NT, 8, lambda i: XN[:, i % 2, :])

            begin(pe, "pe", "qkv")
            for i in range(16):
                high, low = unit_parts(pe, ("qkv", i // 2))
                if i >= 4:
                    pe.wait_ge(qkv_ev[i % 2], (i - 4) // 2 + 1)
                n = L if i < 8 else T
                blk = slice((i % 2) * P, (i % 2) * P + P)
                split_mm(PS[:, i % 4, 0:n], lambda k: ((high[:, k, blk], low[:, k, blk]), x_parts("up", k, slice(0, n))),
                         range(KB), KB).then_inc(qkv_mm, 1)
            for c in (4, 5):
                by_tokens(f"qkv{c}", lambda k, cols: x_parts("up", k, cols), 512, lambda t: (qkv_ev[t % 2], (4 * c + t - 4) // 2 + 1), qkv_mm)
            pe.wait_ge(qkv_mm, 24)
            end()

            begin(pe, "pe", "natt")

            def scores(j):
                h, t, n = N_ITEMS[j]
                rs = slice(64 * (h % 2), 64 * (h % 2) + 64)
                mm(PS[:, j % 3, :], QC[rs, h // 2, t * P:t * P + P], KC[rs, h // 2, :], start=True, stop=False)
                pe.wait_ge(bias_ok, j + 1)
                return mm(PS[:, j % 3, 0:L], CM[:, FLIP, :], BM[:, j % 4, :], start=False, stop=True)

            attention(N_ITEMS, len(M_ITEMS), PC, PCT, scores, lambda h, i, n: VC[:, i, h * DH:h * DH + DH])

            project("out1", 2 * NT, 2, lambda k, t: OC[:, k, t * P:t * P + P])
            norm("norm3", 2, 12, lambda i: X[:, 2 + i, :])

            begin(pe, "pe", "route")
            for t in range(2):
                for k in range(KB):
                    last = mm(PS[:, 0, 8 * t:8 * t + 8], fT[:, k, t * P:t * P + P], RW[:, k, :], start=(k == 0),
                              stop=(k == KB - 1))
            last.then_inc(rt_mm, 1)
            gate_rows(2, 2, 1)
            pe.wait_ge(rt_ev, 1)
            mm(PS[:, 1, 0:8], CM[:, SUP, :], SELM[:, 0, :], start=True, stop=True)
            mm(PS[:, 1, 8:16], CM[:, SUP, :], SELM[:, 1, :], start=True, stop=False)
            mm(PS[:, 1, 8:16], ONE[:, :], SELM[:, 0, :], start=False, stop=True)
            mm(PS[:, 1, 16:24], ONE[:, :], SELM[:, 0, :], start=True, stop=False)
            mm(PS[:, 1, 16:24], ONE[:, :], SELM[:, 1, :], start=False, stop=True).then_inc(rk_mm, 1)
            pe.wait_ge(rk_mm, 1)
            end()

            begin(pe, "pe", "moe")
            waves = pe.value_load(RI[0:1, 0:1], min_val=E, max_val=WAVES)

            def arrive(w, i):
                pe.wait_ge(arrived_e[i % RING_E], (16 * (NEC // RING_E)) * w + 16 * (i // RING_E + 1))
                return BIG[:, (i % RING_E) * SLOT:(i % RING_E) * SLOT + SLOT]

            with pe.Fori(0, waves) as w:
                more = pe.value_load(RIB[0:1, bass.ds(w, 1)], min_val=0, max_val=1)
                pe.wait_ge(e_sel, w + 1)
                for k in range(KB):
                    for t in range(2):
                        last = mm(PS[:, 4 + k // 4, (k % 4) * P:(k % 4) * P + P], X[:, 2 + t, k * P:k * P + P],
                                  SEL[:, t, :], start=(t == 0), stop=(t == 1))
                    if k % 4 == 3:
                        last.then_inc(e_gmm, 1)
                for t in range(2):
                    last = pe.transpose(PS[:, 6, t * P:t * P + P], SEL[:, 2 + t, :], ident())
                last.then_inc(e_tr, 1)

                def columns(s):
                    pe.wait_ge(e_h, NUP * w + s + 1)
                    if s >= 2:
                        pe.wait_ge(e_htev, NUP * w + s - 1)
                    for j in range(4):
                        last = pe.transpose(PS[:, 4 + s % 2, j * P:j * P + P], HE[:, s % 2, j * P:j * P + P], ident())
                    last.then_inc(e_htr, 1)

                pe.wait_ge(e_gev, 2 * w + 2)
                pe.wait_ge(e_add, 4 * w + 4)
                for s in range(NUP):
                    wgu = [arrive(w, 2 * s + u).rearrange("p (k n) -> p k n", k=KB) for u in range(2)]
                    if s >= 2:
                        pe.wait_ge(e_h, NUP * w + s - 1)

                    def gate_up(bank, c0):
                        for k in range(KB):
                            for u in range(2):
                                last = mm(PS[64 * u:64 * u + 64, bank, :], XG[:, k, c0:c0 + 64], wgu[u][:, k, :],
                                          start=(k == 0), stop=(k == KB - 1))
                        return last

                    with pe.If(more > 0):
                        gate_up(2 + s % 2, 64)
                    gate_up(s % 2, 0).then_inc(gu_mm, 1)
                    if s:
                        columns(s - 1)
                columns(NUP - 1)
                pe.wait_ge(e_trev, w + 1)
                for i in range(NDN):
                    slot_e = arrive(w, 2 * NUP + i).rearrange("p (k n) -> p k n", k=4)
                    pe.wait_ge(e_htev, NUP * w + i + 1)

                    def down(bank, c0):
                        for k in range(4):
                            for n in range(2):
                                last = mm(PS[64 * n:64 * n + 64, bank, :], HET[:, 4 * i + k, c0:c0 + 64],
                                          slot_e[:, k, 512 * n:512 * n + 512], start=(i + k == 0),
                                          stop=(i == NDN - 1 and k == 3))
                        return last

                    with pe.If(more > 0):
                        down(7, 64)
                    down(6, 0).then_inc(dn_mm, 1)
                pe.wait_ge(e_y, w + 1)
                for t in range(2):
                    for n in range(2):
                        mm(PS[:, 2 * t + n, :], SELT[:, t, :], YE[:, 0, 512 * n:512 * n + 512], start=True,
                           stop=True).then_inc(e_sc, 1)



_CONSTS = ("masks", "rope", "window")
_INS = ("x", "c", "ctx", "c_ctx", "ada_w", "ada_b", "norm_g", "ev_w_in", "ev_conv_w", "ev_a_log", "ev_dt_bias",
        "ev_gdn_norm_g", "ev_q_norm_g", "ev_w_uq", "ev_kv_norm_g", "ev_w_ukv", "ev_w_out", "ev_ffn_wg", "ev_ffn_wu",
        "ev_ffn_wd", "od_w_qkv", "od_rpb", "od_w_out", "od_router", "od_exp_wg", "od_exp_wu", "od_exp_wd",
        "final_norm_g")


def kernel(**inputs):
    import concourse.bacc as bacc
    from concourse.bass_utils import run_bass_kernel_spmd

    nc = bacc.Bacc("TRN2", target_bir_lowering=False, num_devices=1)
    arrays, A = {}, {}
    for name, a in list(zip(_CONSTS, constants())) + [(n, inputs[n]) for n in _INS]:
        a = np.ascontiguousarray(a)
        arrays[f"in_{name}"] = a
        A[name] = nc.dram_tensor(f"in_{name}", a.shape, mybir.dt.from_np(a.dtype), kind="ExternalInput").ap()
    out = nc.dram_tensor("out", (1, L, D), mybir.dt.float32, kind="ExternalOutput").ap()
    build(nc, A, out)
    r = run_bass_kernel_spmd(nc, [arrays], core_ids=[0])
    return r.results[0]["out"]
```
